# Optimizing a Trainium2 kernel written in Bass

```python
import math
import jax, jax.numpy as jnp
from jax import lax
import numpy as np

D_MODEL = 1024
BATCH = 1
SEQ = 1024
DEPTH = 1
DEC_BATCH = 8
DEC_SEQ = 1
PAST_LEN = 1024
PAGE_SIZE = 128

HEAD_DIM = 64
N_HEADS = D_MODEL // HEAD_DIM
N_KV_HEADS = 4
ROT_DIM = HEAD_DIM // 4
ROPE_THETA = 500000.0
IDX_HEADS = 8
IDX_DIM = 64
TOPK_MAX = 256
Q_BLOCK = 128
SSM_HEAD_DIM = 64
SSM_HEADS = D_MODEL // SSM_HEAD_DIM
D_INNER = SSM_HEADS * SSM_HEAD_DIM
SSM_GROUPS = 4
D_STATE = 128
CONV_W = 4
CONV_DIM = D_INNER + 2 * SSM_GROUPS * D_STATE
SSD_CHUNK = 128
D_FF = 4 * D_MODEL
EPS = 1e-6

ATTN_W = N_HEADS * HEAD_DIM
KV_W = N_KV_HEADS * HEAD_DIM
IN_WIDTHS = (ATTN_W, KV_W, KV_W, IDX_HEADS * IDX_DIM, IDX_DIM, IDX_HEADS, D_INNER, CONV_DIM, SSM_HEADS, D_MODEL, D_MODEL)
D_IN_PROJ = ATTN_W + 2 * KV_W + IDX_HEADS * IDX_DIM + IDX_DIM + IDX_HEADS + D_INNER + CONV_DIM + SSM_HEADS + 2 * D_MODEL

kernel_name = "dsa_ssd_gated_hybrid_decode_step"

def _split(a, widths):
    idx = [int(i) for i in np.cumsum(np.array(widths))[:-1]]
    return jnp.split(a, idx, axis=-1)

def rmsnorm(x, w):
    xf = x.astype(jnp.float32)
    return xf * lax.rsqrt(jnp.mean(xf * xf, axis=-1, keepdims=True) + EPS) * w

def rope_partial(x, pos):
    half = ROT_DIM // 2
    inv = ROPE_THETA ** (-jnp.arange(half, dtype=jnp.float32) * 2.0 / ROT_DIM)
    ang = pos.astype(jnp.float32)[:, None] * inv[None, :]
    cos = jnp.cos(ang)[:, None, :]
    sin = jnp.sin(ang)[:, None, :]
    x1 = x[..., :half]
    x2 = x[..., half:ROT_DIM]
    return jnp.concatenate([x1 * cos - x2 * sin, x1 * sin + x2 * cos, x[..., ROT_DIM:]], axis=-1)

def sparse_attend(q, iq, iw, k, v, ik, q_pos, k_pos, topk):
    B, Tq = q.shape[0], q.shape[1]
    isc = jax.nn.relu(jnp.einsum('bthd,bsd->bths', iq, ik).astype(jnp.float32) * IDX_DIM ** -0.5)
    isc = jnp.einsum('bths,bth->bts', isc, iw.astype(jnp.float32))
    admissible = k_pos[None, :] <= q_pos[:, None]
    isc = jnp.where(admissible[None], isc, -jnp.inf)
    top_val, top_idx = lax.top_k(isc, topk)
    valid = jnp.isfinite(top_val)
    gather = jax.vmap(lambda a, i: a[i])
    kg = gather(k, top_idx)
    vg = gather(v, top_idx)
    qg = q.reshape(B, Tq, N_KV_HEADS, N_HEADS // N_KV_HEADS, HEAD_DIM)
    s = jnp.einsum('bthgd,btjhd->bthgj', qg, kg).astype(jnp.float32) * HEAD_DIM ** -0.5
    s = jnp.where(valid[:, :, None, None, :], s, -jnp.inf)
    p = jax.nn.softmax(s, axis=-1)
    o = jnp.einsum('bthgj,btjhd->bthgd', p.astype(vg.dtype), vg)
    return o.reshape(B, Tq, N_HEADS * HEAD_DIM)

def blocked_self_sparse_attention(q, iq, iw, k, v, ik, pos):
    B, T = q.shape[0], q.shape[1]
    nb = T // Q_BLOCK
    topk = min(TOPK_MAX, T // 4)

    def to_blocks(a):
        return jnp.swapaxes(a.reshape(B, nb, Q_BLOCK, *a.shape[2:]), 0, 1)

    def blk(args):
        qb, iqb, iwb, pb = args
        return sparse_attend(qb, iqb, iwb, k, v, ik, pb, pos, topk)

    out = lax.map(blk, (to_blocks(q), to_blocks(iq), to_blocks(iw), pos.reshape(nb, Q_BLOCK)))
    return jnp.swapaxes(out, 0, 1).reshape(B, T, N_HEADS * HEAD_DIM)

def causal_conv(u, prev, w, b):
    up = jnp.concatenate([prev.astype(u.dtype), u], axis=1)
    out = lax.conv_general_dilated(up, w[:, None, :].astype(u.dtype), (1,), 'VALID',
                                   dimension_numbers=('NWC', 'WIO', 'NWC'),
                                   feature_group_count=u.shape[-1])
    return jax.nn.silu(out + b), up[:, up.shape[1] - (CONV_W - 1):]

def ssd_scan(x, dt, a, bm, cm, s0, chunk):
    B, T, H, P = x.shape
    G, N = bm.shape[2], bm.shape[3]
    HG = H // G
    nc = T // chunk
    f32 = jnp.float32
    x = x.reshape(B, nc, chunk, G, HG, P).astype(f32)
    dt = dt.reshape(B, nc, chunk, G, HG).astype(f32)
    bm = bm.reshape(B, nc, chunk, G, N).astype(f32)
    cm = cm.reshape(B, nc, chunk, G, N).astype(f32)
    cs = jnp.cumsum(dt * a.reshape(G, HG).astype(f32), axis=2)
    seg = cs[:, :, :, None] - cs[:, :, None, :]
    mask = jnp.tril(jnp.ones((chunk, chunk), bool))[:, :, None, None]
    decay = jnp.exp(jnp.where(mask, seg, -jnp.inf))
    xdt = x * dt[..., None]
    cb = jnp.einsum('bcign,bcjgn->bcijg', cm, bm)
    y_diag = jnp.einsum('bcijg,bcijgh,bcjghp->bcighp', cb, decay, xdt)
    decay_end = jnp.exp(cs[:, :, -1:] - cs)
    st = jnp.einsum('bcjgn,bcjgh,bcjghp->bcghpn', bm, decay_end, xdt)
    chunk_decay = jnp.exp(cs[:, :, -1])

    def step(s, inp):
        dec, stc = inp
        return s * dec[..., None, None] + stc, s

    s_init = s0.astype(f32).reshape(B, G, HG, P, N)
    s_last, s_start = lax.scan(step, s_init, (jnp.moveaxis(chunk_decay, 1, 0), jnp.moveaxis(st, 1, 0)))
    s_start = jnp.moveaxis(s_start, 0, 1)
    y_off = jnp.einsum('bcign,bcghpn,bcigh->bcighp', cm, s_start, jnp.exp(cs))
    y = (y_diag + y_off).reshape(B, T, H, P)
    return y, s_last.reshape(B, H, P, N)

def gated_group_rmsnorm(y, z, w):
    g = (y * jax.nn.silu(z)).astype(jnp.float32)
    g = g.reshape(*y.shape[:-1], SSM_GROUPS, D_INNER // SSM_GROUPS)
    g = g * lax.rsqrt(jnp.mean(g * g, axis=-1, keepdims=True) + EPS)
    return g.reshape(y.shape) * w

def hybrid_layer(x, c, pos, past_kv, conv_prev, ssm_prev, w_ada, b_ada, norm1_w, w_in, conv_w, conv_b,
                 dt_bias, a_log, d_skip, ssm_norm_w, w_out, norm2_w, w_up, w_down):
    B, T, _ = x.shape
    mod = jax.nn.silu(c) @ w_ada + b_ada
    sh1, sc1, gt1, sh2, sc2, gt2 = [m[:, None, :] for m in jnp.split(mod, 6, axis=-1)]
    h = rmsnorm(x, norm1_w) * (1.0 + sc1) + sh1
    q, k, v, iq, ik, iw, z, xbc, dt, g_att, g_ssm = _split(h @ w_in, IN_WIDTHS)
    q = rope_partial(q.reshape(B, T, N_HEADS, HEAD_DIM), pos)
    k = rope_partial(k.reshape(B, T, N_KV_HEADS, HEAD_DIM), pos)
    v = v.reshape(B, T, N_KV_HEADS, HEAD_DIM)
    iq = rope_partial(iq.reshape(B, T, IDX_HEADS, IDX_DIM), pos)
    ik = rope_partial(ik[:, :, None, :], pos)[:, :, 0, :]
    iw = iw * IDX_HEADS ** -0.5
    if past_kv is None:
        att = blocked_self_sparse_attention(q, iq, iw, k, v, ik, pos)
    else:
        pk, pv, pik = past_kv
        kk = jnp.concatenate([pk.astype(k.dtype), k], axis=1)
        vv = jnp.concatenate([pv.astype(v.dtype), v], axis=1)
        ikk = jnp.concatenate([pik.astype(ik.dtype), ik], axis=1)
        L = kk.shape[1]
        att = sparse_attend(q, iq, iw, kk, vv, ikk, pos, jnp.arange(L), min(TOPK_MAX, L // 4))
    xbc, conv_new = causal_conv(xbc, conv_prev, conv_w, conv_b)
    xs, bm, cm = _split(xbc, (D_INNER, SSM_GROUPS * D_STATE, SSM_GROUPS * D_STATE))
    xs = xs.reshape(B, T, SSM_HEADS, SSM_HEAD_DIM)
    dt = jax.nn.softplus((dt + dt_bias).astype(jnp.float32))
    a = -jnp.exp(a_log.astype(jnp.float32))
    chunk = SSD_CHUNK if T % SSD_CHUNK == 0 else T
    y, ssm_new = ssd_scan(xs, dt, a, bm.reshape(B, T, SSM_GROUPS, D_STATE),
                          cm.reshape(B, T, SSM_GROUPS, D_STATE), ssm_prev, chunk)
    y = y + d_skip[:, None] * xs
    y = gated_group_rmsnorm(y.reshape(B, T, D_INNER), z, ssm_norm_w)
    merged = jax.nn.sigmoid(g_att) * att + jax.nn.sigmoid(g_ssm) * y
    x = x + gt1 * (merged @ w_out)
    h2 = rmsnorm(x, norm2_w) * (1.0 + sc2) + sh2
    x = x + gt2 * (jnp.square(jax.nn.relu(h2 @ w_up)) @ w_down)
    return x, (k, v, ik, conv_new, ssm_new)

def gather_pages(pool, page_table):
    g = pool[page_table]
    return g.reshape(g.shape[0], g.shape[1] * g.shape[2], *g.shape[3:])

def setup_inputs(seed: int = 0) -> dict:
    key = jax.random.key(seed)
    ks = jax.random.split(key, 32)
    n_pages = PAST_LEN // PAGE_SIZE
    n_phys = (5 * DEC_BATCH * n_pages) // 4

    def nrm(k, shape, s=1.0):
        return jax.random.normal(k, shape, jnp.float32) * s

    page_table = jax.random.permutation(ks[0], n_phys)[:DEC_BATCH * n_pages].reshape(DEC_BATCH, n_pages).astype(jnp.int32)
    dt0 = jnp.exp(jax.random.uniform(ks[1], (DEPTH, SSM_HEADS), jnp.float32, math.log(1e-3), math.log(1e-1)))
    return {
        "x_prompt": nrm(ks[2], (BATCH, SEQ, D_MODEL)),
        "x_sample": nrm(ks[3], (DEC_BATCH, DEC_SEQ, D_MODEL)),
        "cache_k": nrm(ks[4], (DEPTH, n_phys, PAGE_SIZE, N_KV_HEADS, HEAD_DIM)),
        "cache_v": nrm(ks[5], (DEPTH, n_phys, PAGE_SIZE, N_KV_HEADS, HEAD_DIM)),
        "cache_idx_k": nrm(ks[6], (DEPTH, n_phys, PAGE_SIZE, IDX_DIM)),
        "state_conv": nrm(ks[7], (DEPTH, DEC_BATCH, CONV_W - 1, CONV_DIM)),
        "state_ssm": nrm(ks[8], (DEPTH, DEC_BATCH, SSM_HEADS, SSM_HEAD_DIM, D_STATE), 0.5),
        "page_table": page_table,
        "c_prompt": nrm(ks[9], (BATCH, D_MODEL)),
        "c_sample": nrm(ks[10], (DEC_BATCH, D_MODEL)),
        "w_ada": nrm(ks[11], (DEPTH, D_MODEL, 6 * D_MODEL), D_MODEL ** -0.5),
        "b_ada": nrm(ks[12], (DEPTH, 6 * D_MODEL), 0.02),
        "norm1_w": 1.0 + nrm(ks[13], (DEPTH, D_MODEL), 0.02),
        "w_in": nrm(ks[14], (DEPTH, D_MODEL, D_IN_PROJ), D_MODEL ** -0.5),
        "conv_w": nrm(ks[15], (DEPTH, CONV_W, CONV_DIM), CONV_W ** -0.5),
        "conv_b": nrm(ks[16], (DEPTH, CONV_DIM), 0.02),
        "dt_bias": dt0 + jnp.log(-jnp.expm1(-dt0)),
        "a_log": jnp.log(jax.random.uniform(ks[17], (DEPTH, SSM_HEADS), jnp.float32, 1.0, 16.0)),
        "d_skip": 1.0 + nrm(ks[18], (DEPTH, SSM_HEADS), 0.02),
        "ssm_norm_w": 1.0 + nrm(ks[19], (DEPTH, D_INNER), 0.02),
        "w_out": nrm(ks[20], (DEPTH, D_MODEL, D_MODEL), D_MODEL ** -0.5),
        "norm2_w": 1.0 + nrm(ks[21], (DEPTH, D_MODEL), 0.02),
        "w_up": nrm(ks[22], (DEPTH, D_MODEL, D_FF), D_MODEL ** -0.5),
        "w_down": nrm(ks[23], (DEPTH, D_FF, D_MODEL), D_FF ** -0.5),
        "final_norm_w": 1.0 + nrm(ks[24], (D_MODEL,), 0.02),
    }

def reference(x_prompt, x_sample, cache_k, cache_v, cache_idx_k, state_conv, state_ssm, page_table,
              c_prompt, c_sample, w_ada, b_ada, norm1_w, w_in, conv_w, conv_b, dt_bias, a_log, d_skip,
              ssm_norm_w, w_out, norm2_w, w_up, w_down, final_norm_w):
    B, T = x_prompt.shape[0], x_prompt.shape[1]
    TS = x_sample.shape[1]
    past = page_table.shape[1] * cache_k.shape[2]
    pos_p = jnp.arange(T)
    pos_s = past + jnp.arange(TS)
    hp, hs = x_prompt, x_sample
    kp, vp, ikp, cvp, ssp = [], [], [], [], []
    ksm, vsm, iks, cvs, sss = [], [], [], [], []
    for l in range(DEPTH):
        lw = (w_ada[l], b_ada[l], norm1_w[l], w_in[l], conv_w[l], conv_b[l], dt_bias[l], a_log[l],
              d_skip[l], ssm_norm_w[l], w_out[l], norm2_w[l], w_up[l], w_down[l])
        conv0 = jnp.zeros((B, CONV_W - 1, CONV_DIM), x_prompt.dtype)
        ssm0 = jnp.zeros((B, SSM_HEADS, SSM_HEAD_DIM, D_STATE), jnp.float32)
        hp, (k1, v1, ik1, cv1, ss1) = hybrid_layer(hp, c_prompt, pos_p, None, conv0, ssm0, *lw)
        past_kv = (gather_pages(cache_k[l], page_table), gather_pages(cache_v[l], page_table),
                   gather_pages(cache_idx_k[l], page_table))
        hs, (k2, v2, ik2, cv2, ss2) = hybrid_layer(hs, c_sample, pos_s, past_kv, state_conv[l], state_ssm[l], *lw)
        kp.append(k1); vp.append(v1); ikp.append(ik1); cvp.append(cv1); ssp.append(ss1)
        ksm.append(k2); vsm.append(v2); iks.append(ik2); cvs.append(cv2); sss.append(ss2)
    y_prompt = rmsnorm(hp, final_norm_w)
    y_sample = rmsnorm(hs, final_norm_w)
    return (y_prompt, y_sample,
            jnp.stack(kp), jnp.stack(vp), jnp.stack(ikp), jnp.stack(cvp), jnp.stack(ssp),
            jnp.stack(ksm), jnp.stack(vsm), jnp.stack(iks), jnp.stack(cvs), jnp.stack(sss))


_drawn_inputs = setup_inputs


def setup_inputs(seed=0):
    import zlib

    import numpy as np

    out = dict(_drawn_inputs(seed))
    spreads = {}
    factors = {'d_skip': 36.677,
     'ssm_norm_w': 8.0,
     'norm2_w': 3.425,
     'final_norm_w': 2.745,
     'cache_k': 3.2,
     'cache_v': 3.204,
     'cache_idx_k': 3.546}
    for name, (base, spread) in spreads.items():
        noise = np.random.default_rng([zlib.crc32(name.encode()), seed]).standard_normal(out[name].shape)
        drawn = base * np.exp(spread * noise) if base else spread * noise
        out[name] = __import__('jax').numpy.asarray(drawn.astype(out[name].dtype))
    for name, factor in factors.items():
        out[name] = (out[name] * factor).astype(out[name].dtype)
    return out
```

```python
from contextlib import ExitStack

import concourse.bass as bass
from concourse import mybir
from concourse.alu_op_type import AluOpType as ALU

F32 = mybir.dt.float32
F32R = mybir.dt.float32r
I32 = mybir.dt.int32
ACT = mybir.ActivationFunctionType
AX = mybir.AxisListType.X

P = 128
D = 1024
T = 1024
NB = 8
TT = T + NB
W3 = TT // 3
KT = D // P
NT = T // P
L = 1025
TOPK = 256
IDX_SCALE = 0.125
ATT_SCALE = 0.125
EPS = 1e-6
PICKED = -3.0e38
BARRED = -1.0e38
AWAY = -1.0e30
WIN = 7256
C_Q, C_K, C_IQ, C_IK, C_IW, C_Z, C_X, C_DT, C_G = 0, 1024, 1536, 2048, 2112, 2120, 3144, 5192, 5208

K_ID, K_ONE, K_HALF, K_LE, K_GT, K_DIAG, K_GE, K_COS, K_SIN = 0, 128, 256, 384, 512, 640, 768, 896, 896 + TT
K_SEL = K_SIN + TT
K_EXP = K_SEL + P
K_SH = K_EXP + 8 * P
K_BD = K_SH + 64
K_END = K_BD + 8


def off(t):
    return P * t * (t + 1) // 2


class Link:

    def __init__(self, eng, sem):
        self.eng, self.sem, self.base, self.k, self.i, self.per = eng, sem, 0, 0, None, 0

    def __call__(self, ins):
        ins.then_inc(self.sem, 1)
        self.k += 1
        n = self.base + self.k
        self.eng.wait_ge(self.sem, n if self.i is None else self.i * self.per + n)

    def enter(self, i, per):
        self.base, self.k, self.i, self.per = self.base + self.k, 0, i, per

    def leave(self, n):
        assert self.k == self.per, (self.k, self.per)
        self.base, self.k, self.i = self.base + n * self.per, 0, None


def program(nc, x_prompt, x_sample, cache_k, cache_v, cache_idx_k, state_conv, state_ssm, page_table,
            c_prompt, c_sample, w_ada, b_ada, norm1_w, w_in, conv_w, conv_b, dt_bias, a_log, d_skip,
            ssm_norm_w, w_out, norm2_w, w_up, w_down, final_norm_w, consts,
            y_prompt, y_sample, k_prompt, v_prompt, idxk_prompt, conv_prompt, ssm_prompt,
            k_sample, v_sample, idxk_sample, conv_sample, ssm_sample):
    n_phys = cache_k.shape[1]
    with ExitStack() as ctx:
        def sem(name):
            return ctx.enter_context(nc.semaphore(name))

        def sb(name, shape, dt=F32, where=ctx):
            return where.enter_context(nc.sbuf_tensor(name, shape, dt))

        d_x = nc.dram_tensor("scr_x", (KT, P, TT), F32).ap()
        d_q = nc.dram_tensor("scr_q", (KT, P, TT), F32).ap()
        d_z = nc.dram_tensor("scr_z", (KT, P, TT), F32).ap()
        d_g = nc.dram_tensor("scr_g", (2 * KT, P, TT), F32).ap()
        d_c = nc.dram_tensor("scr_c", (2 * KT, P, TT), F32).ap()

        pj = ctx.enter_context(nc.psum_tensor("pj", [P, 2, 3, 512], F32))
        px = ctx.enter_context(nc.psum_tensor("px", [P, 2, 512], F32))
        pjf = [pj[:, s].rearrange("p a b -> p (a b)") for s in range(2)]
        pxf = px[:].rearrange("p a b -> p (a b)")

        cst = sb("cst", [P, K_END])
        ident, ones, halves = cst[:, K_ID:K_ID + P], cst[:, K_ONE:K_ONE + P], cst[:, K_HALF:K_HALF + P]
        le, gt, diag, ge = (cst[:, k:k + P] for k in (K_LE, K_GT, K_DIAG, K_GE))
        cos, sin = cst[:, K_COS:K_COS + TT], cst[:, K_SIN:K_SIN + TT]
        sel = cst[0:8, K_SEL:K_SEL + P]
        expand = cst[0:16, K_EXP:K_EXP + 8 * P].rearrange("h (m p) -> h m p", m=8)
        spread_h = cst[0:8, K_SH:K_SH + 64]
        own_b = cst[0:64, K_BD:K_BD + 8]

        par = sb("par", [P, 96])
        taps = sb("taps", [P, 64])
        modT = sb("modT", [P, 48, 9])
        aff = sb("aff", [P, KT, 9])
        eps = sb("eps", [P, 1])
        dskip = sb("dskip", [P, KT])
        dtb = sb("dtb", [P, 16])
        aneg = sb("aneg", [P, 16])
        misc = sb("misc", [P, NT + 1, 48])
        dtn = sb("dtn", [P, NT + 1, 16])
        dta = sb("dta", [P, NT + 1, 16])
        convS = sb("convS", [P, 16, NB])
        pgt = sb("pgt", [1, 64], I32)
        qs = sb("qs", [P, KT, NB])
        iqs = sb("iqs", [64, 8, NB])
        scT = sb("scT", [P, 16, 24])
        xraw = sb("xraw", [P, 16, 11])

        s_cst, s_par, s_vec, s_pt, s_crow = (sem(n) for n in ("s_cst", "s_par", "s_vec", "s_pt", "s_crow"))
        s_xin = [sem("s_xin0"), sem("s_xin1")]
        s_xt, s_xe = sem("s_xt"), sem("s_xe")
        s_csil = sem("s_csil")
        s_ptr, s_pte = sem("s_ptr"), sem("s_pte")
        s_raw = [sem("s_raw0"), sem("s_raw1")]
        s_ada, s_mod = sem("s_ada"), sem("s_mod")
        s_sq, s_ss, s_rt, s_rs, s_h, s_hh, s_hl = (sem(n) for n in ("s_sq", "s_ss", "s_rt", "s_rs", "s_h", "s_hh", "s_hl"))
        s_split, s_mm, s_ev = (sem(n) for n in ("s_split", "s_mm", "s_ev"))
        s_st = [sem("s_st0"), sem("s_st1")]
        s_xs = sem("s_xs")
        s_c = {e: sem("s_link_" + e) for e in ("act", "dve", "pool")}
        s_tr, s_te, s_nat = sem("s_tr"), sem("s_te"), sem("s_nat")
        s_natd = [sem("s_natd0"), sem("s_natd1")]
        s_is, s_ir, s_ia = sem("s_is"), sem("s_ir"), sem("s_ia")
        s_out = sem("s_out")
        n_out = [0]

        def store(eng, dst, src):
            eng.dma_start(dst, src).then_inc(s_out, 16)
            n_out[0] += 16

        raw = sb("raw", [P, 2, KT * 256])
        whi = sb("whi", [P, 2, KT, P], F32R)
        wlo = sb("wlo", [P, 2, KT, P], F32R)

        w_in2 = w_in[0].rearrange("(k p) n -> p k n", p=P)
        w_ada2 = w_ada[0].rearrange("(k p) n -> p k n", p=P)
        w_up2 = w_up[0].rearrange("(k p) n -> p k n", p=P)
        w_dn2 = w_down[0].rearrange("(e k p) n -> e p k n", p=P, k=4)
        w_out2 = w_out[0].rearrange("(j u a d) n -> j u d a n", j=2, u=2, a=4)

        PAIRS = ([("iq", n, False) for n in range(2)] + [("k", 0, False), ("v", 0, False), ("misc", 0, False)]
                 + [("q", n, True) for n in range(4)] + [("z", n, True) for n in range(4)]
                 + [("g", n, True) for n in range(8)] + [("x", n, True) for n in range(4)]
                 + [("bc", n, False) for n in range(4)])
        B_OUT = 2 * len(PAIRS)
        B_MLP = B_OUT + KT
        COL = {"iq": C_IQ, "k": C_K, "v": C_K + 256, "q": C_Q, "z": C_Z, "g": C_G, "x": C_X, "bc": C_X + D}
        N_ADA = 24

        def load_pair(sp, n):
            name, at, head_order = PAIRS[n]
            slot = n % 2
            v = raw[:, slot].rearrange("p (k n) -> p k n", k=KT)
            if name == "misc":
                parts = [(v[:, :, 0:72], w_in2[:, :, C_IK:C_IK + 72]), (v[:, :, 72:88], w_in2[:, :, C_DT:C_DT + 16])]
            elif head_order:
                c = COL[name] + (at // 2) * 512 + (at % 2) * P
                parts = [(v[:, :, 0:P], w_in2[:, :, c:c + P]), (v[:, :, P:2 * P], w_in2[:, :, c + 256:c + 256 + P])]
            else:
                c = COL[name] + at * 256
                parts = [(v[:], w_in2[:, :, c:c + 256])]
            for dst, src in parts:
                sp.dma_start(dst, src).then_inc(s_raw[slot], 16)

        raw_at = [16 * (N_ADA // 2)] * 2
        PAIR_AT = []
        for n, (name, _, head_order) in enumerate(PAIRS):
            raw_at[n % 2] += 32 if head_order or name == "misc" else 16
            PAIR_AT.append(raw_at[n % 2])

        def weight_parts(name, b, v, head_order):
            if name == "misc":
                if b == 0:
                    return [(v[:, :, 0:64], 0, 64), (v[:, :, 0:64], 64, P)]
                return [(v[:, :, 64:72], 0, 8), (v[:, :, 72:88], 32, 48)]
            if head_order:
                return [(v[:, :, b * 64:b * 64 + 64], 0, 64), (v[:, :, P + b * 64:P + b * 64 + 64], 64, P)]
            return [(v[:, :, b * P:b * P + P], 0, P)]

        def split_block(pool, parts, kt, hs, link):
            for n, (a, c0, c1) in enumerate(parts):
                ins = pool.tensor_copy(whi[:, hs, 0:kt, c0:c1], a)
                if n < len(parts) - 1:
                    ins.then_inc(s_part, 1)
            link(ins)
            if len(parts) == 2:
                parts_done[0] += 1
                pool.wait_ge(s_part, parts_done[0])
            for n, (a, c0, c1) in enumerate(parts):
                ins = pool.tensor_tensor(wlo[:, hs, 0:kt, c0:c1], a, whi[:, hs, 0:kt, c0:c1].bitcast(F32), ALU.subtract)
                if n < len(parts) - 1:
                    ins.then_inc(s_part, 1)
                    parts_done[0] += 1
            if len(parts) == 2:
                pool.wait_ge(s_part, parts_done[0])
            ins.then_inc(s_split, 1)

        s_part = sem("s_part")
        parts_done = [0]

        def products(pe, hs, kt, ahi, alo):
            for n in range(3):
                c = slice(n * W3, n * W3 + W3)
                for k in range(kt):
                    for m, (w, a) in enumerate(((whi, ahi), (whi, alo), (wlo, ahi))):
                        ins = pe.matmul(pj[:, hs, n, 0:W3], w[:, hs, k], a[:, k, c],
                                        start=(k == 0 and m == 0), stop=(k == kt - 1 and m == 2))
            ins.then_inc(s_mm, 1)

        def pe_blocks(pe, b0, n):
            with pe.Fori(0, n // 2) as i:
                for s in range(2):
                    pe.wait_ge(s_split, i * 2 + (b0 + s + 1))
                    pe.wait_ge(s_ev, i * 2 + (b0 + s - 1))
                    products(pe, s, KT, act_hi, act_lo)

        prod = [pj[:, s, :, 0:W3] for s in range(2)]

        def three(ap):
            return ap.rearrange("p (a b) -> p a b", a=3)

        R = ExitStack()
        REGION = off(NT) + 2 * TT + 256 * (NT + 1)
        region = sb("region", [P, REGION], F32, R)
        xT = region[:, 0:KT * TT].rearrange("p (k t) -> p k t", k=KT)
        isc = region[:, 0:off(NT)]
        vT = region[:, 0:2 * TT].rearrange("p (k t) -> p k t", k=2)
        mT = region[:, 2 * TT:3 * TT]
        nst = region[:, 3 * TT:3 * TT + 2 * 624].rearrange("p (s n) -> p s n", s=2)
        r0 = off(NT)
        kT = region[:, r0:r0 + 2 * TT].rearrange("p (k t) -> p k t", k=2)
        vn = region[:, r0 + 2 * TT:].rearrange("p (k t) -> p k t", t=256)
        ikT = sb("ikT", [P, TT], F32, R)
        with ExitStack() as A:
            iqT = sb("iqT", [P, 4, TT], F32, A)
            act_hi = sb("act_hi", [P, KT, TT], F32R, A)
            act_lo = sb("act_lo", [P, KT, TT], F32R, A)
            E = sb("E", [P, 2, TT], F32, A)
            ROT = sb("ROT", [P, TT], F32, A)
            O = sb("O", [P, 2, TT + 3], F32, A)
            cT = sb("cT", [P, KT, 9], F32, A)
            rows = sb("rows", [96, P], F32, A)
            rowb = sb("rowb", [64, P], F32, A)
            m8 = sb("m8", [P, 8], F32, A)
            dtx = sb("dtx", [P, 4, (NT + 1) * 16], F32, A)
            scn = E[0:24].rearrange("p a b -> p (a b)")[:, 0:2 * D]
            crow = ROT[0:9, 0:D]
            xin = O[:, :, 0:D]
            crst = E[0:11].rearrange("p a b -> p (a b)")[:, 0:2 * D]

        with ExitStack() as Bs:
            M = sb("M", [P, KT, TT], F32, Bs)
            gates = sb("gates", [P, 2, KT, NB], F32, Bs)
            k_hh = [w[:].rearrange("p u k n -> p u (k n)") for w in (whi, wlo)]
            k_lo = sb("k_lo", [P, 2, T], F32R, Bs)
            with ExitStack() as B1:
                xb = sb("xb", [P, 2, 16, P], F32, B1)
                zc, gc = (raw[:, s].rearrange("p (s k t) -> p s k t", s=2, k=KT) for s in range(2))
                dtc = sb("dtc", [P, 2, 16], F32, B1)
                dac = sb("dac", [P, 2, 16], F32, B1)
                ex = sb("ex", [P, 48], F32, B1)
                xdt = sb("xdt", [P, 16, 64], F32, B1)
                xw = sb("xw", [P, 16, 64], F32, B1)
                Bn = sb("Bn", [P, 4, P], F32, B1)
                cbm = sb("cbm", [P, 4, P], F32, B1)
                SM = sb("SM", [P, 2, 4, P], F32, B1)
                Lx = sb("Lx", [P, 2, 4, P], F32, B1)
                ML = sb("ML", [P, 2, 4, P], F32, B1)
                ST = sb("ST", [P, D], F32, B1)[:]
                yn = sb("yn", [P, D], F32, B1)[:]
                gg = sb("gg", [P, KT, P], F32, B1)[:]
                xD = sb("xD", [P, KT, P], F32, B1)[:]
                rt = sb("rt", [P, 2, P], F32, B1)
            with ExitStack() as B2:
                qt = sb("qt", [P, 2, 2, KT, P], F32, B2)
                q_hl = sb("q_hl", [P, 2, 2, KT, P], F32R, B2)
                ga = sb("ga", [P, 2, KT, P], F32, B2)
                Sm = sb("Sm", [P, 2, D], F32, B2)
                Pr = sb("Pr", [P, 2, D], F32, B2)
                PT = sb("PT", [P, 2, D], F32, B2)
                an = sb("an", [P, D], F32, B2)
                mx = sb("mx", [P, P], F32, B2)
                nm = sb("nm", [P, P], F32, B2)
                sm = sb("sm", [P, P], F32, B2)
                ri = sb("ri", [P, P], F32, B2)
            with ExitStack() as B3:
                pg = sb("pg", [P, 2, 8, 256], F32, B3)
                kTb = sb("kTb", [P, 2, 2, L], F32, B3)
                sg = sb("sg", [P, 4, KT, NB], F32, B3)
                scol = sb("scol", [P, 8], F32, B3)
                qz = sb("qz", [P, NB * 2 * P + 272], F32, B3)
                iqz = sb("iqz", [64, NB * 64 + 72], F32, B3)
                bwt = sb("bwt", [8, 64], F32, B3)[:]
                m8b = sb("m8b", [P, 8], F32, B3)
                bwz = sb("bwz", [64, 8], F32, B3)
                sS, sP = sb("sS", [P, L], F32, B3)[:], sb("sP", [P, L], F32, B3)[:]
                sT = sb("sT", [P, 9, P], F32, B3)
                vrow = sb("vrow", [1, NB, 256], F32, B3)[:]
            with ExitStack() as B4:
                S0 = sb("S0", [P, 2, KT, P], F32, B4)
                S1 = sb("S1", [P, 2, KT, P], F32, B4)
                S2 = sb("S2", [P, 2, KT, P], F32, B4)
                S3 = sb("S3", [P, KT, P], F32, B4)
                BX = sb("BX", [P, 8, 64], F32, B4)
                sq4 = sb("sq4", [P, 12, KT, NB], F32, B4)
                dT = sb("dT", [16, 2, NB], F32, B4)
        R.close()
        with ExitStack() as C:
            ahi = sb("ahi", [P, KT, TT], F32R, C)
            RC = sb("RC", [P, TT], F32, C)
            tmp8 = sb("tmp8", [P, 2, NB], F32, C)
            zero = sb("zero", [P, P], F32, C)[:]
            sb("room", [P, REGION + TT - (KT * TT + TT + 2 * NB + P)], F32, C)
            sb("keep_M", [P, KT, TT], F32, C)
            u_hi = sb("u_hi", [P, 2, 2, TT], F32R, C)
            alo = sb("alo", [P, KT, TT], F32R, C)
            u_lo = sb("u_lo", [P, 2, 2, TT], F32R, C)
            OC = sb("OC", [P, 2, TT], F32, C)
        x2T = M

        def norm_squares(act, src, sq, n):
            for k in range(KT):
                if 8 * n + k >= 2:
                    act.wait_ge(s_ss, 8 * n + k - 1)
                act.activation(sq[:, k % 2, 0:TT], src[:, k], ACT.Square).then_inc(s_sq, 1)

        def norm_sums(pe, sq, n):
            for k in range(KT):
                pe.wait_ge(s_sq, 8 * n + k + 1)
                for c in range(3):
                    ins = pe.matmul(pj[:, 1, c, 0:W3], ones, sq[:, k % 2, c * W3:(c + 1) * W3],
                                    start=(k == 0), stop=(k == KT - 1))
                ins.then_inc(s_ss, 1)

        def norm_root(act, dst, n):
            act.wait_ge(s_ss, 8 * n + 8)
            act.activation(three(dst), prod[1], ACT.Sqrt, bias=eps[:], scale=1.0 / D).then_inc(s_rt, 1)

        def norm_apply(dve, link, src, rst, dst, nw, sh, sc, n):
            dve.wait_ge(s_rt, n + 1)
            link(dve.reciprocal(rst, rst))
            link(dve.scalar_tensor_tensor(aff[:], modT[:, sc * 8:sc * 8 + 8], 1.0,
                                          nw.unsqueeze(2).broadcast_to([P, KT, 9]), ALU.add, ALU.mult))
            for k in range(KT):
                if 8 * n + k >= 2:
                    dve.wait_ge(s_hl, 8 * n + k - 1)
                d = dst[:, k % 2]
                link(dve.tensor_tensor(d[:, 0:TT], src[:, k], rst, ALU.mult))
                dve.tensor_scalar(d[:, 0:T], d[:, 0:T], aff[:, k, 8:9], modT[:, sh * 8 + k, 8:9],
                                  ALU.mult, ALU.add).then_inc(s_h, 1)
                link(dve.tensor_tensor(d[:, T:TT], d[:, T:TT], aff[:, k, 0:8], ALU.mult))
                dve.tensor_tensor(d[:, T:TT], d[:, T:TT], modT[:, sh * 8 + k, 0:8], ALU.add).then_inc(s_h, 1)

        def norm_hi(act, dst, hi, n):
            for k in range(KT):
                act.wait_ge(s_h, 2 * (8 * n + k) + 2)
                act.activation(hi[:, k], dst[:, k % 2, 0:TT], ACT.Copy).then_inc(s_hh, 1)

        def norm_lo(pool, dst, hi, lo, n):
            for k in range(KT):
                pool.wait_ge(s_hh, 8 * n + k + 1)
                pool.tensor_tensor(lo[:, k], dst[:, k % 2, 0:TT], hi[:, k].bitcast(F32), ALU.subtract).then_inc(s_hl, 1)

        ROPE = [0, 1, 2, 3, 4, 5, 8] + list(range(10, 18))
        IDX = [(t, h) for t in range(2, NT) for h in range(8)]

        def sp_phase_a(sp):
            sp.dma_start(cst[:], consts).then_inc(s_cst, 16)
            sp.dma_start(crow[0:8], c_sample).then_inc(s_crow, 16)
            sp.dma_start(crow[8:9], c_prompt).then_inc(s_crow, 16)
            sp.dma_start(rows[0:48], b_ada[0].rearrange("(r p) -> r p", p=P)).then_inc(s_par, 16)
            sp.dma_start(rows[48:56], norm1_w[0].rearrange("(r p) -> r p", p=P)).then_inc(s_par, 16)
            sp.dma_start(rows[56:64], norm2_w[0].rearrange("(r p) -> r p", p=P)).then_inc(s_par, 16)
            sp.dma_start(rows[64:72], final_norm_w.rearrange("(r p) -> r p", p=P)).then_inc(s_par, 16)
            sp.dma_start(rows[88:96], conv_b[0, D:2 * D].rearrange("(r p) -> r p", p=P)).then_inc(s_par, 16)
            for j in range(2):
                for at, v in ((72, ssm_norm_w[0]), (80, conv_b[0])):
                    sp.dma_start(rows[at + 4 * j:at + 4 * j + 4].rearrange("a (u d) -> a u d", u=2),
                                 v[j * 512:j * 512 + 512].rearrange("(u a d) -> a u d", u=2, a=4)).then_inc(s_par, 16)
                for tap in range(4):
                    sp.dma_start(rowb[16 * tap + 4 * j:16 * tap + 4 * j + 4].rearrange("a (u d) -> a u d", u=2),
                                 conv_w[0, tap, j * 512:j * 512 + 512].rearrange("(u a d) -> a u d", u=2, a=4)
                                 ).then_inc(s_par, 16)
            for tap in range(4):
                sp.dma_start(rowb[16 * tap + 8:16 * tap + 16],
                             conv_w[0, tap, D:2 * D].rearrange("(r p) -> r p", p=P)).then_inc(s_par, 16)
            hist = state_conv[0].rearrange("b t c -> (b t) c")
            sp.dma_start(scn[:, D:2 * D], hist[:, D:2 * D]).then_inc(s_par, 16)
            for j in range(2):
                for u in range(2):
                    sp.dma_start(scn[:, j * 512:j * 512 + 512].rearrange("r (a u d) -> r u a d", u=2, a=4)[:, u],
                                 hist[:, j * 512 + u * 256:j * 512 + u * 256 + 256].rearrange("r (a d) -> r a d", a=4)
                                 ).then_inc(s_par, 16)
            for u in range(2):
                for j in range(2):
                    sp.dma_start(dskip[64 * u:64 * u + 64, 4 * j:4 * j + 4],
                                 d_skip[0:1, 8 * j + 4 * u:8 * j + 4 * u + 4].broadcast_to([64, 4])).then_inc(s_vec, 16)
            sp.dma_start(dtb[:], dt_bias[0:1, :].broadcast_to([P, 16])).then_inc(s_vec, 16)
            sp.dma_start(aneg[:], a_log[0:1, :].broadcast_to([P, 16])).then_inc(s_vec, 16)
            sp.dma_start(pgt[:], page_table.rearrange("b n -> (b n)").unsqueeze(0)).then_inc(s_pt, 16)
            for t in range(NT + 1):
                if t >= 2:
                    sp.wait_ge(s_xt, t - 1)
                src = x_prompt[0, t * P:t * P + P] if t < NT else x_sample[:, 0]
                sp.dma_start(xin[0:src.shape[0], t % 2], src).then_inc(s_xin[t % 2], 16)
            for s in range(2):
                sp.dma_start(raw[:, s].rearrange("p (k n) -> p k n", k=KT),
                             w_ada2[:, :, s * 256:s * 256 + 256]).then_inc(s_raw[s], 16)
            with sp.Fori(1, N_ADA // 2) as i:
                for s in range(2):
                    sp.wait_ge(s_ada, i * 2 + (s - 1))
                    sp.dma_start(raw[:, s].rearrange("p (k n) -> p k n", k=KT),
                                 w_ada2[:, :, bass.ds(i * 512 + s * 256, 256)]).then_inc(s_raw[s], 16)
            for n in range(len(PAIRS)):
                if n < 2:
                    sp.wait_ge(s_ada, N_ADA - 1 + n)
                else:
                    sp.wait_ge(s_split, 2 * n - 2)
                load_pair(sp, n)

        def pool_phase_a(pool, link):
            pool.memset(eps[:], EPS).then_inc(s_eps, 1)
            pool.memset(misc[:], 0.0).then_inc(s_eps, 1)
            norm_lo(pool, O, act_hi, act_lo, 0)
            pool.wait_ge(s_hl, 8)
            pool.memset(O[:, :, 0:3], 0.0).then_inc(s_eps, 1)
            for n, (name, _, head_order) in enumerate(PAIRS):
                v = raw[:, n % 2].rearrange("p (k n) -> p k n", k=KT)
                pool.wait_ge(s_raw[n % 2], PAIR_AT[n])
                for b in range(2):
                    if 2 * n + b >= 2:
                        pool.wait_ge(s_mm, 2 * n + b - 1)
                    split_block(pool, weight_parts(name, b, v, head_order), KT, b, link)

        def pe_phase_a(pe):
            pe.wait_ge(s_cst, 16)
            pe.wait_ge(s_csil, 1)
            for k in range(KT):
                ins = pe.transpose(px[:, 0, k * 9:k * 9 + 9], crow[:, k * P:k * P + P], ident[0:9, 0:9])
            pe.wait_ge(s_par, 16 * N_PAR)
            pe.transpose(px[:, 0, 72:168], rows[:], ident[0:96, 0:96])
            pe.transpose(px[:, 0, 168:232], rowb[:], ident[0:64, 0:64])
            for m in range(16):
                ins = pe.transpose(px[:, 1, m * 24:m * 24 + 24], scn[:, m * P:m * P + P], ident[0:24, 0:24])
            ins.then_inc(s_ptr, 1)
            for t in range(NT + 1):
                w = P if t < NT else NB
                pe.wait_ge(s_xin[t % 2], 16 * (t // 2 + 1))
                if t >= 2:
                    pe.wait_ge(s_xe, t - 1)
                for k in range(KT):
                    ins = pe.transpose(pjf[t % 2][:, k * P:k * P + w], xin[0:w, t % 2, k * P:k * P + P], ident[0:w, 0:w])
                ins.then_inc(s_xt, 1)
            pe.wait_ge(s_pte, 4)
            with pe.Fori(0, N_ADA // 2) as i:
                for s in range(2):
                    pe.wait_ge(s_raw[s], i * 16 + 16)
                    v = raw[:, s].rearrange("p (k n) -> p k n", k=KT)
                    for b in range(2):
                        for k in range(KT):
                            ins = pe.matmul(px[:, 0, bass.ds(i * 36 + (s * 18 + b * 9), 9)], v[:, k, b * P:b * P + P],
                                            cT[:, k], start=(k == 0), stop=(k == KT - 1))
                    ins.then_inc(s_ada, 1)
            pe.wait_ge(s_xe, NT + 1)
            norm_sums(pe, E, 0)
            pe.wait_ge(s_hl, 8)
            pe.wait_ge(s_rt, 1)
            for b in range(2):
                pe.wait_ge(s_split, b + 1)
                products(pe, b, KT, act_hi, act_lo)
            pe_blocks(pe, 2, 8)
            pe.wait_ge(s_ev, 10)
            pe.wait_ge(s_rope, 7)
            for t in range(NT + 1):
                w = P if t < NT else NB
                if t >= 2:
                    pe.wait_ge(s_te, 2 * t - 2)
                o = pjf[t % 2]
                for j in range(2):
                    pe.transpose(o[0:w, j * P:j * P + P], kT[:, j, t * P:t * P + w], ident)
                    pe.transpose(o[0:w, 256 + j * P:256 + j * P + P], vT[:, j, t * P:t * P + w], ident)
                pe.transpose(o[0:w, 512:576], ikT[0:64, t * P:t * P + w], ident[0:64, 0:64])
                pe.transpose(o[0:w, 576:624], mT[0:48, t * P:t * P + w], ident[0:48, 0:48]).then_inc(s_tr, 1)
            pe.wait_ge(s_te, 2 * (NT + 1))
            for n, (t, h) in enumerate(IDX):
                if n >= 2:
                    pe.wait_ge(s_ir, n - 1)
                u, w = 64 * (h % 2), P * (t + 1)
                for c in range(0, w, 512):
                    e = min(w, c + 512)
                    ins = pe.matmul(pjf[n % 2][:, c:e], iqT[u:u + 64, h // 2, t * P:t * P + P], ikT[u:u + 64, c:e],
                                    start=True, stop=True)
                ins.then_inc(s_is, 1)
            pe.wait_ge(s_ir, len(IDX))
            pe_blocks(pe, 10, B_OUT - 10)
            pe.wait_ge(s_ev, B_OUT)
            pe.wait_ge(s_conv, 16)
            for m in range(16):
                if m % 8 == 0:
                    o = pjf[m // 8]
                ins = pe.transpose(o[0:11, (m % 8) * P:(m % 8) * P + P], xraw[:, m], ident)
            ins.then_inc(s_xrt, 1)

        st_at = [0, 0]
        uses = {}

        def act_phase_a(act, link):
            act.wait_ge(s_crow, 32)
            act.activation(crow, crow, ACT.Silu).then_inc(s_csil, 1)
            for t in range(NT + 1):
                w = P if t < NT else NB
                act.wait_ge(s_xt, t + 1)
                act.activation(xT[:, :, t * P:t * P + w], pjf[t % 2][:, 0:D].rearrange("p (k t) -> p k t", k=KT)[:, :, 0:w],
                               ACT.Copy).then_inc(s_xe, 1)
            act.wait_ge(s_xe, NT + 1)
            act.dma_start(d_x.rearrange("k p t -> p k t"), xT).then_inc(s_xs, 16)
            act.wait_ge(s_eps, 1)
            act.wait_ge(s_pte, 4)
            norm_squares(act, xT, E, 0)
            act.wait_ge(s_ct2, 1)
            norm_root(act, ROT[:], 0)
            norm_hi(act, O, act_hi, 0)
            pending = []

            def put(slot, dst, src):
                act.dma_start(dst, src).then_inc(s_st[slot], 16)
                st_at[slot] += 1

            def slot_stored(slot):
                if st_at[slot]:
                    act.wait_ge(s_st[slot], 16 * st_at[slot])

            def rope_in(b, r):
                s = b % 2
                act.wait_ge(s_mm, b + 1)
                if r >= 2:
                    act.wait_ge(s_rope, r - 1)
                act.activation(three(E[:, s]), prod[s], ACT.Copy).then_inc(s_ev, 1)

            r = 0
            act.wait_ge(s_ss, 8)
            for b in range(10):
                if b in ROPE:
                    rope_in(b, r)
                    r += 1
                else:
                    act.wait_ge(s_mm, b + 1)
                    if b < 8:
                        act.wait_ge(s_xs, 16)
                        act.activation(three(vT[:, b - 6]), prod[b % 2], ACT.Copy).then_inc(s_ev, 1)
                    else:
                        act.activation(three(mT[:]), prod[b % 2], ACT.Copy).then_inc(s_ev, 1)
            for t in range(NT + 1):
                w, s = (P if t < NT else NB), t % 2
                act.wait_ge(s_tr, t + 1)
                if t >= 2:
                    act.wait_ge(s_natd[s], 48 * (t // 2))
                    act.wait_ge(s_nat, 2 * t - 2)
                act.activation(nst[0:w, s, 0:512], pjf[s][0:w, 0:512], ACT.Copy).then_inc(s_te, 1)
                act.activation(nst[0:w, s, 512:624], pjf[s][0:w, 512:624], ACT.Copy).then_inc(s_te, 1)
                act.wait_ge(s_te, 2 * t + 2)
                if t < NT:
                    outs = (k_prompt[0, 0, t * P:t * P + P].rearrange("t h d -> t (h d)"),
                            v_prompt[0, 0, t * P:t * P + P].rearrange("t h d -> t (h d)"),
                            idxk_prompt[0, 0, t * P:t * P + P])
                else:
                    outs = (k_sample[0, :, 0].rearrange("t h d -> t (h d)"), v_sample[0, :, 0].rearrange("t h d -> t (h d)"),
                            idxk_sample[0, :, 0])
                for dst, src in zip(outs, (nst[0:w, s, 0:256], nst[0:w, s, 256:512], nst[0:w, s, 512:576])):
                    act.dma_start(dst, src).then_inc(s_natd[s], 16)
            act.wait_ge(s_vec, 96)
            link(act.activation(aneg[:], aneg[:], ACT.Exp))
            act.wait_ge(s_dtx, 1)
            act.activation(dtx[:, 2], dtx[:, 1], ACT.Exp, scale=-1.0).then_inc(s_dte, 1)
            act.wait_ge(s_rope, 7)
            for n, (t, h) in enumerate(IDX):
                w = P * (t + 1)
                act.wait_ge(s_is, n + 1)
                if n >= 2:
                    act.wait_ge(s_ia, n - 1)
                act.activation(E[:, n % 2, 0:w], pjf[n % 2][:, 0:w], ACT.Relu, scale=IDX_SCALE).then_inc(s_ir, 1)
            act.wait_ge(s_ia, len(IDX))
            for b in range(10, 18):
                rope_in(b, r)
                r += 1
                if b > 10:
                    act.wait_ge(s_rope, r - 1)
                    put((b - 1) % 2, d_q[b - 11], O[:, (b - 1) % 2, 3:3 + TT])
            act.wait_ge(s_rope, r)
            put(1, d_q[7], O[:, 1, 3:3 + TT])
            act.wait_ge(s_qs, 8)
            for b in range(18, 42):
                s = b % 2
                act.wait_ge(s_mm, b + 1)
                slot_stored(s)
                act.activation(three(O[:, s, 3:3 + TT]), prod[s], ACT.Silu if b < 26 else ACT.Sigmoid).then_inc(s_ev, 1)
                if b > 18:
                    act.wait_ge(s_ev, b)
                    put(1 - s, *prev)
                prev = ((d_z[b - 18] if b < 26 else d_g[b - 26]), O[:, s, 3:3 + TT])
            act.wait_ge(s_ev, 42)
            put(1, *prev)
            gates_at = tuple(st_at)
            act.wait_ge(s_eps, 3)
            def conv_out(m):
                s = m % 2
                act.wait_ge(s_conv, m + 1)
                link(act.activation(E[:, s], E[:, s], ACT.Silu))
                link(act.activation(convS[:, m], E[:, s, T:TT], ACT.Copy))
                put(s, d_c[m], E[:, s])
            for m in range(16):
                b, s = 42 + m, m % 2
                act.wait_ge(s_mm, b + 1)
                slot_stored(s)
                if m >= 2:
                    act.wait_ge(s_conv, m - 1)
                link(act.activation(three(O[:, s, 3:3 + TT]), prod[s], ACT.Copy))
                act.activation(three(E[:, s]), prod[s], ACT.Identity, bias=par[:, 80 + m:81 + m],
                               scale=taps[:, 48 + m:49 + m]).then_inc(s_ev, 1)
                if m:
                    conv_out(m - 1)
            conv_out(15)
            for s in range(2):
                slot_stored(s)
            act.wait_ge(s_xrt, 1)
            for j in range(2):
                link(act.activation(crst[:, j * 512:j * 512 + 512].rearrange("r (u a d) -> r a u d", u=2, a=4),
                                    pjf[0][0:11, j * 512:j * 512 + 512].rearrange("r (a u d) -> r a u d", u=2, a=4), ACT.Copy))
            link(act.activation(crst[:, D:2 * D], pjf[1][0:11, 0:D], ACT.Copy))
            store(act, conv_prompt[0, 0], crst[0:3])
            store(act, conv_sample[0, :, 2], crst[3:11])
            store(act, conv_sample[0, :, 0:2], state_conv[0, :, 1:3])
            act.wait_ge(s_out, 48)
            return gates_at

        def dve_phase_a(dve, link):
            dve.wait_ge(s_ptr, 1)
            dve.tensor_copy(cT[:], px[:, 0, 0:72].rearrange("p (k c) -> p k c", k=KT)).then_inc(s_pte, 1)
            dve.tensor_copy(par[:], px[:, 0, 72:168]).then_inc(s_pte, 1)
            dve.tensor_copy(taps[:], px[:, 0, 168:232]).then_inc(s_pte, 1)
            dve.tensor_copy(scT[:], px[:, 1, 0:384].rearrange("p (m c) -> p m c", m=16)).then_inc(s_pte, 1)
            dve.wait_ge(s_pte, 4)
            dve.wait_ge(s_ada, N_ADA)
            link(dve.tensor_tensor(modT[:], px[:, 0, 0:432].rearrange("p (m c) -> p m c", m=48),
                                   par[:, 0:48].unsqueeze(2).broadcast_to([P, 48, 9]), ALU.add))
            dve.sem_inc(s_ct2, 1)
            dve.wait_ge(s_xt, NT + 1)
            norm_apply(dve, link, xT, ROT[:], O, par[:, 48:56], 0, 1, 0)
            dve.wait_ge(s_hl, 8)
            dve.wait_ge(s_xs, 16)

            def rope(b, dst):
                s = b % 2
                dve.wait_ge(s_ev, b + 1)
                link(dve.stream_shuffle(ROT[:], E[:, s], TURN))
                link(dve.tensor_tensor(ROT[:], ROT[:], sin, ALU.mult))
                link(dve.tensor_tensor(dst, E[:, s], cos, ALU.mult))
                dve.tensor_tensor(dst, dst, ROT[:], ALU.add).then_inc(s_rope, 1)
                ropes[0] += 1
                dve.wait_ge(s_rope, ropes[0])

            ropes = [0]
            for b in range(4):
                rope(b, iqT[:, b])
            for b in range(4, 6):
                rope(b, kT[:, b - 4])
            rope(8, ikT[:])
            for h in range(8):
                link(dve.tensor_copy(iqs[:, h], iqT[64 * (h % 2):64 * (h % 2) + 64, h // 2, T:TT]))
            for t in range(NT + 1):
                w = P if t < NT else NB
                dve.wait_ge(s_te, 2 * t + 2)
                dve.tensor_copy(vn[0:w, t], nst[0:w, t % 2, 256:512]).then_inc(s_nat, 1)
                if t == 0:
                    dve.wait_ge(s_eps, 2)
                dve.tensor_copy(misc[0:w, t], nst[0:w, t % 2, 576:624]).then_inc(s_nat, 1)
            dve.wait_ge(s_nat, 2 * (NT + 1))
            dve.wait_ge(s_vec, 96)
            xv = dtx[:, 0].rearrange("p (t h) -> p t h", h=16)
            link(dve.tensor_tensor(xv, misc[:, :, 32:48], dtb[:].unsqueeze(1).broadcast_to([P, NT + 1, 16]), ALU.add))
            link(dve.tensor_scalar(dtx[:, 1], dtx[:, 0], -1.0, None, ALU.mult))
            link(dve.tensor_tensor(dtx[:, 1], dtx[:, 0], dtx[:, 1], ALU.max))
            dve.sem_inc(s_dtx, 1)
            link(dve.tensor_scalar(misc[:, :, 0:8], misc[:, :, 0:8], 8.0 ** -0.5, None, ALU.mult))
            dve.wait_ge(s_dte, 1)
            link(dve.tensor_scalar(dtx[:, 1], dtx[:, 2], 2.0, None, ALU.add))
            link(dve.reciprocal(dtx[:, 1], dtx[:, 1]))
            link(dve.tensor_tensor(dtx[:, 1], dtx[:, 1], dtx[:, 2], ALU.mult))
            link(dve.tensor_tensor(dtx[:, 2], dtx[:, 1], dtx[:, 1], ALU.mult))
            link(dve.tensor_scalar(dtx[:, 3], dtx[:, 2], 1.0 / 17, 1.0 / 15, ALU.mult, ALU.add))
            for c in (13, 11, 9, 7, 5, 3, 1):
                link(dve.tensor_tensor(dtx[:, 3], dtx[:, 3], dtx[:, 2], ALU.mult))
                link(dve.tensor_scalar(dtx[:, 3], dtx[:, 3], 1.0 / c, None, ALU.add))
            link(dve.tensor_tensor(dtx[:, 3], dtx[:, 3], dtx[:, 1], ALU.mult))
            link(dve.tensor_scalar(dtx[:, 3], dtx[:, 3], 2.0, None, ALU.mult))
            link(dve.tensor_scalar(dtx[:, 0], dtx[:, 0], 0.0, None, ALU.max))
            link(dve.tensor_tensor(dtn[:].rearrange("p t h -> p (t h)"), dtx[:, 0], dtx[:, 3], ALU.add))
            link(dve.tensor_scalar(dta[:], dtn[:], -1.0, None, ALU.mult))
            link(dve.tensor_tensor(dta[:], dta[:], aneg[:].unsqueeze(1).broadcast_to([P, NT + 1, 16]), ALU.mult))
            dve.wait_ge(s_tr, NT + 1)
            dve.wait_ge(s_natd[0], 48 * 5)
            dve.wait_ge(s_natd[1], 48 * 4)
            dve.wait_ge(s_te, 2 * (NT + 1))
            link(dve.memset(isc[:, 0:off(2)], 0.0))
            for t in range(2):
                d = isc[:, off(t) + t * P:off(t + 1)]
                link(dve.tensor_scalar(d, diag, -AWAY, None, ALU.mult))
            for n, (t, h) in enumerate(IDX):
                w = P * (t + 1)
                d = isc[:, off(t):off(t + 1)]
                dve.wait_ge(s_ir, n + 1)
                if h == 0:
                    dve.tensor_scalar(d, E[:, n % 2, 0:w], misc[:, t, h:h + 1], None, ALU.mult).then_inc(s_ia, 1)
                else:
                    dve.scalar_tensor_tensor(d, E[:, n % 2, 0:w], misc[:, t, h:h + 1], d, ALU.mult, ALU.add).then_inc(s_ia, 1)
                dve.wait_ge(s_ia, n + 1)
                if h == 7:
                    g = isc[:, off(t) + t * P:off(t + 1)]
                    link(dve.scalar_tensor_tensor(g, diag, -BARRED, g, ALU.mult, ALU.add))
            for b in range(10, 18):
                if b >= 12:
                    dve.wait_ge(s_st[b % 2], 16 * ((b - 10) // 2))
                    dve.wait_ge(s_qs, b - 11)
                if b == 10:
                    dve.wait_ge(s_eps, 3)
                rope(b, O[:, b % 2, 3:3 + TT])
                dve.tensor_copy(qs[:, b - 10], O[:, b % 2, 3 + T:3 + TT]).then_inc(s_qs, 1)
            for t in range(2, NT - 1):
                pick(dve, link, isc[:, off(t):off(t + 1)], m8[:], 0, ROUNDS)
            last = isc[:, off(NT - 1):off(NT)]
            for m in range(16):
                b, s = 42 + m, m % 2
                dve.wait_ge(s_ev, b + 1)
                for tap in range(3):
                    w = taps[:, 16 * tap + m:16 * tap + m + 1]
                    dve.scalar_tensor_tensor(E[:, s, T:TT], scT[:, m, tap:24:3], w, E[:, s, T:TT],
                                             ALU.mult, ALU.add).then_inc(s_cs, 1)
                    link(dve.scalar_tensor_tensor(E[:, s, 0:T], O[:, s, tap:tap + T], w, E[:, s, 0:T], ALU.mult, ALU.add))
                    dve.wait_ge(s_cs, 3 * m + tap + 1)
                dve.tensor_copy(xraw[:, m], O[:, s, T:T + 11]).then_inc(s_conv, 1)
                pick(dve, link, last, m8[:], 2 * m, 2 * m + 2)

        ROUNDS = TOPK // 8

        def pick(dve, link, row, m8, r0, r1):
            for _ in range(r0, r1):
                link(dve.max(m8, row))
                link(dve.match_replace(row, m8, row, PICKED))
            if r1 < ROUNDS:
                return
            link(dve.tensor_scalar(row, row, 2 * BARRED, AWAY, ALU.is_gt, ALU.mult))

        s_eps, s_ct2, s_rope, s_dtx, s_dte, s_conv, s_cs, s_xrt, s_qs = (
            sem(n) for n in ("s_eps", "s_ct2", "s_rope", "s_dtx", "s_dte", "s_conv", "s_cs", "s_xrt", "s_qs"))
        N_PAR = 9 + 12 + 5
        TURN = [p + 8 if p < 8 else p - 8 if p < 16 else p for p in range(32)]

        NC = NT // 2
        SD = {n: sem("ssd_" + n) for n in (
            "dtc", "cum", "ex", "xt", "xdt", "bn", "xw", "cb", "cbm", "mask", "seg", "decay", "ml", "y", "yo", "dst",
            "yn", "st", "yt", "xd", "g", "sq", "ss", "rt", "gcw", "done", "stt", "ste")}
        s_cin = [sem("s_cin0"), sem("s_cin1")]

        def by_head(ap, j):
            return ap[:, j * 512:j * 512 + 512].rearrange("p (u a d) -> p u a d", u=2, a=4)

        def in_blocks(ap, j):
            return ap[:, j * 512:j * 512 + 512].rearrange("p (a u d) -> p u a d", u=2, a=4)

        def sp_ssd(sp):
            c3, z3, g3 = (d.rearrange("m p t -> p m t") for d in (d_c, d_z, d_g))

            def load(s, c0):
                sp.dma_start(xb[:, s], c3[:, :, bass.ds(c0, P)]).then_inc(s_cin[s], 16)
                sp.dma_start(zc[:, s], z3[:, :, bass.ds(c0, P)]).then_inc(s_cin[s], 16)
                sp.dma_start(gc[:, s], g3[:, KT:2 * KT, bass.ds(c0, P)]).then_inc(s_cin[s], 16)

            for s in range(2):
                sp.wait_ge(s_st[s], 16 * ST_ALL)
            sp.wait_ge(s_split, B_OUT)
            sp.wait_ge(s_xrt, 1)
            sp.wait_ge(s_out, 48)
            sp.wait_ge(s_qs, 8)
            for s in range(2):
                load(s, s * P)
            with sp.Fori(1, NC) as i:
                for s in range(2):
                    sp.wait_ge(SD["done"], i * 2 + (s - 1))
                    load(s, i * 256 + s * P)

        def pe_ssd(pe):
            pe.wait_ge(s_out, 48)
            with pe.Fori(0, NC) as i:
                for s in range(2):
                    def at(n, k):
                        return i * (2 * n) + (s * n + k)
                    pe.wait_ge(SD["dtc"], at(1, 1))
                    for n, m in enumerate((le, gt, ones)):
                        ins = pe.matmul(px[:, 1, 16 * n:16 * n + 16], m, dac[:, s], start=True, stop=True)
                    ins.then_inc(SD["cum"], 1)
                    pe.wait_ge(s_cin[s], i * 48 + 48)
                    for m in range(KT):
                        pe.transpose(pjf[0][:, m * P:m * P + P], xb[:, s, m], ident)
                    for g in range(4):
                        ins = pe.transpose(pj[:, 0, 2, g * P:g * P + P], xb[:, s, 8 + g], ident)
                    ins.then_inc(SD["xt"], 1)
                    for g in range(4):
                        ins = pe.matmul(pj[:, 1, 2, g * P:g * P + P], xb[:, s, 8 + g], xb[:, s, 12 + g], start=True, stop=True)
                    ins.then_inc(SD["cb"], 1)
                    pe.wait_ge(SD["xdt"], at(2, 2))
                    for g in range(5):
                        if g < 4:
                            pe.wait_ge(SD["mask"], at(4, g + 1))
                            if g == 0:
                                pe.wait_ge(SD["bn"], at(1, 1))
                            elif g == 1:
                                pe.wait_ge(SD["cbm"], at(1, 1))
                            else:
                                pe.wait_ge(SD["decay"], at(4, g - 1))
                            for h in range(4):
                                ins = pe.matmul(pj[:, g % 2, 2, h * P:h * P + P], SM[:, g % 2, h], le, start=True, stop=True)
                            ins.then_inc(SD["seg"], 1)
                        if g > 0:
                            pe.wait_ge(SD["ml"], at(4, g))
                            for h in range(4):
                                hh = 4 * (g - 1) + h
                                ins = pe.matmul(pjf[1][:, hh * 64:hh * 64 + 64], ML[:, (g - 1) % 2, h], xdt[:, hh],
                                                start=True, stop=True)
                            ins.then_inc(SD["y"], 1)
                    for g in range(4):
                        ins = pe.matmul(pjf[0][:, g * 256:g * 256 + 256], xb[:, s, 12 + g], ST[:, g * 256:g * 256 + 256],
                                        start=True, stop=True)
                    ins.then_inc(SD["yo"], 1)
                    pe.wait_ge(SD["xw"], at(1, 1))
                    pe.wait_ge(SD["ex"], at(1, 1))
                    for g in range(4):
                        ins = pe.matmul(pxf[:, g * 256:g * 256 + 256], Bn[:, g], xw[:, 4 * g:4 * g + 4].rearrange("p h d -> p (h d)"),
                                        start=True, stop=True)
                    ins.then_inc(SD["dst"], 1)
                    pe.wait_ge(SD["yn"], at(1, 1))
                    for m in range(KT):
                        ins = pe.transpose(pjf[0][:, m * P:m * P + P], yn[:, m * P:m * P + P], ident)
                    ins.then_inc(SD["yt"], 1)
                    pe.wait_ge(SD["sq"], at(1, 1))
                    pe.wait_ge(SD["st"], at(1, 1))
                    for j in range(2):
                        for a in range(4):
                            ins = pe.matmul(px[:, 0, j * P:j * P + P], halves, xD[:, 4 * j + a], start=(a == 0), stop=(a == 3))
                    ins.then_inc(SD["ss"], 1)
            pe.wait_ge(SD["done"], NT)
            for m in range(KT):
                ins = pe.transpose(pjf[0][:, m * P:m * P + P], ST[:, m * P:m * P + P], ident)
            ins.then_inc(SD["stt"], 1)

        def act_ssd(act, link):
            act_keys(act)
            with act.Fori(0, NC) as i:
                for s in range(2):
                    def at(n, k):
                        return i * (2 * n) + (s * n + k)
                    act.wait_ge(SD["cum"], at(1, 1))
                    act.activation(ex[:], px[:, 1, 0:48], ACT.Exp).then_inc(SD["ex"], 1)
                    act.wait_ge(SD["xt"], at(1, 1))
                    act.activation(Bn[:], pj[:, 0, 2].rearrange("p (g n) -> p g n", g=4), ACT.Copy).then_inc(SD["bn"], 1)
                    for g in range(4):
                        act.wait_ge(SD["seg"], at(4, g + 1))
                        if g >= 2:
                            act.wait_ge(SD["ml"], at(4, g - 1))
                        act.activation(Lx[:, g % 2], pj[:, g % 2, 2].rearrange("p (h n) -> p h n", h=4), ACT.Exp
                                       ).then_inc(SD["decay"], 1)
                    act.wait_ge(SD["g"], at(1, 1))
                    act.activation(xD[:], gg[:], ACT.Square).then_inc(SD["sq"], 1)
                    act.wait_ge(SD["ss"], at(1, 1))
                    act.activation(rt[:], px[:, 0, 0:256].rearrange("p (j t) -> p j t", j=2), ACT.Sqrt, bias=eps[:],
                                   scale=1.0 / 256).then_inc(SD["rt"], 1)
            act.wait_ge(SD["stt"], 1)
            act.activation(yn[:], pjf[0][:, 0:D], ACT.Copy).then_inc(SD["ste"], 1)
            act.wait_ge(SD["ste"], 1)
            store(act, ssm_prompt[0, 0].rearrange("(m h) p n -> (h p) m n", m=KT), yn[:].rearrange("p (m n) -> p m n", m=KT))
            act.wait_ge(s_out, 64)

        def pool_ssd(pool, link):
            pool_keys(pool, link)
            with pool.Fori(0, NC) as i:
                for s in range(2):
                    def at(n, k):
                        return i * (2 * n) + (s * n + k)
                    pool.wait_ge(SD["dtc"], at(1, 1))
                    for g in range(4):
                        if g >= 2:
                            pool.wait_ge(SD["seg"], at(4, g - 1))
                        pool.tensor_tensor(SM[:, g % 2], gt.unsqueeze(1).broadcast_to([P, 4, P]),
                                           dac[:, s, 4 * g:4 * g + 4].unsqueeze(2).broadcast_to([P, 4, P]), ALU.mult
                                           ).then_inc(SD["mask"], 1)
                    pool.wait_ge(SD["xdt"], at(2, 2))
                    pool.wait_ge(SD["ex"], at(1, 1))
                    pool.tensor_tensor(xw[:], xdt[:], ex[:, 16:32].unsqueeze(2).broadcast_to([P, 16, 64]), ALU.mult
                                       ).then_inc(SD["xw"], 1)
                    pool.wait_ge(s_cin[s], i * 48 + 48)
                    pool.tensor_tensor(xD[:], xb[:, s, 0:KT], dskip[:].unsqueeze(2).broadcast_to([P, KT, P]), ALU.mult
                                       ).then_inc(SD["xd"], 1)
                    pool.tensor_tensor(gc[:, s], gc[:, s], par[:, 72:80].unsqueeze(2).broadcast_to([P, KT, P]), ALU.mult
                                       ).then_inc(SD["gcw"], 1)

        def dve_ssd(dve, link):
            for s in range(2):
                dve.wait_ge(s_st[s], 16 * ST_ALL)
            dve.wait_ge(s_out, 48)
            link(dve.memset(ST[:], 0.0))
            with dve.Fori(0, NC) as i:
                link.enter(i, 12)
                for s in range(2):
                    def at(n, k):
                        return i * (2 * n) + (s * n + k)
                    c = i * 2 + s
                    link(dve.tensor_scalar(dtc[:, s], dtn[:, bass.ds(c, 1)].rearrange("p a h -> p (a h)"), 1.0, None, ALU.mult))
                    dve.tensor_scalar(dac[:, s], dta[:, bass.ds(c, 1)].rearrange("p a h -> p (a h)"), 1.0, None, ALU.mult
                                      ).then_inc(SD["dtc"], 1)
                    dve.wait_ge(SD["xt"], at(1, 1))
                    for j in range(2):
                        dve.tensor_tensor(xdt[:, 8 * j:8 * j + 8].rearrange("p (u a) d -> p u a d", u=2),
                                          in_blocks(pjf[0], j),
                                          dtc[:, s, 8 * j:8 * j + 8].rearrange("p (u a) -> p u a", u=2).unsqueeze(3).broadcast_to([P, 2, 4, 64]),
                                          ALU.mult).then_inc(SD["xdt"], 1)
                    dve.wait_ge(SD["cb"], at(1, 1))
                    dve.tensor_tensor(cbm[:], pj[:, 1, 2].rearrange("p (g n) -> p g n", g=4),
                                      le.unsqueeze(1).broadcast_to([P, 4, P]), ALU.mult).then_inc(SD["cbm"], 1)
                    for g in range(4):
                        dve.wait_ge(SD["decay"], at(4, g + 1))
                        if g == 0:
                            dve.wait_ge(SD["cbm"], at(1, 1))
                        if g >= 2:
                            dve.wait_ge(SD["y"], at(4, g - 1))
                        dve.tensor_tensor(ML[:, g % 2], Lx[:, g % 2], cbm[:, g:g + 1].broadcast_to([P, 4, P]), ALU.mult
                                          ).then_inc(SD["ml"], 1)
                    dve.wait_ge(SD["yo"], at(1, 1))
                    dve.wait_ge(SD["y"], at(4, 4))
                    for j in range(2):
                        ins = dve.tensor_tensor(in_blocks(yn, j), by_head(pjf[0], j),
                                                ex[:, 8 * j:8 * j + 8].rearrange("p (u a) -> p u a", u=2).unsqueeze(3).broadcast_to([P, 2, 4, 64]),
                                                ALU.mult)
                        link(ins)
                    link(dve.tensor_tensor(in_blocks(yn, 0), in_blocks(yn, 0), by_head(pjf[1], 0), ALU.add))
                    dve.tensor_tensor(in_blocks(yn, 1), in_blocks(yn, 1), by_head(pjf[1], 1), ALU.add).then_inc(SD["yn"], 1)
                    st3 = ST.rearrange("p (h d) -> p h d", d=64)
                    dve.wait_ge(SD["dst"], at(1, 1))
                    link(dve.tensor_tensor(st3, st3, ex[:, 32:48].unsqueeze(2).broadcast_to([P, 16, 64]), ALU.mult))
                    dve.tensor_tensor(ST, ST, pxf, ALU.add).then_inc(SD["st"], 1)
                    dve.wait_ge(SD["yt"], at(1, 1))
                    dve.wait_ge(SD["xd"], at(1, 1))
                    link(dve.tensor_tensor(gg, pjf[0][:, 0:D].rearrange("p (k t) -> p k t", k=KT), xD, ALU.add))
                    dve.tensor_tensor(gg, gg, zc[:, s], ALU.mult).then_inc(SD["g"], 1)
                    dve.wait_ge(SD["rt"], at(1, 1))
                    dve.reciprocal(rt[:], rt[:]).then_inc(SD["rtr"], 1)
                    dve.wait_ge(SD["rtr"], at(1, 1))
                    dve.wait_ge(SD["gcw"], at(1, 1))
                    for j in range(2):
                        dve.tensor_tensor(gg[:, 4 * j:4 * j + 4], gg[:, 4 * j:4 * j + 4], rt[:, j:j + 1].broadcast_to([P, 4, P]),
                                          ALU.mult).then_inc(SD["gn"], 1)
                    dve.wait_ge(SD["gn"], at(2, 2))
                    dve.tensor_tensor(M[:, :, bass.ds(i * 256 + s * P, P)], gg, gc[:, s], ALU.mult).then_inc(SD["done"], 1)
            link.leave(NC)

        SD["rtr"], SD["gn"] = sem("ssd_rtr"), sem("ssd_gn")
        ST_ALL = 4 + 12 + 8

        HEADS = [(t, 4 * j + a, j, u, 8 * j + 4 * u + a) for t in range(NT) for j in range(2) for a in range(4) for u in range(2)]
        s_q = [sem("s_q0"), sem("s_q1")]
        AT = {n: sem("att_" + n) for n in ("kh", "kl", "q", "s", "m", "nm", "p", "t", "c0", "c1", "o", "n", "nt", "nr", "mul")}
        N_HEADS = len(HEADS)

        def sp_att(sp):
            q3, g3 = d_q.rearrange("m p t -> p m t"), d_g.rearrange("m p t -> p m t")
            sp.wait_ge(SD["done"], NT)
            sp.wait_ge(s_out, 64)
            for t in range(NT):
                if t >= 2:
                    sp.wait_ge(AT["q"], t - 1)
                for u in range(2):
                    for half in range(2):
                        sp.dma_start(qt[64 * half:64 * half + 64, t % 2, u], q3[64 * u:64 * u + 64, :, t * P:t * P + P]
                                     ).then_inc(s_q[t % 2], 16)
                if t >= 2:
                    sp.wait_ge(AT["mul"], 2 * (t - 1))
                sp.dma_start(ga[:, t % 2], g3[:, 0:KT, t * P:t * P + P]).then_inc(s_q[t % 2], 16)

        def pool_att(pool, link):
            pool.wait_ge(SD["done"], NT)
            pool.wait_ge(SD["ste"], 1)
            for t in range(NT):
                s = t % 2
                pool.wait_ge(s_q[s], 80 * (t // 2 + 1))
                if t >= 2:
                    pool.wait_ge(AT["s"], 16 * (t - 1))
                link(pool.tensor_copy(q_hl[:, s], qt[:, s]))
                for u in range(2):
                    low = slice(64 - 64 * u, P - 64 * u)
                    link(pool.tensor_tensor(q_hl[low, s, u], qt[low, s, u], q_hl[low, s, u].bitcast(F32), ALU.subtract))
                pool.sem_inc(AT["q"], 1)

        def act_keys(act):
            act.wait_ge(s_mm, B_OUT)
            for j in range(2):
                for u in range(2):
                    for half in range(2):
                        act.activation(k_hh[j][64 * half:64 * half + 64, u], kT[64 * u:64 * u + 64, j, 0:T], ACT.Copy
                                       ).then_inc(AT["kh"], 1)

        def pool_keys(pool, link):
            for j in range(2):
                pool.wait_ge(AT["kh"], 4 * j + 4)
                for u in range(2):
                    p = slice(64 * u, 64 * u + 64)
                    pool.tensor_tensor(k_lo[p, j], kT[p, j, 0:T], k_hh[j][p, u].bitcast(F32), ALU.subtract).then_inc(AT["kl"], 1)
                    pool.wait_ge(AT["kl"], 2 * j + u + 1)

        def groups(t):
            return 1 if t < 4 else 2

        def count(n, g):
            return sum(1 for t, *_ in HEADS[:n] if groups(t) > g)

        def pe_att(pe):
            pe.wait_ge(SD["ste"], 1)
            pe.wait_ge(AT["kl"], 4)

            def score(n):
                t, m, j, u, h = HEADS[n]
                w, s, p = P * (t + 1), t % 2, slice(64 * u, 64 * u + 64)
                if n % 16 == 0:
                    pe.wait_ge(AT["q"], t + 1)
                if n >= 2:
                    pe.wait_ge(AT["m"], n - 1)
                for c in range(0, w, 512):
                    e = min(w, c + 512)
                    pe.matmul(pjf[n % 2][:, c:e], q_hl[:, s, u, m], k_hh[j][:, u, c:e], start=True, stop=False)
                    ins = pe.matmul(pjf[n % 2][:, c:e], q_hl[p, s, u, m], k_lo[p, j, c:e], start=False, stop=True)
                ins.then_inc(AT["s"], 1)

            def turn(n):
                t = HEADS[n][0]
                pe.wait_ge(AT["p"], n + 1)
                for g in range(groups(t)):
                    k = count(n, g)
                    if k:
                        pe.wait_ge(AT["c%d" % g], k)
                    if g == 1:
                        pe.wait_ge(AT["nr"], max(n - 3, 0) // 8)
                    for x in range(4 * g, min(4 * g + 4, t + 1)):
                        ins = pe.transpose(pj[:, g, 2, (x % 4) * P:(x % 4) * P + P], Pr[:, n % 2, x * P:x * P + P], ident)
                    ins.then_inc(AT["t"], 1)

            def values(n):
                t, m, j, u, h = HEADS[n]
                if n % 8 == 0 and t:
                    pe.wait_ge(AT["n"], n // 8 - 1)
                for g in range(groups(t)):
                    pe.wait_ge(AT["c%d" % g], count(n, g) + 1)
                    for x in range(4 * g, min(4 * g + 4, t + 1)):
                        ins = pe.matmul(pxf[:, h * 64:h * 64 + 64], PT[:, n % 2, x * P:x * P + P],
                                        vn[:, x, (h // 4) * 64:(h // 4) * 64 + 64], start=(x == 0), stop=(x == t))
                ins.then_inc(AT["o"], 1)

            def outputs(f):
                j = f % 2
                pe.wait_ge(AT["n"], f + 1)
                if count(8 * f + 11, 1):
                    pe.wait_ge(AT["c1"], count(min(8 * f + 11, N_HEADS), 1))
                if f:
                    pe.wait_ge(AT["nr"], f)
                for m in range(4):
                    ins = pe.transpose(pj[:, 1, 2, m * P:m * P + P], an[:, (4 * j + m) * P:(4 * j + m) * P + P], ident)
                ins.then_inc(AT["nt"], 1)

            score(0)
            score(1)
            for n in range(N_HEADS + 3):
                if n + 2 < N_HEADS:
                    score(n + 2)
                if n < N_HEADS:
                    turn(n)
                if 1 <= n <= N_HEADS:
                    values(n - 1)
                if n >= 10 and n % 8 == 2:
                    outputs(n // 8 - 1)

        def act_att(act, link):
            act.wait_ge(SD["ste"], 1)
            for n in range(N_HEADS + 2):
                if n < N_HEADS:
                    w = P * (HEADS[n][0] + 1)
                    act.wait_ge(AT["nm"], n + 1)
                    if n >= 2:
                        act.wait_ge(AT["t"], count(n - 1, 0) + count(n - 1, 1))
                    act.activation(Pr[:, n % 2, 0:w], Sm[:, n % 2, 0:w], ACT.Exp, bias=nm[:, n:n + 1], scale=ATT_SCALE,
                                   accum_out=sm[:, n:n + 1]).then_inc(AT["p"], 1)
                if n >= 2:
                    second(act, n - 2)

        def second(act, n):
            t = HEADS[n][0]
            if groups(t) == 2:
                act.wait_ge(AT["t"], count(n + 1, 0) + count(n + 1, 1))
                if n >= 2:
                    act.wait_ge(AT["o"], n - 1)
                act.activation(PT[:, n % 2, 512:P * (t + 1)], pj[:, 1, 2, 0:P * (t + 1) - 512], ACT.Copy).then_inc(AT["c1"], 1)

        def dve_att(dve, link):
            dve.wait_ge(SD["done"], NT)

            def first(n):
                t = HEADS[n][0]
                w = min(512, P * (t + 1))
                dve.wait_ge(AT["t"], count(n, 0) + count(n, 1) + 1)
                if n >= 2:
                    dve.wait_ge(AT["o"], n - 1)
                dve.tensor_copy(PT[:, n % 2, 0:w], pj[:, 0, 2, 0:w]).then_inc(AT["c0"], 1)

            def normalize(f):
                t, j = f // 2, f % 2
                c = slice(8 * f, 8 * f + 8)
                dve.wait_ge(AT["p"], 8 * f + 8)
                link(dve.reciprocal(ri[:, c], sm[:, c]))
                dve.wait_ge(AT["o"], 8 * f + 8)
                if f >= 2:
                    dve.wait_ge(AT["nt"], f - 1)
                r = ri[:, c].rearrange("p (a u) -> p u a", u=2)
                dve.tensor_tensor(in_blocks(an, j), by_head(pxf, j), r.unsqueeze(3).broadcast_to([P, 2, 4, 64]), ALU.mult
                                  ).then_inc(AT["n"], 1)

            def gate(f):
                t, j = f // 2, f % 2
                g, c = ga[:, t % 2, 4 * j:4 * j + 4], slice(t * P, t * P + P)
                dve.wait_ge(AT["nt"], f + 1)
                dve.wait_ge(s_q[t % 2], 80 * (t // 2 + 1))
                dve.tensor_tensor(g, pj[:, 1, 2].rearrange("p (m t) -> p m t", m=4), g, ALU.mult).then_inc(AT["nr"], 1)
                dve.wait_ge(AT["nr"], f + 1)
                dve.tensor_tensor(M[:, 4 * j:4 * j + 4, c], M[:, 4 * j:4 * j + 4, c], g, ALU.add).then_inc(AT["mul"], 1)

            for n in range(N_HEADS + 6):
                if n < N_HEADS:
                    t = HEADS[n][0]
                    w = P * (t + 1)
                    dve.wait_ge(AT["s"], n + 1)
                    if n >= 2:
                        dve.wait_ge(AT["p"], n - 1)
                    dve.tensor_tensor_reduce(out=Sm[:, n % 2, 0:w], in0=pjf[n % 2][:, 0:w], in1=isc[:, off(t):off(t + 1)],
                                             scale=1.0, scalar=-3.0e38, op0=ALU.add, op1=ALU.max,
                                             accum_out=mx[:, n:n + 1]).then_inc(AT["m"], 1)
                    dve.wait_ge(AT["m"], n + 1)
                    dve.tensor_scalar(nm[:, n:n + 1], mx[:, n:n + 1], -ATT_SCALE, None, ALU.mult).then_inc(AT["nm"], 1)
                if n >= 13 and n % 8 == 5:
                    gate(n // 8 - 1)
                if 2 <= n < N_HEADS + 2:
                    first(n - 2)
                if n >= 11 and n % 8 == 3:
                    normalize(n // 8 - 1)

        s_pg = [sem("s_pg0"), sem("s_pg1")]
        SA = {n: sem("smp_" + n) for n in ("zero", "iqz", "it", "ik", "self", "is", "relu", "w", "wc", "sc", "scc", "pick",
                                           "kt", "k0", "k1", "s", "nm", "p", "pn", "pt", "ptc", "o", "att")}
        qzf, iqzf = qz[:], iqz[:]

        def page_loads(sp, cache, width, gate, base):
            def load(b_reg, s):
                for k in range(8):
                    v = sp.value_load(pgt[0:1, bass.ds(b_reg + k, 1)], min_val=0, max_val=n_phys - 1)
                    src = cache[0, bass.ds(v, 1)]
                    src = src.rearrange("a s d -> s (a d)") if width == 64 else src.rearrange("a s h d -> s (a h d)")
                    sp.dma_start(pg[:, s, k, 0:width], src).then_inc(s_pg[s], 16)
            for s in range(2):
                if base:
                    sp.wait_ge(base, 7 + s)
                load(s * 8, s)
            with sp.Fori(1, NB // 2) as i:
                for s in range(2):
                    sp.wait_ge(gate, i * 2 + (s - 1))
                    load(i * 16 + s * 8, s)

        def sp_smp(sp):
            sp.wait_ge(s_pt, 16)
            sp.wait_ge(AT["mul"], 2 * NT)
            page_loads(sp, cache_idx_k, 64, SA["it"], None)
            sp.wait_ge(s_natd[0], 48 * 5)
            sp.dma_start(vrow, v_sample[0, :, 0].rearrange("b h d -> b (h d)").unsqueeze(0)).then_inc(s_pt, 16)
            sp.dma_start(sg[:, 0], d_z.rearrange("m p t -> p m t")[:, :, T:TT]).then_inc(s_vec, 16)
            sp.dma_start(sg[:, 1], d_g.rearrange("m p t -> p m t")[:, 0:KT, T:TT]).then_inc(s_vec, 16)
            sp.dma_start(sg[:, 2], d_g.rearrange("m p t -> p m t")[:, KT:2 * KT, T:TT]).then_inc(s_vec, 16)
            page_loads(sp, cache_k, 256, SA["kt"], SA["it"])
            page_loads(sp, cache_v, 256, SA["o"], SA["kt"])

        def pe_smp(pe):
            pe.wait_ge(AT["mul"], 2 * NT)
            pe.wait_ge(SA["iqz"], 1)
            for b in range(NB):
                s = b % 2
                o = (pxf, pjf[1])[s]
                pe.wait_ge(s_pg[s], 128 * (b // 2 + 1))
                if b >= 2:
                    pe.wait_ge(SA["ik"], b - 1)
                for k in range(8):
                    ins = pe.transpose(o[0:64, k * P:k * P + P], pg[:, s, k, 0:64], ident)
                ins.then_inc(SA["it"], 1)
                if b:
                    idx_scores(pe, b - 1)
            idx_scores(pe, NB - 1)
            pe.transpose(px[0:64, 0, 0:8], bwt, ident[0:8, 0:8]).then_inc(SA["w"], 1)
            pe.wait_ge(SA["relu"], 1)
            pe.wait_ge(SA["wc"], 1)
            for c0, c1 in ((0, 512), (512, 1024), (1024, L)):
                ins = pe.matmul(pjf[1][0:8, c0:c1], bwz[:], sS[0:64, c0:c1], start=True, stop=True)
            ins.then_inc(SA["sc"], 1)
            pe.wait_ge(SA["scc"], 1)
            for b in range(NB):
                s = b % 2
                pe.wait_ge(s_pg[s], 512 + 128 * (b // 2 + 1))
                for j in range(2):
                    if b:
                        pe.wait_ge(SA["k%d" % j], b)
                    o = (pxf, pjf[1])[j]
                    for k in range(8):
                        ins = pe.transpose(o[:, k * P:k * P + P], pg[:, s, k, j * P:j * P + P], ident)
                ins.then_inc(SA["kt"], 1)
                if b:
                    key_scores(pe, b - 1)
            key_scores(pe, NB - 1)
            pe.wait_ge(SA["pick"], 1)
            for c0, c1 in ((0, 512), (512, 1024), (1024, L)):
                ins = pe.matmul(pjf[0][:, c0:c1], sel, sP[0:8, c0:c1], start=False, stop=True)
            ins.then_inc(SA["s"], 1)
            pe.wait_ge(SA["pn"], 1)
            for k in range(8):
                pe.transpose(pxf[:, k * P:k * P + P], sS[:, k * P:k * P + P], ident)
            pe.transpose(pj[0:1, 1, 0, 0:P], sS[:, T:L], ident).then_inc(SA["pt"], 1)
            pe.wait_ge(SA["ptc"], 2)
            pe.wait_ge(s_pt, 32)
            for b in range(NB):
                s = b % 2
                pe.wait_ge(s_pg[s], 1024 + 128 * (b // 2 + 1))
                c = slice(b * 16, b * 16 + 16)
                for j in range(2):
                    o = px[:, 0, j * P + b * 16:j * P + b * 16 + 16]
                    for k in range(8):
                        pe.matmul(o, pg[:, s, k, j * P:j * P + P], sT[:, k, c], start=(k == 0), stop=False)
                    ins = pe.matmul(o, vrow[0:1, b, j * P:j * P + P], sT[0:1, 8, c], start=False, stop=True)
                ins.then_inc(SA["o"], 1)

        def idx_scores(pe, b):
            pe.wait_ge(SA["ik"], b + 1)
            pe.wait_ge(SA["self"], b + 1)
            for c0, c1 in ((0, 512), (512, 1024), (1024, L)):
                ins = pe.matmul(pjf[0][0:64, c0:c1], iqzf[:, b * 64:b * 64 + 64], kTb[0:64, b % 2, 0, c0:c1],
                                start=(b == 0), stop=(b == NB - 1))
            ins.then_inc(SA["is"], 1)

        def key_scores(pe, b):
            for j in range(2):
                pe.wait_ge(SA["k%d" % j], b + 1)
            pe.wait_ge(SA["self"], NB + 2 * b + 2)
            for j in range(2):
                for c0, c1 in ((0, 512), (512, 1024), (1024, L)):
                    ins = pe.matmul(pjf[0][:, c0:c1], qzf[:, (2 * b + j) * P:(2 * b + j) * P + P], kTb[:, b % 2, j, c0:c1],
                                    start=(b == 0 and j == 0), stop=False)
            ins.then_inc(SA["is"], 1)

        def act_smp(act, link):
            act.wait_ge(AT["mul"], 2 * NT)
            for b in range(NB):
                s = b % 2
                act.wait_ge(SA["it"], b + 1)
                if b >= 2:
                    act.wait_ge(SA["is"], b - 1)
                act.activation(kTb[0:64, s, 0, 0:T], (pxf, pjf[1])[s][0:64, 0:T], ACT.Copy).then_inc(SA["ik"], 1)
            act.wait_ge(SA["is"], NB)
            act.activation(sS[0:64], pjf[0][0:64, 0:L], ACT.Relu, scale=IDX_SCALE).then_inc(SA["relu"], 1)
            act.wait_ge(SA["sc"], 1)
            act.activation(sP[0:8], pjf[1][0:8, 0:L], ACT.Copy).then_inc(SA["scc"], 1)
            for b in range(NB):
                act.wait_ge(SA["kt"], b + 1)
                act.wait_ge(SA["is"], NB + max(b - 1, 0))
                act.activation(kTb[:, b % 2, 0, 0:T], pxf, ACT.Copy).then_inc(SA["k0"], 1)
                act.activation(kTb[:, b % 2, 1, 0:T], pjf[1][:, 0:T], ACT.Copy).then_inc(SA["k1"], 1)
            act.wait_ge(SA["nm"], 1)
            act.activation(sS, pjf[0][:, 0:L], ACT.Exp, bias=scol[:, 1:2], scale=ATT_SCALE, accum_out=scol[:, 2:3]
                           ).then_inc(SA["p"], 1)
            act.wait_ge(SA["pt"], 1)
            act.activation(sT[:, 0:8], pxf.rearrange("p (k c) -> p k c", k=8), ACT.Copy).then_inc(SA["ptc"], 1)
            act.activation(sT[0:1, 8], pj[0:1, 1, 0, 0:P], ACT.Copy).then_inc(SA["ptc"], 1)

        def pool_smp(pool, link):
            pool.wait_ge(AT["mul"], 2 * NT)
            for b in range(NB):
                if b >= 2:
                    pool.wait_ge(SA["is"], b - 1)
                pool.tensor_copy(kTb[0:64, b % 2, 0, T:L], ikT[0:64, T + b:T + b + 1]).then_inc(SA["self"], 1)
            for b in range(NB):
                pool.wait_ge(SA["is"], NB + max(b - 1, 0))
                for j in range(2):
                    pool.tensor_copy(kTb[:, b % 2, j, T:L], kT[:, j, T + b:T + b + 1]).then_inc(SA["self"], 1)

        def dve_smp(dve, link):
            dve.wait_ge(AT["mul"], 2 * NT)
            link(dve.memset(qzf, 0.0))
            link(dve.memset(iqzf, 0.0))
            for j in range(2):
                for u in range(2):
                    at = j * P + 8 * j + 4 * u
                    link(dve.tensor_copy(qzf[64 * u:64 * u + 64, at:at + NB * 272].rearrange("p (b x) -> p b x", x=272)[:, :, 0:4],
                                         qs[64 * u:64 * u + 64, 4 * j:4 * j + 4].rearrange("p a b -> p b a")))
            link(dve.tensor_copy(iqzf[:, 0:NB * 72].rearrange("p (b x) -> p b x", x=72)[:, :, 0:8],
                                 iqs[:].rearrange("p h b -> p b h")))
            link(dve.tensor_tensor(bwt.rearrange("p (b h) -> p b h", h=8), misc[0:8, NT, 0:8].unsqueeze(1).broadcast_to([8, 8, 8]),
                                   ident[0:8, 0:8].unsqueeze(2).broadcast_to([8, 8, 8]), ALU.mult))
            dve.sem_inc(SA["iqz"], 1)
            dve.wait_ge(SA["w"], 1)
            dve.tensor_copy(bwz[:], px[0:64, 0, 0:8]).then_inc(SA["wc"], 1)
            dve.wait_ge(SA["scc"], 1)
            pick(dve, link, sP[0:8], m8b[0:8], 0, ROUNDS)
            dve.sem_inc(SA["pick"], 1)
            dve.wait_ge(SA["s"], 1)
            link(dve.tensor_reduce(scol[:, 0:1], pjf[0][:, 0:L], AX, ALU.max))
            dve.tensor_scalar(scol[:, 1:2], scol[:, 0:1], -ATT_SCALE, None, ALU.mult).then_inc(SA["nm"], 1)
            dve.wait_ge(SA["p"], 1)
            link(dve.reciprocal(scol[:, 3:4], scol[:, 2:3]))
            dve.tensor_scalar(sS, sS, scol[:, 3:4], None, ALU.mult).then_inc(SA["pn"], 1)
            dve.wait_ge(SA["o"], NB)
            for j in range(2):
                for u in range(2):
                    p = slice(64 * u, 64 * u + 64)
                    h = 8 * j + 4 * u
                    link(dve.tensor_copy(sg[p, 3, 4 * j:4 * j + 4], px[p, 0, j * P:j * P + P].rearrange("p (b h) -> p h b", h=16)[:, h:h + 4]))
            dve.wait_ge(s_vec, 96 + 48)
            link(dve.tensor_tensor(M[:, :, T:TT], sg[:, 3], sg[:, 1], ALU.mult))
            dve.tensor_copy(gates[:, 0:2], sg[:, 0:4:2]).then_inc(SA["att"], 1)
            dve.wait_ge(SA["att"], 1)

        s_s0 = [sem("s_s00"), sem("s_s01")]
        s_s1 = [sem("s_s10"), sem("s_s11")]
        SS = {n: sem("sss_" + n) for n in ("dt", "dtc", "e", "ec", "dec", "bx", "bc", "s1", "new", "y", "g", "sq", "ss", "rt", "m")}
        y8, dt8, dc8, xd8, g8, w8 = (sq4[:, n] for n in range(6))
        sq8, rt8 = sq4[:, 6], sq4[:, 7, 0:2]

        def sp_sss(sp):
            sp.wait_ge(SA["att"], 1)
            for b in range(NB):
                s = b % 2
                if b >= 2:
                    sp.wait_ge(SS["s1"], b - 1)
                for j in range(2):
                    for u in range(2):
                        h = 8 * j + 4 * u
                        sp.dma_start(S0[64 * u:64 * u + 64, s, 4 * j:4 * j + 4],
                                     state_ssm[0, b, h:h + 4].rearrange("a d n -> d a n")).then_inc(s_s0[s], 16)

        def pe_sss(pe):
            pe.wait_ge(SA["att"], 1)
            pe.transpose(px[0:16, 1, 0:8], dtn[0:8, NT], ident[0:8, 0:8])
            pe.transpose(px[0:16, 1, 8:16], dta[0:8, NT], ident[0:8, 0:8]).then_inc(SS["dt"], 1)
            pe.wait_ge(SS["dtc"], 1)
            for m in range(KT):
                ins = pe.matmul(px[:, 0, m * 16:m * 16 + 16], expand[:, m], dT[:].rearrange("h w b -> h (w b)"), start=True, stop=True)
            ins.then_inc(SS["e"], 1)
            for b in range(NB):
                if b >= 2:
                    pe.wait_ge(SS["y"], b - 1)
                pe.wait_ge(SS["bx"], b + 1)
                for w in range(4):
                    ins = pe.matmul(pj[:, b % 2, 0, w * P:w * P + P], BX[:, 2 * w:2 * w + 2].rearrange("p u d -> p (u d)"), ident,
                                    start=True, stop=True)
                ins.then_inc(SS["bc"], 1)
            pe.wait_ge(SS["sq"], 1)
            for j in range(2):
                for a in range(4):
                    ins = pe.matmul(px[:, 1, j * 8:j * 8 + 8], halves, sq8[:, 4 * j + a], start=(a == 0), stop=(a == 3))
            ins.then_inc(SS["ss"], 1)

        def act_sss(act, link):
            act.wait_ge(SS["ec"], 1)
            act.activation(dc8, dc8, ACT.Exp).then_inc(SS["dec"], 1)
            for b in range(NB):
                act.wait_ge(SS["new"], b + 1)
                for j in range(2):
                    for u in range(2):
                        h = 8 * j + 4 * u
                        act.dma_start(ssm_sample[0, b, h:h + 4].rearrange("a d n -> d a n"),
                                      S1[64 * u:64 * u + 64, b % 2, 4 * j:4 * j + 4]).then_inc(s_s1[b % 2], 16)
            act.wait_ge(SS["g"], 1)
            act.activation(sq8, g8, ACT.Square).then_inc(SS["sq"], 1)
            act.wait_ge(SS["ss"], 1)
            act.activation(rt8, px[:, 1, 0:16].rearrange("p (j b) -> p j b", j=2), ACT.Sqrt, bias=eps[:], scale=1.0 / 256
                           ).then_inc(SS["rt"], 1)
            for s in range(2):
                act.wait_ge(s_s1[s], 64 * 4)

        def pool_sss(pool, link):
            pool.wait_ge(SS["dec"], 1)
            for b in range(NB):
                s = b % 2
                pool.wait_ge(s_s0[s], 64 * (b // 2 + 1))
                if b >= 2:
                    pool.wait_ge(s_s1[s], 64 * (b // 2))
                    pool.wait_ge(SS["y"], b - 1)
                pool.tensor_tensor(S1[:, s], S0[:, s], dc8[:, :, b:b + 1].broadcast_to([P, KT, P]), ALU.mult).then_inc(SS["s1"], 1)

        def dve_sss(dve, link):
            dve.wait_ge(SS["dt"], 1)
            dve.tensor_copy(dT[:], px[0:16, 1, 0:16].rearrange("p (w b) -> p w b", w=2)).then_inc(SS["dtc"], 1)
            dve.wait_ge(SS["e"], 1)
            e = px[:, 0, 0:P].rearrange("p (m w b) -> p m w b", m=KT, w=2)
            link(dve.tensor_copy(dt8, e[:, :, 0]))
            dve.tensor_copy(dc8, e[:, :, 1]).then_inc(SS["ec"], 1)
            link(dve.tensor_tensor(xd8, dt8, convS[:, 0:KT], ALU.mult))

            def spread(b):
                if b:
                    dve.wait_ge(SS["bc"], b)
                dve.tensor_copy(BX[:], convS[:, KT:16, b:b + 1].broadcast_to([P, 8, 64])).then_inc(SS["bx"], 1)

            spread(0)
            for b in range(NB):
                s = b % 2
                if b + 1 < NB:
                    spread(b + 1)
                dve.wait_ge(SS["bc"], b + 1)
                bc = pj[:, s, 0].rearrange("p (w j n) -> p w j n", w=2, j=2)
                for j in range(2):
                    link(dve.tensor_tensor(S2[:, s, 4 * j:4 * j + 4], bc[:, 0, j:j + 1].broadcast_to([P, 4, P]),
                                           xd8[:, 4 * j:4 * j + 4, b:b + 1].broadcast_to([P, 4, P]), ALU.mult))
                dve.wait_ge(SS["s1"], b + 1)
                link(dve.tensor_tensor(S1[:, s], S1[:, s], S2[:, s], ALU.add))
                dve.sem_inc(SS["new"], 1)
                for j in range(2):
                    link(dve.tensor_tensor(S3[:, 4 * j:4 * j + 4], bc[:, 1, j:j + 1].broadcast_to([P, 4, P]),
                                           S1[:, s, 4 * j:4 * j + 4], ALU.mult))
                dve.tensor_reduce(y8[:, :, b:b + 1], S3[:], AX, ALU.add).then_inc(SS["y"], 1)
            dve.wait_ge(SS["y"], NB)
            link(dve.tensor_tensor(w8, convS[:, 0:KT], dskip[:].unsqueeze(2).broadcast_to([P, KT, NB]), ALU.mult))
            link(dve.tensor_tensor(g8, y8, w8, ALU.add))
            dve.tensor_tensor(g8, g8, gates[:, 0], ALU.mult).then_inc(SS["g"], 1)
            dve.wait_ge(SS["g"], 1)
            dve.wait_ge(SS["rt"], 1)
            link(dve.reciprocal(rt8, rt8))
            for j in range(2):
                link(dve.tensor_tensor(g8[:, 4 * j:4 * j + 4], g8[:, 4 * j:4 * j + 4], rt8[:, j:j + 1].broadcast_to([P, 4, NB]), ALU.mult))
            link(dve.tensor_tensor(g8, g8, par[:, 72:80].unsqueeze(2).broadcast_to([P, KT, NB]), ALU.mult))
            link(dve.tensor_tensor(g8, g8, gates[:, 1], ALU.mult))
            dve.tensor_tensor(M[:, :, T:TT], M[:, :, T:TT], g8, ALU.add).then_inc(SS["m"], 1)

        FS = 16
        s_mh, s_ml, s_uh, s_ul = (sem(n) for n in ("s_mh", "s_ml", "s_uh", "s_ul"))
        s_yt, s_ye = sem("s_yt"), sem("s_ye")
        s_yo = [sem("s_yo0"), sem("s_yo1")]
        wo_view = [raw[:, s].rearrange("p (k n) -> p k n", k=KT) for s in range(2)]
        N0 = len(PAIRS)

        def out_at(n):
            return raw_at[(N0 + n) % 2] + 64 * (n // 2 + 1)

        SU, SV = (N0 + 4) % 2, (N0 + 5) % 2
        MLP_AT = [raw_at[s] + 128 for s in range(2)]

        def sp_out(sp, out_pairs):
            sp.wait_ge(SD["done"], NT)
            for n in out_pairs:
                s = (N0 + n) % 2
                sp.wait_ge(s_split, 2 * (N0 + n) - 2)
                for j in range(2):
                    for u in range(2):
                        sp.dma_start(wo_view[s][64 * u:64 * u + 64, 4 * j:4 * j + 4], w_out2[j, u][:, :, n * 256:n * 256 + 256]
                                     ).then_inc(s_raw[s], 16)

        def sp_mlp(sp):
            sp.wait_ge(s_ml, KT)
            sp.dma_start(x2T[:], d_x.rearrange("k p t -> p k t")).then_inc(s_crow, 16)

            def up(e):
                sp.dma_start(wo_view[SU], w_up2[:, :, bass.ds(e * 256, 256)]).then_inc(s_raw[SU], 16)

            def down(e):
                sp.dma_start(raw[:, SV].rearrange("p (k n) -> p k n", k=2), w_dn3[bass.ds(e, 1)].rearrange("e p k n -> p (e k) n")
                             ).then_inc(s_raw[SV], 16)

            sp.wait_ge(s_split, B_MLP - 2)
            up(0)
            sp.wait_ge(s_split, B_MLP)
            down(0)
            sp.wait_ge(s_split, B_MLP + 2)
            up(1)
            with sp.Fori(0, FS - 2) as e:
                sp.wait_ge(s_split, e * 10 + (B_MLP + 4))
                up(e + 2)
                sp.wait_ge(s_split, e * 10 + (B_MLP + 12))
                down(e + 1)
            sp.wait_ge(s_split, (FS - 2) * 10 + (B_MLP + 12))
            down(FS - 1)

        w_dn3 = w_down[0].rearrange("(e k p) n -> e p k n", p=P, k=2)

        def pool_mlp(pool, link):
            pool.wait_ge(SS["m"], 1)
            for k in range(KT):
                pool.wait_ge(s_mh, k + 1)
                pool.tensor_tensor(alo[:, k], M[:, k], ahi[:, k].bitcast(F32), ALU.subtract).then_inc(s_ml, 1)
            for n in range(4):
                s = (N0 + n) % 2
                pool.wait_ge(s_raw[s], out_at(n))
                for b in range(2):
                    pool.wait_ge(s_mm, 2 * (N0 + n) + b - 1)
                    split_block(pool, [(wo_view[s][:, :, b * P:b * P + P], 0, P)], KT, b, link)
            link(pool.memset(zero, 0.0))
            norm_lo(pool, OC, ahi, alo, 1)
            dn = raw[:, SV].rearrange("p (k n) -> p k n", k=2)

            def up(at, block, raw_n):
                pool.wait_ge(s_raw[SU], at(16, MLP_AT[SU] + 16 * raw_n))
                for b in range(2):
                    pool.wait_ge(s_mm, at(10, block + b - 1))
                    half_split(pool, wo_view[SU][:, :, b * P:b * P + P], KT, b, link)

            def down(at, block):
                pool.wait_ge(s_raw[SV], at(16, MLP_AT[SV] + 16))
                for b in range(8):
                    pool.wait_ge(s_mm, at(10, block + b - 1))
                    half_split(pool, dn[:, :, b * P:b * P + P], 2, b % 2, link)

            up(lambda per, c: c, B_MLP, 1)
            with pool.Fori(0, FS - 1) as e:
                link.enter(e, 10)
                up(lambda per, c: e * per + c, B_MLP + 2, 2)
                down(lambda per, c: e * per + c, B_MLP + 4)
            link.leave(FS - 1)
            down(lambda per, c: (FS - 1) * per + c, B_MLP + 2)

        def half_split(pool, src, kt, hs, link):
            link(pool.tensor_tensor(whi[:, hs, 0:kt], src, zero.unsqueeze(1).broadcast_to([P, kt, P]), ALU.add))
            pool.tensor_tensor(wlo[:, hs, 0:kt], src, whi[:, hs, 0:kt].bitcast(F32), ALU.subtract).then_inc(s_split, 1)

        def slices(eng, step, link, per=0):
            with eng.Fori(0, FS // 2 - 1) as i:
                if link:
                    link.enter(i, 2 * per)
                for s in range(2):
                    step(lambda n, c: i * (2 * n) + (s * n + c), s)
            if link:
                link.leave(FS // 2 - 1)
            step(lambda n, c: (FS - 2) * n + c, 0)

        def pe_mlp(pe):
            pe.wait_ge(s_ml, KT)
            pe.wait_ge(SS["m"], 1)
            for s in range(2):
                pe.wait_ge(s_split, B_OUT + s + 1)
                products(pe, s, KT, ahi, alo)
            with pe.Fori(1, KT // 2) as i:
                for s in range(2):
                    pe.wait_ge(s_split, i * 2 + (B_OUT + s + 1))
                    pe.wait_ge(s_evd, i * 2 + (s - 1))
                    products(pe, s, KT, ahi, alo)
            pe.wait_ge(s_evd, KT)
            norm_sums(pe, OC, 1)
            pe.wait_ge(s_hl, 16)

            def down(at, s, block, last=False):
                pe.wait_ge(s_ul, at(2, 2))
                for m in range(KT):
                    pe.wait_ge(s_split, at(10, block + m + 1))
                    if m < 2 and not last:
                        pe.wait_ge(s_ev, at(2, B_OUT + 2 + m + 1))
                    elif m >= 2:
                        pe.wait_ge(s_evd, at(KT, KT + m - 1))
                    else:
                        pe.wait_ge(s_evd, at(KT, m - 1 + KT))
                    products(pe, m % 2, 2, u_hi[:, s], u_lo[:, s])

            def step(at, s):
                for b in range(2):
                    pe.wait_ge(s_split, at(10, B_MLP + 2 + b + 1))
                    pe.wait_ge(s_evd, at(KT, KT + b - 1))
                    products(pe, b, KT, ahi, alo)
                down(at, s, B_MLP + 4)

            for b in range(2):
                pe.wait_ge(s_split, B_MLP + b + 1)
                products(pe, b, KT, ahi, alo)
            pe.wait_ge(s_ev, B_OUT + 2)
            slices(pe, step, None)
            down(lambda per, c: (FS - 1) * per + c, 1, B_MLP + 2, last=True)
            pe.wait_ge(s_evd, KT + KT * FS)
            norm_sums(pe, OC, 2)
            pe.wait_ge(s_fn, KT)
            for t in range(NT + 1):
                w = P if t < NT else NB
                if t >= 2:
                    pe.wait_ge(s_ye, t - 1)
                for k in range(KT):
                    ins = pe.transpose(pjf[t % 2][0:w, k * P:k * P + P], x2T[:, k, t * P:t * P + w], ident)
                ins.then_inc(s_yt, 1)

        def act_mlp(act, link):
            act.wait_ge(SS["m"], 1)
            for k in range(KT):
                act.activation(ahi[:, k], M[:, k], ACT.Copy).then_inc(s_mh, 1)
            act.wait_ge(s_x2, KT)
            norm_squares(act, x2T, OC, 1)
            norm_root(act, RC[:], 1)
            norm_hi(act, OC, ahi, 1)

            def up(at, s, e):
                for b in range(2):
                    act.wait_ge(s_mm, at(10, B_MLP + 2 * e + b + 1))
                    if e:
                        act.wait_ge(s_ul, at(2, b + 1))
                    act.activation(three(OC[:, b]), prod[b], ACT.Relu).then_inc(s_ev, 1)
                for b in range(2):
                    act.wait_ge(s_sq2, at(2, 2 * e + b + 1))
                    act.activation(u_hi[:, s, b], OC[:, b], ACT.Copy).then_inc(s_uh, 1)

            up(lambda per, c: c, 0, 0)
            slices(act, lambda at, s: up(at, 1 - s, 1), None)
            act.wait_ge(s_x2, KT + FS * KT)
            norm_squares(act, x2T, OC, 2)
            norm_root(act, RC[:], 2)
            for t in range(NT + 1):
                w = P if t < NT else NB
                act.wait_ge(s_yt, t + 1)
                if t >= 2:
                    act.wait_ge(s_yo[t % 2], 16 * (t // 2))
                act.activation(OC[0:w, t % 2, 0:D], pjf[t % 2][0:w, 0:D], ACT.Copy).then_inc(s_ye, 1)
                act.wait_ge(s_ye, t + 1)
                act.dma_start(y_prompt[0, t * P:t * P + P] if t < NT else y_sample[:, 0], OC[0:w, t % 2, 0:D]).then_inc(s_yo[t % 2], 16)
            act.wait_ge(s_yo[0], 16 * 5)
            act.wait_ge(s_yo[1], 16 * 4)

        def add_gated(dve, slot, m, gate, signal):
            x, g = x2T[:, m], modT[:, gate + m, 8:9]
            a = x[:, 0:2 * W3].rearrange("p (a b) -> p a b", a=2)
            end = W3 - NB
            dve.scalar_tensor_tensor(a, prod[slot][:, 0:2], g, a, ALU.mult, ALU.add).then_inc(s_add, 1)
            dve.scalar_tensor_tensor(x[:, 2 * W3:T], prod[slot][:, 2, 0:end], g, x[:, 2 * W3:T], ALU.mult, ALU.add).then_inc(s_add, 1)
            dve.tensor_tensor(tmp8[:, slot], prod[slot][:, 2, end:W3], modT[:, gate + m, 0:8], ALU.mult).then_inc(s_add, 1)

        def dve_mlp(dve, link):
            dve.wait_ge(s_crow, 48)
            for m in range(KT):
                dve.wait_ge(s_mm, B_OUT + m + 1)
                add_gated(dve, m % 2, m, 16, None)
                dve.wait_ge(s_add, 3 * m + 3)
                dve.tensor_tensor(x2T[:, m, T:TT], x2T[:, m, T:TT], tmp8[:, m % 2], ALU.add).then_inc(s_x2, 1)
                dve.sem_inc(s_evd, 1)
            dve.wait_ge(s_x2, KT)
            norm_apply(dve, link, x2T, RC[:], OC, par[:, 56:64], 24 // 8, 32 // 8, 1)

            def up(at, s, e):
                for b in range(2):
                    dve.wait_ge(s_ev, at(2, B_OUT + 2 * e + b + 1))
                    dve.tensor_tensor(OC[:, b], OC[:, b], OC[:, b], ALU.mult).then_inc(s_sq2, 1)
                for b in range(2):
                    dve.wait_ge(s_uh, at(2, 2 * e + b + 1))
                    dve.tensor_tensor(u_lo[:, s, b], OC[:, b], u_hi[:, s, b].bitcast(F32), ALU.subtract).then_inc(s_ul, 1)

            def down(at, block):
                for m in range(KT):
                    dve.wait_ge(s_mm, at(10, block + m + 1))
                    add_gated(dve, m % 2, m, 40, None)
                    dve.wait_ge(s_add, at(3 * KT, 3 * KT + 3 * m + 3))
                    dve.tensor_tensor(x2T[:, m, T:TT], x2T[:, m, T:TT], tmp8[:, m % 2], ALU.add).then_inc(s_x2, 1)
                    dve.wait_ge(s_x2, at(KT, KT + m + 1))
                    dve.sem_inc(s_evd, 1)

            up(lambda per, c: c, 0, 0)
            slices(dve, lambda at, s: (up(at, 1 - s, 1), down(at, B_MLP + 4)), None)
            down(lambda per, c: (FS - 1) * per + c, B_MLP + 2)
            dve.wait_ge(s_rt, 3)
            link(dve.reciprocal(RC[:], RC[:]))
            for k in range(KT):
                link(dve.tensor_tensor(x2T[:, k], x2T[:, k], RC[:], ALU.mult))
                dve.tensor_scalar(x2T[:, k], x2T[:, k], par[:, 64 + k:65 + k], None, ALU.mult).then_inc(s_fn, 1)

        s_x2, s_add, s_sq2, s_fn, s_evd = (sem(n) for n in ("s_x2", "s_add", "s_sq2", "s_fn", "s_evd"))

        block = ctx.enter_context(nc.Block())

        @block.sync
        def _(sp):
            sp_phase_a(sp)
            sp_ssd(sp)
            sp_out(sp, (0, 1))
            sp_att(sp)
            sp_smp(sp)
            sp_sss(sp)
            sp_out(sp, (2, 3))
            sp_mlp(sp)

        @block.gpsimd
        def _(pool):
            link = Link(pool, s_c["pool"])
            pool_phase_a(pool, link)
            pool_ssd(pool, link)
            pool_att(pool, link)
            pool_smp(pool, link)
            pool_sss(pool, link)
            pool_mlp(pool, link)

        @block.tensor
        def _(pe):
            pe_phase_a(pe)
            pe_ssd(pe)
            pe_att(pe)
            pe_smp(pe)
            pe_sss(pe)
            pe_mlp(pe)

        @block.scalar
        def _(act):
            link = Link(act, s_c["act"])
            act_phase_a(act, link)
            act_ssd(act, link)
            act_att(act, link)
            act_smp(act, link)
            act_sss(act, link)
            act_mlp(act, link)
            act.wait_ge(s_out, n_out[0])

        @block.vector
        def _(dve):
            link = Link(dve, s_c["dve"])
            dve_phase_a(dve, link)
            dve_ssd(dve, link)
            dve_att(dve, link)
            dve_smp(dve, link)
            dve_sss(dve, link)
            dve_mlp(dve, link)


def constants():
    import numpy as np
    f = np.float32
    c = np.zeros((P, K_END), f)
    p, q = np.arange(P)[:, None], np.arange(P)[None, :]
    c[:, K_ID:K_ID + P] = p == q
    c[:, K_ONE:K_ONE + P] = 1
    c[:, K_HALF:K_HALF + P] = p // 64 == q // 64
    c[:, K_LE:K_LE + P] = p <= q
    c[:, K_GT:K_GT + P] = p > q
    c[:, K_DIAG:K_DIAG + P] = -(q > p).astype(f)
    d = np.arange(P) % 64
    pos = np.concatenate([np.arange(T), np.full(NB, T)]).astype(f)
    inv = f(500000.0) ** (-np.arange(8, dtype=f) * f(2.0) / f(16))
    ang = (pos[None, :] * inv.astype(f)[d % 8][:, None]).astype(f)
    turned = (d < 16)[:, None]
    c[:, K_COS:K_COS + TT] = np.where(turned, np.cos(ang), 1)
    c[:, K_SIN:K_SIN + TT] = np.where(turned, np.where((d < 8)[:, None], -np.sin(ang), np.sin(ang)), 0)
    c[0:8, K_SEL:K_SEL + P] = np.arange(8)[:, None] == q // 16
    for m in range(8):
        head = 8 * (m // 4) + 4 * (np.arange(P) // 64) + m % 4
        c[0:16, K_EXP + m * P:K_EXP + (m + 1) * P] = np.arange(16)[:, None] == head[None, :]
    c[0:8, K_SH:K_SH + 64] = np.arange(8)[:, None] == np.arange(64)[None, :] % 8
    c[0:64, K_BD:K_BD + 8] = np.arange(64)[:, None] // 8 == np.arange(8)[None, :]
    return c


_INS = ["x_prompt", "x_sample", "cache_k", "cache_v", "cache_idx_k", "state_conv", "state_ssm", "page_table",
        "c_prompt", "c_sample", "w_ada", "b_ada", "norm1_w", "w_in", "conv_w", "conv_b", "dt_bias", "a_log", "d_skip",
        "ssm_norm_w", "w_out", "norm2_w", "w_up", "w_down", "final_norm_w"]
_OUTS = [(1, T, D), (NB, 1, D), (1, 1, T, 4, 64), (1, 1, T, 4, 64), (1, 1, T, 64), (1, 1, 3, 2 * D),
         (1, 1, 16, 64, P), (1, NB, 1, 4, 64), (1, NB, 1, 4, 64), (1, NB, 1, 64), (1, NB, 3, 2 * D), (1, NB, 16, 64, P)]


def kernel(**inputs):
    import numpy as np
    import concourse.bacc as bacc
    from concourse.bass_utils import run_bass_kernel_spmd

    nc = bacc.Bacc("TRN2", target_bir_lowering=False, num_devices=1)
    arrays, args = {}, []
    for name in _INS:
        a = np.ascontiguousarray(inputs[name])
        arrays["in_" + name] = a
        args.append(nc.dram_tensor("in_" + name, a.shape, mybir.dt.from_np(a.dtype), kind="ExternalInput").ap())
    arrays["in_consts"] = constants()
    args.append(nc.dram_tensor("in_consts", (P, K_END), F32, kind="ExternalInput").ap())
    for i, shape in enumerate(_OUTS):
        args.append(nc.dram_tensor(f"out_{i}", shape, F32, kind="ExternalOutput").ap())
    program(nc, *args)
    r = run_bass_kernel_spmd(nc, [arrays], core_ids=[0])
    return tuple(r.results[0][f"out_{i}"] for i in range(len(_OUTS)))
```

```python
from contextlib import ExitStack

import concourse.bass as bass
from concourse import mybir
from concourse.alu_op_type import AluOpType as ALU

F32 = mybir.dt.float32
F32R = mybir.dt.float32r
I32 = mybir.dt.int32
ACT = mybir.ActivationFunctionType
AX = mybir.AxisListType.X

P = 128
D = 1024
T = 1024
NB = 8
TT = T + NB
W3 = TT // 3
KT = D // P
NT = T // P
L = 1025
TOPK = 256
IDX_SCALE = 0.125
ATT_SCALE = 0.125
EPS = 1e-6
PICKED = -3.0e38
BARRED = -1.0e38
AWAY = -1.0e30
WIN = 7256
C_Q, C_K, C_IQ, C_IK, C_IW, C_Z, C_X, C_DT, C_G = 0, 1024, 1536, 2048, 2112, 2120, 3144, 5192, 5208

K_ID, K_ONE, K_HALF, K_LE, K_GT, K_DIAG, K_COS, K_SIN = 0, 128, 256, 384, 512, 640, 768, 768 + TT
K_SEL = K_SIN + TT
K_EXP = K_SEL + P
K_END = K_EXP + 8 * P


def off(t):
    return P * t * (t + 1) // 2


class Link:

    def __init__(self, eng, sem):
        self.eng, self.sem, self.base, self.k, self.i, self.per = eng, sem, 0, 0, None, 0

    def __call__(self, ins):
        ins.then_inc(self.sem, 1)
        self.k += 1
        n = self.base + self.k
        self.eng.wait_ge(self.sem, n if self.i is None else self.i * self.per + n)

    def enter(self, i, per):
        self.base, self.k, self.i, self.per = self.base + self.k, 0, i, per

    def leave(self, n):
        assert self.k == self.per, (self.k, self.per)
        self.base, self.k, self.i = self.base + n * self.per, 0, None


def program(nc, x_prompt, x_sample, cache_k, cache_v, cache_idx_k, state_conv, state_ssm, page_table,
            c_prompt, c_sample, w_ada, b_ada, norm1_w, w_in, conv_w, conv_b, dt_bias, a_log, d_skip,
            ssm_norm_w, w_out, norm2_w, w_up, w_down, final_norm_w, consts,
            y_prompt, y_sample, k_prompt, v_prompt, idxk_prompt, conv_prompt, ssm_prompt,
            k_sample, v_sample, idxk_sample, conv_sample, ssm_sample):
    n_phys = cache_k.shape[1]
    with ExitStack() as ctx:
        def sem(name):
            return ctx.enter_context(nc.semaphore(name))

        def sb(name, shape, dt=F32, where=ctx):
            return where.enter_context(nc.sbuf_tensor(name, shape, dt))

        d_x = nc.dram_tensor("scr_x", (KT, P, TT), F32).ap()
        d_q = nc.dram_tensor("scr_q", (KT, P, TT), F32).ap()
        d_z = nc.dram_tensor("scr_z", (KT, P, TT), F32).ap()
        d_g = nc.dram_tensor("scr_g", (2 * KT, P, TT), F32).ap()
        d_c = nc.dram_tensor("scr_c", (2 * KT, P, TT), F32).ap()

        pj = ctx.enter_context(nc.psum_tensor("pj", [P, 2, 3, 512], F32))
        px = ctx.enter_context(nc.psum_tensor("px", [P, 2, 512], F32))
        pjf = [pj[:, s].rearrange("p a b -> p (a b)") for s in range(2)]
        pxf = px[:].rearrange("p a b -> p (a b)")

        cst = sb("cst", [P, K_END])
        ident, ones, halves = cst[:, K_ID:K_ID + P], cst[:, K_ONE:K_ONE + P], cst[:, K_HALF:K_HALF + P]
        le, gt, diag = (cst[:, k:k + P] for k in (K_LE, K_GT, K_DIAG))
        cos, sin = cst[:, K_COS:K_COS + TT], cst[:, K_SIN:K_SIN + TT]
        sel = cst[0:8, K_SEL:K_SEL + P]
        expand = cst[0:16, K_EXP:K_EXP + 8 * P].rearrange("h (m p) -> h m p", m=8)

        par = sb("par", [P, 96])
        taps = sb("taps", [P, 64])
        modT = sb("modT", [P, 48, 9])
        aff = sb("aff", [P, KT, 9])
        eps = sb("eps", [P, 1])
        dskip = sb("dskip", [P, KT])
        dtb = sb("dtb", [P, 16])
        aneg = sb("aneg", [P, 16])
        misc = sb("misc", [P, NT + 1, 48])
        dtn = sb("dtn", [P, NT + 1, 16])
        dta = sb("dta", [P, NT + 1, 16])
        convS = sb("convS", [P, 16, NB])
        pgt = sb("pgt", [1, 64], I32)
        qs = sb("qs", [P, KT, NB])
        iqs = sb("iqs", [64, 8, NB])
        scT = sb("scT", [P, 16, 24])
        xraw = sb("xraw", [P, 16, 11])

        s_cst, s_par, s_vec, s_pt, s_crow = (sem(n) for n in ("s_cst", "s_par", "s_vec", "s_pt", "s_crow"))
        s_xin = [sem("s_xin0"), sem("s_xin1")]
        s_xt, s_xe = sem("s_xt"), sem("s_xe")
        s_csil = sem("s_csil")
        s_ptr, s_pte = sem("s_ptr"), sem("s_pte")
        s_raw = [sem("s_raw0"), sem("s_raw1")]
        s_ada, s_mod = sem("s_ada"), sem("s_mod")
        s_sq, s_ss, s_rt, s_rs, s_h, s_hh, s_hl = (sem(n) for n in ("s_sq", "s_ss", "s_rt", "s_rs", "s_h", "s_hh", "s_hl"))
        s_split, s_mm, s_ev = (sem(n) for n in ("s_split", "s_mm", "s_ev"))
        s_st = [sem("s_st0"), sem("s_st1")]
        s_xs = sem("s_xs")
        s_c = {e: sem("s_link_" + e) for e in ("act", "dve", "pool")}
        s_tr, s_te, s_nat = sem("s_tr"), sem("s_te"), sem("s_nat")
        s_natd = [sem("s_natd0"), sem("s_natd1")]
        s_is, s_ir, s_ia = sem("s_is"), sem("s_ir"), sem("s_ia")
        s_out = sem("s_out")
        n_out = [0]

        def store(eng, dst, src):
            eng.dma_start(dst, src).then_inc(s_out, 16)
            n_out[0] += 16

        raw = sb("raw", [P, 2, KT * 256])
        whi = sb("whi", [P, 2, KT, P], F32R)
        wlo = sb("wlo", [P, 2, KT, P], F32R)

        w_in2 = w_in[0].rearrange("(k p) n -> p k n", p=P)
        w_ada2 = w_ada[0].rearrange("(k p) n -> p k n", p=P)
        w_up2 = w_up[0].rearrange("(k p) n -> p k n", p=P)
        w_out2 = w_out[0].rearrange("(j u a d) n -> j u d a n", j=2, u=2, a=4)

        PAIRS = ([("iq", n, False) for n in range(2)] + [("k", 0, False), ("v", 0, False), ("misc", 0, False)]
                 + [("q", n, True) for n in range(4)] + [("z", n, True) for n in range(4)]
                 + [("g", n, True) for n in range(8)] + [("x", n, True) for n in range(4)]
                 + [("bc", n, False) for n in range(4)])
        B_OUT = 2 * len(PAIRS)
        B_MLP = B_OUT + KT
        COL = {"iq": C_IQ, "k": C_K, "v": C_K + 256, "q": C_Q, "z": C_Z, "g": C_G, "x": C_X, "bc": C_X + D}
        N_ADA = 24

        def load_pair(sp, n):
            name, at, head_order = PAIRS[n]
            slot = n % 2
            v = raw[:, slot].rearrange("p (k n) -> p k n", k=KT)
            if name == "misc":
                parts = [(v[:, :, 0:72], w_in2[:, :, C_IK:C_IK + 72]), (v[:, :, 72:88], w_in2[:, :, C_DT:C_DT + 16])]
            elif head_order:
                c = COL[name] + (at // 2) * 512 + (at % 2) * P
                parts = [(v[:, :, 0:P], w_in2[:, :, c:c + P]), (v[:, :, P:2 * P], w_in2[:, :, c + 256:c + 256 + P])]
            else:
                c = COL[name] + at * 256
                parts = [(v[:], w_in2[:, :, c:c + 256])]
            for dst, src in parts:
                sp.dma_start(dst, src).then_inc(s_raw[slot], 16)

        raw_at = [16 * (N_ADA // 2)] * 2
        PAIR_AT = []
        for n, (name, _, head_order) in enumerate(PAIRS):
            raw_at[n % 2] += 32 if head_order or name == "misc" else 16
            PAIR_AT.append(raw_at[n % 2])

        def weight_parts(name, b, v, head_order):
            if name == "misc":
                if b == 0:
                    return [(v[:, :, 0:64], 0, 64), (v[:, :, 0:64], 64, P)]
                return [(v[:, :, 64:72], 0, 8), (v[:, :, 72:88], 32, 48)]
            if head_order:
                return [(v[:, :, b * 64:b * 64 + 64], 0, 64), (v[:, :, P + b * 64:P + b * 64 + 64], 64, P)]
            return [(v[:, :, b * P:b * P + P], 0, P)]

        def split_block(pool, parts, kt, hs, link):
            for n, (a, c0, c1) in enumerate(parts):
                ins = pool.tensor_copy(whi[:, hs, 0:kt, c0:c1], a)
                if n < len(parts) - 1:
                    ins.then_inc(s_part, 1)
            link(ins)
            if len(parts) == 2:
                parts_done[0] += 1
                pool.wait_ge(s_part, parts_done[0])
            for n, (a, c0, c1) in enumerate(parts):
                ins = pool.tensor_tensor(wlo[:, hs, 0:kt, c0:c1], a, whi[:, hs, 0:kt, c0:c1].bitcast(F32), ALU.subtract)
                if n < len(parts) - 1:
                    ins.then_inc(s_part, 1)
                    parts_done[0] += 1
            if len(parts) == 2:
                pool.wait_ge(s_part, parts_done[0])
            ins.then_inc(s_split, 1)

        s_part = sem("s_part")
        parts_done = [0]

        def products(pe, hs, kt, ahi, alo, whi=whi, wlo=wlo):
            for n in range(3):
                c = slice(n * W3, n * W3 + W3)
                for k in range(kt):
                    for m, (w, a) in enumerate(((whi, ahi), (whi, alo), (wlo, ahi))):
                        ins = pe.matmul(pj[:, hs, n, 0:W3], w[:, hs, k], a[:, k, c],
                                        start=(k == 0 and m == 0), stop=(k == kt - 1 and m == 2))
            ins.then_inc(s_mm, 1)

        def first_products(pe, ahi, alo, ready):
            for k in range(KT):
                ready(k)
                for hs in range(2):
                    for n in range(3):
                        c = slice(n * W3, n * W3 + W3)
                        for m, (w, a) in enumerate(((whi, ahi), (whi, alo), (wlo, ahi))):
                            ins = pe.matmul(pj[:, hs, n, 0:W3], w[:, hs, k], a[:, k, c],
                                            start=(k == 0 and m == 0), stop=(k == KT - 1 and m == 2))
                    if k == KT - 1:
                        ins.then_inc(s_mm, 1)

        def pe_blocks(pe, b0, n):
            with pe.Fori(0, n // 2) as i:
                for s in range(2):
                    pe.wait_ge(s_split, i * 2 + (b0 + s + 1))
                    pe.wait_ge(s_ev, i * 2 + (b0 + s - 1))
                    products(pe, s, KT, act_hi, act_lo)

        prod = [pj[:, s, :, 0:W3] for s in range(2)]

        def three(ap):
            return ap.rearrange("p (a b) -> p a b", a=3)

        R = ExitStack()
        REGION = off(NT) + 2 * TT + 256 * (NT + 1)
        region = sb("region", [P, REGION], F32, R)
        xT = region[:, 0:KT * TT].rearrange("p (k t) -> p k t", k=KT)
        isc = region[:, 0:off(NT)]
        vT = region[:, 0:2 * TT].rearrange("p (k t) -> p k t", k=2)
        mT = region[:, 2 * TT:3 * TT]
        nst = region[:, 3 * TT:3 * TT + 2 * 624].rearrange("p (s n) -> p s n", s=2)
        r0 = off(NT)
        kT = region[:, r0:r0 + 2 * TT].rearrange("p (k t) -> p k t", k=2)
        vn = region[:, r0 + 2 * TT:].rearrange("p (k t) -> p k t", t=256)
        ikT = sb("ikT", [P, TT], F32, R)
        with ExitStack() as A:
            iqT = sb("iqT", [P, 4, TT], F32, A)
            act_hi = sb("act_hi", [P, KT, TT], F32R, A)
            act_lo = sb("act_lo", [P, KT, TT], F32R, A)
            E = sb("E", [P, 2, TT], F32, A)
            ROT = sb("ROT", [P, TT], F32, A)
            O = sb("O", [P, 2, TT + 3], F32, A)
            cT = sb("cT", [P, KT, 9], F32, A)
            rows = sb("rows", [96, P], F32, A)
            rowb = sb("rowb", [64, P], F32, A)
            m8 = sb("m8", [P, 8], F32, A)
            dtx = sb("dtx", [P, 4, (NT + 1) * 16], F32, A)
            scn = E[0:24].rearrange("p a b -> p (a b)")[:, 0:2 * D]
            crow = ROT[0:9, 0:D]
            mod_rows = O[0:9, 0, 0:512]
            xin = O[:, :, 0:D]
            crst = E[0:11].rearrange("p a b -> p (a b)")[:, 0:2 * D]

        with ExitStack() as Bs:
            gates = sb("gates", [P, 2, KT, NB], F32, Bs)
            M = sb("M", [P, KT, TT], F32, Bs)
            k_hh = [w[:].rearrange("p u k n -> p u (k n)") for w in (whi, wlo)]
            k_lo = sb("k_lo", [P, 2, T], F32R, Bs)
            with ExitStack() as B1:
                xb = sb("xb", [P, 2, 16, P], F32, B1)
                zc, gc = (raw[:, s].rearrange("p (s k t) -> p s k t", s=2, k=KT) for s in range(2))
                dtc = sb("dtc", [P, 2, 16], F32, B1)
                dac = sb("dac", [P, 2, 16], F32, B1)
                ex = sb("ex", [P, 48], F32, B1)
                xdt = sb("xdt", [P, 16, 64], F32, B1)
                xw = sb("xw", [P, 16, 64], F32, B1)
                Bn = sb("Bn", [P, 4, P], F32, B1)
                cbm = sb("cbm", [P, 4, P], F32, B1)
                SM = sb("SM", [P, 2, 4, P], F32, B1)
                Lx = sb("Lx", [P, 2, 4, P], F32, B1)
                ML = sb("ML", [P, 2, 4, P], F32, B1)
                ST = sb("ST", [P, D], F32, B1)[:]
                yn = sb("yn", [P, D], F32, B1)[:]
                gg = sb("gg", [P, 2, KT, P], F32, B1)[:]
                xD = sb("xD", [P, KT, P], F32, B1)[:]
                rt = sb("rt", [P, 2, P], F32, B1)
            with ExitStack() as B2:
                q_hl = sb("q_hl", [P, 2, 2, KT, P], F32R, B2)
                ga = sb("ga", [P, 2, KT, P], F32, B2)
                Sm = sb("Sm", [P, 2, D], F32, B2)
                Pr = sb("Pr", [P, 2, D], F32, B2)
                PT = sb("PT", [P, 2, D], F32, B2)
                an = sb("an", [P, D], F32, B2)
                mx = sb("mx", [P, P], F32, B2)
                nm = sb("nm", [P, P], F32, B2)
                sm = sb("sm", [P, P], F32, B2)
                ri = sb("ri", [P, P], F32, B2)
                qt = [sb("qt%d" % s, [P, 2, KT, P], F32, B2) for s in (1, 0)][::-1]
            with ExitStack() as B3:
                pg = sb("pg", [P, 2, 8, 256], F32, B3)
                kTb = sb("kTb", [P, 2, 2, L], F32, B3)
                sg = sb("sg", [P, 4, KT, NB], F32, B3)
                scol = sb("scol", [P, 8], F32, B3)
                qz = sb("qz", [P, NB * 2 * P + 272], F32, B3)
                iqz = sb("iqz", [64, NB * 64 + 72], F32, B3)
                bwt = sb("bwt", [8, 64], F32, B3)[:]
                m8b = sb("m8b", [P, 8], F32, B3)
                bwz = sb("bwz", [64, 8], F32, B3)
                sS, sP = sb("sS", [P, L], F32, B3)[:], sb("sP", [P, L], F32, B3)[:]
                sT = sb("sT", [P, 9, P], F32, B3)
                vrow = sb("vrow", [1, NB, 256], F32, B3)[:]
            with ExitStack() as B4:
                sb("keep_low", [P, KT * TT - 2 * T], F32, B4)
                S0 = sb("S0", [P, 2, KT, P], F32, B4)
                S1 = sb("S1", [P, 2, KT, P], F32, B4)
                S2 = sb("S2", [P, 2, KT, P], F32, B4)
                S3 = sb("S3", [P, KT, P], F32, B4)
                BX = sb("BX", [P, 8, 64], F32, B4)
                sq4 = sb("sq4", [P, 12, KT, NB], F32, B4)
                dT = sb("dT", [16, 2, NB], F32, B4)
        R.close()
        with ExitStack() as C:
            ahi = sb("ahi", [P, KT, TT], F32R, C)
            RC = sb("RC", [P, TT], F32, C)
            tmp8 = sb("tmp8", [P, 2, NB], F32, C)
            zero = sb("zero", [P, P], F32, C)[:]
            d_hi = sb("d_hi", [P, 2, 2, P], F32R, C)
            rt9 = sb("rt9", [P, 3, 16], F32, C)
            sb("room", [P, REGION + TT + 2 * KT * NB - (KT * TT + TT + 2 * NB + P + 4 * P + 3 * 16)], F32, C)
            sb("keep_M", [P, KT, TT], F32, C)
            alo = sb("alo", [P, KT, TT], F32R, C)
            u_hi = sb("u_hi", [P, 2, 2, TT], F32R, C)
            u_lo = sb("u_lo", [P, 2, 2, TT], F32R, C)
            OC = sb("OC", [P, 2, TT], F32, C)
            wrow = sb("wrow", [P, D], F32, C)
            d_lo = sb("d_lo", [P, 2, 2, P], F32R, C)
        x2T = M

        def norm_squares(act, src, sq, n):
            for k in range(KT):
                if 8 * n + k >= 2:
                    act.wait_ge(s_ss, 8 * n + k - 1)
                act.activation(sq[:, k % 2, 0:TT], src[:, k], ACT.Square).then_inc(s_sq, 1)

        def norm_sums(pe, sq, n):
            for k in range(KT):
                pe.wait_ge(s_sq, 8 * n + k + 1)
                for c in range(3):
                    ins = pe.matmul(pj[:, 1, c, 0:W3], ones, sq[:, k % 2, c * W3:(c + 1) * W3],
                                    start=(k == 0), stop=(k == KT - 1))
                ins.then_inc(s_ss, 1)

        def norm_root(act, dst, n):
            act.wait_ge(s_ss, 8 * n + 8)
            act.activation(three(dst), prod[1], ACT.Sqrt, bias=eps[:], scale=1.0 / D).then_inc(s_rt, 1)

        def norm_apply(dve, link, src, rst, dst, nw, sh, sc, n):
            link(dve.scalar_tensor_tensor(aff[:], modT[:, sc * 8:sc * 8 + 8], 1.0,
                                          nw.unsqueeze(2).broadcast_to([P, KT, 9]), ALU.add, ALU.mult))
            for k in range(KT):
                if 8 * n + k >= 2:
                    dve.wait_ge(s_hl, 8 * n + k - 1)
                d = dst[:, k % 2]
                link(dve.tensor_tensor(d[:, 0:TT], src[:, k], rst, ALU.mult))
                dve.tensor_scalar(d[:, 0:T], d[:, 0:T], aff[:, k, 8:9], modT[:, sh * 8 + k, 8:9],
                                  ALU.mult, ALU.add).then_inc(s_h, 1)
                link(dve.tensor_tensor(d[:, T:TT], d[:, T:TT], aff[:, k, 0:8], ALU.mult))
                dve.tensor_tensor(d[:, T:TT], d[:, T:TT], modT[:, sh * 8 + k, 0:8], ALU.add).then_inc(s_h, 1)

        def norm_hi(act, dst, hi, n):
            for k in range(KT):
                act.wait_ge(s_h, 2 * (8 * n + k) + 2)
                act.activation(hi[:, k], dst[:, k % 2, 0:TT], ACT.Copy).then_inc(s_hh, 1)

        def norm_lo(pool, dst, hi, lo, n):
            for k in range(KT):
                pool.wait_ge(s_hh, 8 * n + k + 1)
                pool.tensor_tensor(lo[:, k], dst[:, k % 2, 0:TT], hi[:, k].bitcast(F32), ALU.subtract).then_inc(s_hl, 1)

        ROPE = [0, 1, 2, 3, 4, 5, 8] + list(range(10, 18))
        IDX = [(t, h) for t in range(2, NT) for h in range(8)]

        def sp_phase_a(sp):
            sp.dma_start(cst[:], consts).then_inc(s_cst, 16)
            sp.dma_start(crow[0:8], c_sample).then_inc(s_crow, 16)
            sp.dma_start(crow[8:9], c_prompt).then_inc(s_crow, 16)
            sp.dma_start(rows[0:48], b_ada[0].rearrange("(r p) -> r p", p=P)).then_inc(s_par, 16)
            sp.dma_start(rows[48:56], norm1_w[0].rearrange("(r p) -> r p", p=P)).then_inc(s_par, 16)
            sp.dma_start(rows[56:64], norm2_w[0].rearrange("(r p) -> r p", p=P)).then_inc(s_par, 16)
            sp.dma_start(rows[64:72], final_norm_w.rearrange("(r p) -> r p", p=P)).then_inc(s_par, 16)
            sp.dma_start(rows[88:96], conv_b[0, D:2 * D].rearrange("(r p) -> r p", p=P)).then_inc(s_par, 16)
            for j in range(2):
                for at, v in ((72, ssm_norm_w[0]), (80, conv_b[0])):
                    sp.dma_start(rows[at + 4 * j:at + 4 * j + 4].rearrange("a (u d) -> a u d", u=2),
                                 v[j * 512:j * 512 + 512].rearrange("(u a d) -> a u d", u=2, a=4)).then_inc(s_par, 16)
                for tap in range(4):
                    sp.dma_start(rowb[16 * tap + 4 * j:16 * tap + 4 * j + 4].rearrange("a (u d) -> a u d", u=2),
                                 conv_w[0, tap, j * 512:j * 512 + 512].rearrange("(u a d) -> a u d", u=2, a=4)
                                 ).then_inc(s_par, 16)
            for tap in range(4):
                sp.dma_start(rowb[16 * tap + 8:16 * tap + 16],
                             conv_w[0, tap, D:2 * D].rearrange("(r p) -> r p", p=P)).then_inc(s_par, 16)
            hist = state_conv[0].rearrange("b t c -> (b t) c")
            sp.dma_start(scn[:, D:2 * D], hist[:, D:2 * D]).then_inc(s_par, 16)
            for j in range(2):
                for u in range(2):
                    sp.dma_start(scn[:, j * 512:j * 512 + 512].rearrange("r (a u d) -> r u a d", u=2, a=4)[:, u],
                                 hist[:, j * 512 + u * 256:j * 512 + u * 256 + 256].rearrange("r (a d) -> r a d", a=4)
                                 ).then_inc(s_par, 16)
            for u in range(2):
                for j in range(2):
                    sp.dma_start(dskip[64 * u:64 * u + 64, 4 * j:4 * j + 4],
                                 d_skip[0:1, 8 * j + 4 * u:8 * j + 4 * u + 4].broadcast_to([64, 4])).then_inc(s_vec, 16)
            sp.dma_start(dtb[:], dt_bias[0:1, :].broadcast_to([P, 16])).then_inc(s_vec, 16)
            sp.dma_start(aneg[:], a_log[0:1, :].broadcast_to([P, 16])).then_inc(s_vec, 16)
            sp.dma_start(pgt[:], page_table.rearrange("b n -> (b n)").unsqueeze(0)).then_inc(s_pt, 16)
            for t in range(NT + 1):
                if t >= 2:
                    sp.wait_ge(s_xt, t - 1)
                src = x_prompt[0, t * P:t * P + P] if t < NT else x_sample[:, 0]
                sp.dma_start(xin[0:src.shape[0], t % 2], src).then_inc(s_xin[t % 2], 16)
            for s in range(2):
                sp.dma_start(raw[:, s].rearrange("p (k n) -> p k n", k=KT),
                             w_ada2[:, :, s * 256:s * 256 + 256]).then_inc(s_raw[s], 16)
            with sp.Fori(1, N_ADA // 2) as i:
                for s in range(2):
                    sp.wait_ge(s_ada, i * 2 + (s - 1))
                    sp.dma_start(raw[:, s].rearrange("p (k n) -> p k n", k=KT),
                                 w_ada2[:, :, bass.ds(i * 512 + s * 256, 256)]).then_inc(s_raw[s], 16)
            for n in range(len(PAIRS)):
                if n < 2:
                    sp.wait_ge(s_ada, N_ADA - 1 + n)
                else:
                    sp.wait_ge(s_split, 2 * n - 2)
                load_pair(sp, n)

        def pool_phase_a(pool, link):
            pool.memset(eps[:], EPS).then_inc(s_eps, 1)
            pool.memset(misc[:], 0.0).then_inc(s_eps, 1)
            for n, (name, _, head_order) in enumerate(PAIRS):
                if n == 1:
                    norm_lo(pool, O, act_hi, act_lo, 0)
                    pool.wait_ge(s_hl, 8)
                    pool.memset(O[:, :, 0:3], 0.0).then_inc(s_eps, 1)
                v = raw[:, n % 2].rearrange("p (k n) -> p k n", k=KT)
                pool.wait_ge(s_raw[n % 2], PAIR_AT[n])
                for b in range(2):
                    if 2 * n + b >= 2:
                        pool.wait_ge(s_mm, 2 * n + b - 1)
                    split_block(pool, weight_parts(name, b, v, head_order), KT, b, link)

        def pe_phase_a(pe):
            pe.wait_ge(s_cst, 16)
            pe.wait_ge(s_csil, 1)
            for k in range(KT):
                ins = pe.transpose(px[:, 0, k * 9:k * 9 + 9], crow[:, k * P:k * P + P], ident[0:9, 0:9])
            pe.wait_ge(s_par, 16 * N_PAR)
            pe.transpose(px[:, 0, 72:168], rows[:], ident[0:96, 0:96])
            pe.transpose(px[:, 0, 168:232], rowb[:], ident[0:64, 0:64])
            for m in range(16):
                ins = pe.transpose(px[:, 1, m * 24:m * 24 + 24], scn[:, m * P:m * P + P], ident[0:24, 0:24])
            ins.then_inc(s_ptr, 1)
            for t in range(NT + 1):
                w = P if t < NT else NB
                pe.wait_ge(s_xin[t % 2], 16 * (t // 2 + 1))
                if t >= 2:
                    pe.wait_ge(s_xe, t - 1)
                for k in range(KT):
                    ins = pe.transpose(pjf[t % 2][:, k * P:k * P + w], xin[0:w, t % 2, k * P:k * P + P], ident[0:w, 0:w])
                ins.then_inc(s_xt, 1)
            pe.wait_ge(s_pte, 4)
            pe.wait_ge(s_xe, NT + 1)
            norm_sums(pe, E, 0)
            with pe.Fori(0, N_ADA // 2) as i:
                for s in range(2):
                    pe.wait_ge(s_raw[s], i * 16 + 16)
                    v = raw[:, s].rearrange("p (k n) -> p k n", k=KT)
                    for k in range(KT):
                        ins = pe.matmul(pj[0:9, 0, s, 0:256], cT[:, k], v[:, k], start=(k == 0), stop=(k == KT - 1))
                    ins.then_inc(s_ada, 1)
                for s in range(2):
                    pe.wait_ge(s_arow, i * 2 + (s + 1))
                    for b in range(2):
                        ins = pe.matmul(px[:, 0, bass.ds(i * 36 + (s * 18 + b * 9), 9)],
                                        mod_rows[:, s * 256 + b * P:s * 256 + b * P + P], ident[0:9, 0:9], start=True, stop=True)
                    ins.then_inc(s_ptr, 1)
            pe.wait_ge(s_rt, 1)
            pe.wait_ge(s_split, 2)
            first_products(pe, act_hi, act_lo, lambda k: pe.wait_ge(s_hl, k + 1))
            pe_blocks(pe, 2, 8)
            pe.wait_ge(s_ev, 10)
            pe.wait_ge(s_rope, 7)
            for t in range(NT + 1):
                w = P if t < NT else NB
                if t >= 2:
                    pe.wait_ge(s_te, 2 * t - 2)
                o = pjf[t % 2]
                for j in range(2):
                    pe.transpose(o[0:w, j * P:j * P + P], kT[:, j, t * P:t * P + w], ident)
                    pe.transpose(o[0:w, 256 + j * P:256 + j * P + P], vT[:, j, t * P:t * P + w], ident)
                pe.transpose(o[0:w, 512:576], ikT[0:64, t * P:t * P + w], ident[0:64, 0:64])
                pe.transpose(o[0:w, 576:624], mT[0:48, t * P:t * P + w], ident[0:48, 0:48]).then_inc(s_tr, 1)
            pe.wait_ge(s_te, 2 * (NT + 1))
            for n, (t, h) in enumerate(IDX):
                if n >= 2:
                    pe.wait_ge(s_ir, n - 1)
                u, w = 64 * (h % 2), P * (t + 1)
                for c in range(0, w, 512):
                    e = min(w, c + 512)
                    ins = pe.matmul(pjf[n % 2][:, c:e], iqT[u:u + 64, h // 2, t * P:t * P + P], ikT[u:u + 64, c:e],
                                    start=True, stop=True)
                ins.then_inc(s_is, 1)
            pe.wait_ge(s_ir, len(IDX))
            pe_blocks(pe, 10, B_OUT - 10)
            pe.wait_ge(s_ev, B_OUT)
            pe.wait_ge(s_conv, 16)
            for m in range(16):
                if m % 8 == 0:
                    o = pjf[m // 8]
                ins = pe.transpose(o[0:11, (m % 8) * P:(m % 8) * P + P], xraw[:, m], ident)
            ins.then_inc(s_xrt, 1)

        st_at = [0, 0]
        uses = {}

        def act_phase_a(act, link):
            act.wait_ge(s_crow, 32)
            act.activation(crow, crow, ACT.Silu).then_inc(s_csil, 1)
            for t in range(NT + 1):
                w = P if t < NT else NB
                act.wait_ge(s_xt, t + 1)
                act.activation(xT[:, :, t * P:t * P + w], pjf[t % 2][:, 0:D].rearrange("p (k t) -> p k t", k=KT)[:, :, 0:w],
                               ACT.Copy).then_inc(s_xe, 1)
            act.wait_ge(s_xe, NT + 1)
            act.dma_start(d_x.rearrange("k p t -> p k t"), xT).then_inc(s_xs, 16)
            act.wait_ge(s_eps, 1)
            act.wait_ge(s_pte, 4)
            norm_squares(act, xT, E, 0)
            norm_root(act, ROT[:], 0)
            with act.Fori(0, N_ADA // 2) as i:
                for s in range(2):
                    act.wait_ge(s_ada, i * 2 + (s + 1))
                    act.activation(mod_rows[:, s * 256:s * 256 + 256], pj[0:9, 0, s, 0:256], ACT.Copy).then_inc(s_arow, 1)
            norm_hi(act, O, act_hi, 0)
            pending = []

            def put(slot, dst, src):
                act.dma_start(dst, src).then_inc(s_st[slot], 16)
                st_at[slot] += 1

            def slot_stored(slot):
                if st_at[slot]:
                    act.wait_ge(s_st[slot], 16 * st_at[slot])

            def rope_in(b, r):
                s = b % 2
                act.wait_ge(s_mm, b + 1)
                if r >= 2:
                    act.wait_ge(s_rope, r - 1)
                act.activation(three(E[:, s]), prod[s], ACT.Copy).then_inc(s_ev, 1)

            r = 0
            act.wait_ge(s_ss, 8)
            for b in range(10):
                if b in ROPE:
                    rope_in(b, r)
                    r += 1
                else:
                    act.wait_ge(s_mm, b + 1)
                    if b < 8:
                        act.wait_ge(s_xs, 16)
                        act.activation(three(vT[:, b - 6]), prod[b % 2], ACT.Copy).then_inc(s_ev, 1)
                    else:
                        act.activation(three(mT[:]), prod[b % 2], ACT.Copy).then_inc(s_ev, 1)
            for t in range(NT + 1):
                w, s = (P if t < NT else NB), t % 2
                act.wait_ge(s_tr, t + 1)
                if t >= 2:
                    act.wait_ge(s_natd[s], 48 * (t // 2))
                    act.wait_ge(s_nat, 2 * t - 2)
                act.activation(nst[0:w, s, 0:512], pjf[s][0:w, 0:512], ACT.Copy).then_inc(s_te, 1)
                act.activation(nst[0:w, s, 512:624], pjf[s][0:w, 512:624], ACT.Copy).then_inc(s_te, 1)
                act.wait_ge(s_te, 2 * t + 2)
                if t < NT:
                    outs = (k_prompt[0, 0, t * P:t * P + P].rearrange("t h d -> t (h d)"),
                            v_prompt[0, 0, t * P:t * P + P].rearrange("t h d -> t (h d)"),
                            idxk_prompt[0, 0, t * P:t * P + P])
                else:
                    outs = (k_sample[0, :, 0].rearrange("t h d -> t (h d)"), v_sample[0, :, 0].rearrange("t h d -> t (h d)"),
                            idxk_sample[0, :, 0])
                for dst, src in zip(outs, (nst[0:w, s, 0:256], nst[0:w, s, 256:512], nst[0:w, s, 512:576])):
                    act.dma_start(dst, src).then_inc(s_natd[s], 16)
            act.wait_ge(s_vec, 96)
            link(act.activation(aneg[:], aneg[:], ACT.Exp))
            act.wait_ge(s_dtx, 1)
            act.activation(dtx[:, 2], dtx[:, 1], ACT.Exp, scale=-1.0).then_inc(s_dte, 1)
            act.wait_ge(s_rope, 7)
            for n, (t, h) in enumerate(IDX):
                w = P * (t + 1)
                act.wait_ge(s_is, n + 1)
                if n >= 2:
                    act.wait_ge(s_ia, n - 1)
                act.activation(E[:, n % 2, 0:w], pjf[n % 2][:, 0:w], ACT.Relu, scale=IDX_SCALE).then_inc(s_ir, 1)
            act.wait_ge(s_ia, len(IDX))
            for b in range(10, 18):
                rope_in(b, r)
                r += 1
                if b > 10:
                    act.wait_ge(s_rope, r - 1)
                    put((b - 1) % 2, d_q[b - 11], O[:, (b - 1) % 2, 3:3 + TT])
            act.wait_ge(s_rope, r)
            put(1, d_q[7], O[:, 1, 3:3 + TT])
            act.wait_ge(s_qs, 8)
            for b in range(18, 42):
                s = b % 2
                act.wait_ge(s_mm, b + 1)
                slot_stored(s)
                act.activation(three(O[:, s, 3:3 + TT]), prod[s], ACT.Silu if b < 26 else ACT.Sigmoid).then_inc(s_ev, 1)
                if b > 18:
                    act.wait_ge(s_ev, b)
                    put(1 - s, *prev)
                prev = ((d_z[b - 18] if b < 26 else d_g[b - 26]), O[:, s, 3:3 + TT])
            act.wait_ge(s_ev, 42)
            put(1, *prev)
            gates_at = tuple(st_at)
            act.wait_ge(s_eps, 3)
            def conv_out(m):
                s = m % 2
                act.wait_ge(s_conv, m + 1)
                link(act.activation(E[:, s], E[:, s], ACT.Silu))
                link(act.activation(convS[:, m], E[:, s, T:TT], ACT.Copy))
                put(s, d_c[m], E[:, s])
            for m in range(16):
                b, s = 42 + m, m % 2
                act.wait_ge(s_mm, b + 1)
                slot_stored(s)
                if m >= 2:
                    act.wait_ge(s_conv, m - 1)
                link(act.activation(three(O[:, s, 3:3 + TT]), prod[s], ACT.Copy))
                act.activation(three(E[:, s]), prod[s], ACT.Identity, bias=par[:, 80 + m:81 + m],
                               scale=taps[:, 48 + m:49 + m]).then_inc(s_ev, 1)
                if m:
                    conv_out(m - 1)
            conv_out(15)
            for s in range(2):
                slot_stored(s)
            act.wait_ge(s_xrt, 1)
            for j in range(2):
                link(act.activation(crst[:, j * 512:j * 512 + 512].rearrange("r (u a d) -> r a u d", u=2, a=4),
                                    pjf[0][0:11, j * 512:j * 512 + 512].rearrange("r (a u d) -> r a u d", u=2, a=4), ACT.Copy))
            link(act.activation(crst[:, D:2 * D], pjf[1][0:11, 0:D], ACT.Copy))
            store(act, conv_prompt[0, 0], crst[0:3])
            store(act, conv_sample[0, :, 2], crst[3:11])
            store(act, conv_sample[0, :, 0:2], state_conv[0, :, 1:3])
            act.wait_ge(s_out, 48)
            return gates_at

        def dve_phase_a(dve, link):
            dve.wait_ge(s_ptr, 1)
            dve.tensor_copy(cT[:], px[:, 0, 0:72].rearrange("p (k c) -> p k c", k=KT)).then_inc(s_pte, 1)
            dve.tensor_copy(par[:], px[:, 0, 72:168]).then_inc(s_pte, 1)
            dve.tensor_copy(taps[:], px[:, 0, 168:232]).then_inc(s_pte, 1)
            dve.tensor_copy(scT[:], px[:, 1, 0:384].rearrange("p (m c) -> p m c", m=16)).then_inc(s_pte, 1)
            dve.wait_ge(s_pte, 4)
            dve.wait_ge(s_rt, 1)
            link(dve.reciprocal(ROT[:], ROT[:]))
            dve.wait_ge(s_ptr, 1 + N_ADA)
            link(dve.tensor_tensor(modT[:], px[:, 0, 0:432].rearrange("p (m c) -> p m c", m=48),
                                   par[:, 0:48].unsqueeze(2).broadcast_to([P, 48, 9]), ALU.add))
            dve.wait_ge(s_xt, NT + 1)
            norm_apply(dve, link, xT, ROT[:], O, par[:, 48:56], 0, 1, 0)
            dve.wait_ge(s_hl, 8)
            dve.wait_ge(s_xs, 16)

            def rope(b, dst):
                s = b % 2
                dve.wait_ge(s_ev, b + 1)
                link(dve.stream_shuffle(ROT[:], E[:, s], TURN))
                link(dve.tensor_tensor(ROT[:], ROT[:], sin, ALU.mult))
                link(dve.tensor_tensor(dst, E[:, s], cos, ALU.mult))
                dve.tensor_tensor(dst, dst, ROT[:], ALU.add).then_inc(s_rope, 1)
                ropes[0] += 1
                dve.wait_ge(s_rope, ropes[0])

            ropes = [0]
            for b in range(4):
                rope(b, iqT[:, b])
            for b in range(4, 6):
                rope(b, kT[:, b - 4])
            rope(8, ikT[:])
            for h in range(8):
                link(dve.tensor_copy(iqs[:, h], iqT[64 * (h % 2):64 * (h % 2) + 64, h // 2, T:TT]))
            for t in range(NT + 1):
                w = P if t < NT else NB
                dve.wait_ge(s_te, 2 * t + 2)
                dve.tensor_copy(vn[0:w, t], nst[0:w, t % 2, 256:512]).then_inc(s_nat, 1)
                if t == 0:
                    dve.wait_ge(s_eps, 2)
                dve.tensor_copy(misc[0:w, t], nst[0:w, t % 2, 576:624]).then_inc(s_nat, 1)
            dve.wait_ge(s_nat, 2 * (NT + 1))
            dve.wait_ge(s_vec, 96)
            xv = dtx[:, 0].rearrange("p (t h) -> p t h", h=16)
            link(dve.tensor_tensor(xv, misc[:, :, 32:48], dtb[:].unsqueeze(1).broadcast_to([P, NT + 1, 16]), ALU.add))
            link(dve.tensor_scalar(dtx[:, 1], dtx[:, 0], -1.0, None, ALU.mult))
            link(dve.tensor_tensor(dtx[:, 1], dtx[:, 0], dtx[:, 1], ALU.max))
            dve.sem_inc(s_dtx, 1)
            link(dve.tensor_scalar(misc[:, :, 0:8], misc[:, :, 0:8], 8.0 ** -0.5, None, ALU.mult))
            dve.wait_ge(s_dte, 1)
            link(dve.tensor_scalar(dtx[:, 1], dtx[:, 2], 2.0, None, ALU.add))
            link(dve.reciprocal(dtx[:, 1], dtx[:, 1]))
            link(dve.tensor_tensor(dtx[:, 1], dtx[:, 1], dtx[:, 2], ALU.mult))
            link(dve.tensor_tensor(dtx[:, 2], dtx[:, 1], dtx[:, 1], ALU.mult))
            link(dve.tensor_scalar(dtx[:, 3], dtx[:, 2], 1.0 / 17, 1.0 / 15, ALU.mult, ALU.add))
            for c in (13, 11, 9, 7, 5, 3, 1):
                link(dve.tensor_tensor(dtx[:, 3], dtx[:, 3], dtx[:, 2], ALU.mult))
                link(dve.tensor_scalar(dtx[:, 3], dtx[:, 3], 1.0 / c, None, ALU.add))
            link(dve.tensor_tensor(dtx[:, 3], dtx[:, 3], dtx[:, 1], ALU.mult))
            link(dve.tensor_scalar(dtx[:, 3], dtx[:, 3], 2.0, None, ALU.mult))
            link(dve.tensor_scalar(dtx[:, 0], dtx[:, 0], 0.0, None, ALU.max))
            link(dve.tensor_tensor(dtn[:].rearrange("p t h -> p (t h)"), dtx[:, 0], dtx[:, 3], ALU.add))
            link(dve.tensor_scalar(dta[:], dtn[:], -1.0, None, ALU.mult))
            link(dve.tensor_tensor(dta[:], dta[:], aneg[:].unsqueeze(1).broadcast_to([P, NT + 1, 16]), ALU.mult))
            dve.wait_ge(s_tr, NT + 1)
            dve.wait_ge(s_natd[0], 48 * 5)
            dve.wait_ge(s_natd[1], 48 * 4)
            dve.wait_ge(s_te, 2 * (NT + 1))
            link(dve.memset(isc[:, 0:off(2)], 0.0))
            for t in range(2):
                d = isc[:, off(t) + t * P:off(t + 1)]
                link(dve.tensor_scalar(d, diag, -AWAY, None, ALU.mult))
            for n, (t, h) in enumerate(IDX):
                w = P * (t + 1)
                d = isc[:, off(t):off(t + 1)]
                dve.wait_ge(s_ir, n + 1)
                if h == 0:
                    dve.tensor_scalar(d, E[:, n % 2, 0:w], misc[:, t, h:h + 1], None, ALU.mult).then_inc(s_ia, 1)
                else:
                    dve.scalar_tensor_tensor(d, E[:, n % 2, 0:w], misc[:, t, h:h + 1], d, ALU.mult, ALU.add).then_inc(s_ia, 1)
                dve.wait_ge(s_ia, n + 1)
                if h == 7:
                    g = isc[:, off(t) + t * P:off(t + 1)]
                    link(dve.scalar_tensor_tensor(g, diag, -BARRED, g, ALU.mult, ALU.add))
            for b in range(10, 18):
                if b >= 12:
                    dve.wait_ge(s_st[b % 2], 16 * ((b - 10) // 2))
                    dve.wait_ge(s_qs, b - 11)
                if b == 10:
                    dve.wait_ge(s_eps, 3)
                rope(b, O[:, b % 2, 3:3 + TT])
                dve.tensor_copy(qs[:, b - 10], O[:, b % 2, 3 + T:3 + TT]).then_inc(s_qs, 1)
            for t in range(2, NT - 1):
                pick(dve, link, isc[:, off(t):off(t + 1)], m8[:], 0, ROUNDS)
            last = isc[:, off(NT - 1):off(NT)]
            for m in range(16):
                b, s = 42 + m, m % 2
                dve.wait_ge(s_ev, b + 1)
                for tap in range(3):
                    w = taps[:, 16 * tap + m:16 * tap + m + 1]
                    dve.scalar_tensor_tensor(E[:, s, T:TT], scT[:, m, tap:24:3], w, E[:, s, T:TT],
                                             ALU.mult, ALU.add).then_inc(s_cs, 1)
                    link(dve.scalar_tensor_tensor(E[:, s, 0:T], O[:, s, tap:tap + T], w, E[:, s, 0:T], ALU.mult, ALU.add))
                    dve.wait_ge(s_cs, 3 * m + tap + 1)
                dve.tensor_copy(xraw[:, m], O[:, s, T:T + 11]).then_inc(s_conv, 1)
                pick(dve, link, last, m8[:], 2 * m, 2 * m + 2)

        ROUNDS = TOPK // 8

        def pick(dve, link, row, m8, r0, r1):
            for _ in range(r0, r1):
                link(dve.max(m8, row))
                link(dve.match_replace(row, m8, row, PICKED))
            if r1 < ROUNDS:
                return
            link(dve.tensor_scalar(row, row, 2 * BARRED, AWAY, ALU.is_gt, ALU.mult))

        s_eps, s_arow, s_rope, s_dtx, s_dte, s_conv, s_cs, s_xrt, s_qs = (
            sem(n) for n in ("s_eps", "s_arow", "s_rope", "s_dtx", "s_dte", "s_conv", "s_cs", "s_xrt", "s_qs"))
        N_PAR = 9 + 12 + 5
        TURN = [p + 8 if p < 8 else p - 8 if p < 16 else p for p in range(32)]

        NC = NT // 2
        SD = {n: sem("ssd_" + n) for n in (
            "dtc", "cum", "ex", "xt", "xdt", "bn", "xw", "cb", "cbm", "mask", "seg", "decay", "ml", "y", "yo", "dst",
            "yn", "st", "yt", "xd", "g", "sq", "ss", "rt", "gcw", "done", "stt", "ste")}
        s_cin = [sem("s_cin0"), sem("s_cin1")]

        def by_head(ap, j):
            return ap[:, j * 512:j * 512 + 512].rearrange("p (u a d) -> p u a d", u=2, a=4)

        def in_blocks(ap, j):
            return ap[:, j * 512:j * 512 + 512].rearrange("p (a u d) -> p u a d", u=2, a=4)

        def sp_ssd(sp):
            c3, z3, g3 = (d.rearrange("m p t -> p m t") for d in (d_c, d_z, d_g))

            def load(s, c0):
                sp.dma_start(xb[:, s], c3[:, :, bass.ds(c0, P)]).then_inc(s_cin[s], 16)
                sp.dma_start(zc[:, s], z3[:, :, bass.ds(c0, P)]).then_inc(s_cin[s], 16)
                sp.dma_start(gc[:, s], g3[:, KT:2 * KT, bass.ds(c0, P)]).then_inc(s_cin[s], 16)

            for s in range(2):
                sp.wait_ge(s_st[s], 16 * ST_ALL)
            sp.wait_ge(s_split, B_OUT)
            sp.wait_ge(s_xrt, 1)
            sp.wait_ge(s_out, 48)
            sp.wait_ge(s_qs, 8)
            for s in range(2):
                load(s, s * P)
            with sp.Fori(1, NC) as i:
                for s in range(2):
                    sp.wait_ge(SD["gn"], i * 2 + (s - 1))
                    load(s, i * 256 + s * P)

        def chunks(eng, chunk, link=None, per=0):
            def turn(i, first):
                for s in range(2):
                    chunk(lambda n, k: i * (2 * n) + (s * n + k), s, i, first, s > 0 or not first)

            turn(0, True)
            with eng.Fori(1, NC) as i:
                if link:
                    link.enter(i - 1, per)
                turn(i, False)
            if link:
                link.leave(NC - 1)

        def pe_ssd(pe):
            def squares(at, j):
                if j == 0:
                    pe.wait_ge(SD["sq"], at(1, 0))
                for a in range(4):
                    ins = pe.matmul(px[:, 0, j * P:j * P + P], halves, xD[:, 4 * j + a], start=(a == 0), stop=(a == 3))
                if j == 1:
                    ins.then_inc(SD["ss"], 1)

            def chunk(at, s, i, first, later):
                pe.wait_ge(s_cin[s], i * 48 + 48)
                if later:
                    pe.wait_ge(SD["yr"], at(1, 0))
                for m in range(KT):
                    pe.transpose(pjf[0][:, m * P:m * P + P], xb[:, s, m], ident)
                for g in range(4):
                    ins = pe.transpose(pj[:, 0, 2, g * P:g * P + P], xb[:, s, 8 + g], ident)
                ins.then_inc(SD["xt"], 1)
                for g in range(4):
                    ins = pe.matmul(pj[:, 1, 2, g * P:g * P + P], xb[:, s, 8 + g], xb[:, s, 12 + g], start=True, stop=True)
                ins.then_inc(SD["cb"], 1)
                pe.wait_ge(SD["dtc"], at(1, 1))
                if later:
                    pe.wait_ge(SD["st"], at(1, 0))
                for n, m in enumerate((le, gt, ones)):
                    ins = pe.matmul(px[:, 1, 16 * n:16 * n + 16], m, dac[:, s], start=True, stop=True)
                ins.then_inc(SD["cum"], 1)
                for g in range(5):
                    if g < 4:
                        pe.wait_ge(SD["mask"], at(4, g + 1))
                        if g == 0:
                            pe.wait_ge(SD["bn"], at(1, 1))
                        elif g == 1:
                            pe.wait_ge(SD["cbm"], at(1, 1))
                        else:
                            pe.wait_ge(SD["decay"], at(4, g - 1))
                        for h in range(4):
                            ins = pe.matmul(pj[:, g % 2, 2, h * P:h * P + P], SM[:, g % 2, h], le, start=True, stop=True)
                        ins.then_inc(SD["seg"], 1)
                    if later and g in (1, 2):
                        squares(at, g - 1)
                    if g > 0:
                        if g == 1:
                            pe.wait_ge(SD["xdt"], at(2, 2))
                        pe.wait_ge(SD["ml"], at(4, g))
                        for h in range(4):
                            hh = 4 * (g - 1) + h
                            ins = pe.matmul(pjf[1][:, hh * 64:hh * 64 + 64], ML[:, (g - 1) % 2, h], xdt[:, hh],
                                            start=True, stop=True)
                        ins.then_inc(SD["y"], 1)
                for g in range(4):
                    ins = pe.matmul(pjf[0][:, g * 256:g * 256 + 256], xb[:, s, 12 + g], ST[:, g * 256:g * 256 + 256],
                                    start=True, stop=True)
                ins.then_inc(SD["yo"], 1)
                pe.wait_ge(SD["xw"], at(1, 1))
                pe.wait_ge(SD["ex"], at(1, 1))
                if later:
                    pe.wait_ge(SD["rt"], at(1, 0))
                for g in range(4):
                    ins = pe.matmul(pxf[:, g * 256:g * 256 + 256], Bn[:, g], xw[:, 4 * g:4 * g + 4].rearrange("p h d -> p (h d)"),
                                    start=True, stop=True)
                ins.then_inc(SD["dst"], 1)
                pe.wait_ge(SD["yn"], at(1, 1))
                for m in range(KT):
                    ins = pe.transpose(pjf[0][:, m * P:m * P + P], yn[:, m * P:m * P + P], ident)
                ins.then_inc(SD["yt"], 1)

            pe.wait_ge(s_out, 48)
            chunks(pe, chunk)
            pe.wait_ge(SD["st"], NT)
            for j in range(2):
                squares(lambda n, k: NT * n + k, j)
            pe.wait_ge(SD["yr"], NT)
            for m in range(KT):
                ins = pe.transpose(pjf[0][:, m * P:m * P + P], ST[:, m * P:m * P + P], ident)
            ins.then_inc(SD["stt"], 1)

        def act_ssd(act, link):
            act_keys(act)

            def root(at, first=False):
                act.wait_ge(SD["ss"], at(1, 0))
                if not first:
                    act.wait_ge(SD["done"], at(1, -1))
                act.activation(rt[:], px[:, 0, 0:256].rearrange("p (j t) -> p j t", j=2), ACT.Sqrt, bias=eps[:],
                               scale=1.0 / 256).then_inc(SD["rt"], 1)

            def chunk(at, s, i, first, later):
                act.wait_ge(SD["xt"], at(1, 1))
                act.activation(Bn[:], pj[:, 0, 2].rearrange("p (g n) -> p g n", g=4), ACT.Copy).then_inc(SD["bn"], 1)
                act.wait_ge(SD["cum"], at(1, 1))
                act.activation(ex[:], px[:, 1, 0:48], ACT.Exp).then_inc(SD["ex"], 1)
                for g in range(4):
                    act.wait_ge(SD["seg"], at(4, g + 1))
                    if g >= 2:
                        act.wait_ge(SD["ml"], at(4, g - 1))
                    act.activation(Lx[:, g % 2], pj[:, g % 2, 2].rearrange("p (h n) -> p h n", h=4), ACT.Exp
                                   ).then_inc(SD["decay"], 1)
                if later:
                    root(at, first)
                act.wait_ge(SD["g"], at(1, 1))
                act.activation(xD[:], gg[:, s], ACT.Square).then_inc(SD["sq"], 1)

            chunks(act, chunk)
            root(lambda n, k: NT * n + k)
            act.wait_ge(SD["stt"], 1)
            act.activation(yn[:], pjf[0][:, 0:D], ACT.Copy).then_inc(SD["ste"], 1)
            act.wait_ge(SD["ste"], 1)
            store(act, ssm_prompt[0, 0].rearrange("(m h) p n -> (h p) m n", m=KT), yn[:].rearrange("p (m n) -> p m n", m=KT))
            act.wait_ge(s_out, 64)

        def pool_ssd(pool, link):
            pool_keys(pool, link)

            def chunk(at, s, i, first, later):
                pool.wait_ge(SD["dtc"], at(1, 1))
                for g in range(4):
                    if g >= 2 or later:
                        pool.wait_ge(SD["seg"], at(4, g - 1))
                    pool.tensor_tensor(SM[:, g % 2], gt.unsqueeze(1).broadcast_to([P, 4, P]),
                                       dac[:, s, 4 * g:4 * g + 4].unsqueeze(2).broadcast_to([P, 4, P]), ALU.mult
                                       ).then_inc(SD["mask"], 1)
                pool.wait_ge(SD["xdt"], at(2, 2))
                pool.wait_ge(SD["ex"], at(1, 1))
                pool.tensor_tensor(xw[:], xdt[:], ex[:, 16:32].unsqueeze(2).broadcast_to([P, 16, 64]), ALU.mult
                                   ).then_inc(SD["xw"], 1)
                pool.wait_ge(s_cin[s], i * 48 + 48)
                if later:
                    pool.wait_ge(SD["ss"], at(1, 0))
                pool.tensor_tensor(xD[:], xb[:, s, 0:KT], dskip[:].unsqueeze(2).broadcast_to([P, KT, P]), ALU.mult
                                   ).then_inc(SD["xd"], 1)
                pool.tensor_tensor(gc[:, s], gc[:, s], par[:, 72:80].unsqueeze(2).broadcast_to([P, KT, P]), ALU.mult
                                   ).then_inc(SD["gcw"], 1)

            chunks(pool, chunk)

        def dve_ssd(dve, link):
            def steps(slot, c):
                link(dve.tensor_scalar(dtc[:, slot], dtn[:, c].rearrange("p a h -> p (a h)"), 1.0, None, ALU.mult))
                dve.tensor_scalar(dac[:, slot], dta[:, c].rearrange("p a h -> p (a h)"), 1.0, None, ALU.mult
                                  ).then_inc(SD["dtc"], 1)

            def inverse(at):
                dve.wait_ge(SD["rt"], at(1, -1))
                link(dve.reciprocal(rt[:], rt[:]))

            def norm(at, s, cols):
                dve.wait_ge(SD["gn"], at(1, -1))
                for j in range(2):
                    ins = dve.tensor_tensor(M[:, 4 * j:4 * j + 4, cols], gg[:, s, 4 * j:4 * j + 4],
                                            rt[:, j:j + 1].broadcast_to([P, 4, P]), ALU.mult)
                    if j == 0:
                        link(ins)
                ins.then_inc(SD["done"], 1)

            def gate(at, s):
                dve.wait_ge(SD["sq"], at(1, 0))
                dve.wait_ge(SD["gcw"], at(1, 0))
                dve.tensor_tensor(gg[:, s], gg[:, s], gc[:, s], ALU.mult).then_inc(SD["gn"], 1)

            def chunk(at, s, i, first, later):
                dve.wait_ge(SD["xt"], at(1, 1))
                for j in range(2):
                    dve.tensor_tensor(xdt[:, 8 * j:8 * j + 8].rearrange("p (u a) d -> p u a d", u=2),
                                      in_blocks(pjf[0], j),
                                      dtc[:, s, 8 * j:8 * j + 8].rearrange("p (u a) -> p u a", u=2).unsqueeze(3).broadcast_to([P, 2, 4, 64]),
                                      ALU.mult).then_inc(SD["xdt"], 1)
                dve.wait_ge(SD["cb"], at(1, 1))
                dve.tensor_tensor(cbm[:], pj[:, 1, 2].rearrange("p (g n) -> p g n", g=4),
                                  le.unsqueeze(1).broadcast_to([P, 4, P]), ALU.mult).then_inc(SD["cbm"], 1)
                for g in range(4):
                    dve.wait_ge(SD["decay"], at(4, g + 1))
                    if g == 0:
                        dve.wait_ge(SD["cbm"], at(1, 1))
                    if g >= 2:
                        dve.wait_ge(SD["y"], at(4, g - 1))
                    dve.tensor_tensor(ML[:, g % 2], Lx[:, g % 2], cbm[:, g:g + 1].broadcast_to([P, 4, P]), ALU.mult
                                      ).then_inc(SD["ml"], 1)
                    if g == 0 and not first:
                        inverse(at)
                    if g == 1 and not first:
                        norm(at, s, bass.ds(i * 256 + (s - 2) * P, P))
                    if g == 2 and later:
                        gate(at, 1 - s)
                steps(1 - s, bass.ds(i * 2 + (s + 1), 1))
                dve.wait_ge(SD["yo"], at(1, 1))
                dve.wait_ge(SD["y"], at(4, 4))
                for j in range(2):
                    ins = dve.tensor_tensor(in_blocks(yn, j), by_head(pjf[0], j),
                                            ex[:, 8 * j:8 * j + 8].rearrange("p (u a) -> p u a", u=2).unsqueeze(3).broadcast_to([P, 2, 4, 64]),
                                            ALU.mult)
                    link(ins)
                link(dve.tensor_tensor(in_blocks(yn, 0), in_blocks(yn, 0), by_head(pjf[1], 0), ALU.add))
                dve.tensor_tensor(in_blocks(yn, 1), in_blocks(yn, 1), by_head(pjf[1], 1), ALU.add).then_inc(SD["yn"], 1)
                st3 = ST.rearrange("p (h d) -> p h d", d=64)
                link(dve.tensor_tensor(st3, st3, ex[:, 32:48].unsqueeze(2).broadcast_to([P, 16, 64]), ALU.mult))
                dve.wait_ge(SD["yt"], at(1, 1))
                dve.wait_ge(SD["xd"], at(1, 1))
                dve.tensor_tensor(gg[:, s], pjf[0][:, 0:D].rearrange("p (k t) -> p k t", k=KT), xD, ALU.add).then_inc(SD["yr"], 1)
                dve.wait_ge(SD["dst"], at(1, 1))
                dve.tensor_tensor(ST, ST, pxf, ALU.add).then_inc(SD["st"], 1)
                dve.wait_ge(SD["yr"], at(1, 1))
                dve.tensor_tensor(gg[:, s], gg[:, s], zc[:, s], ALU.mult).then_inc(SD["g"], 1)

            for s in range(2):
                dve.wait_ge(s_st[s], 16 * ST_ALL)
            dve.wait_ge(s_out, 48)
            link(dve.memset(ST[:], 0.0))
            steps(0, slice(0, 1))
            chunks(dve, chunk, link, 14)
            for c in (NT - 2, NT - 1):
                inverse(lambda n, k: (c + 2) * n + k)
                if c == NT - 2:
                    gate(lambda n, k: NT * n + k, 1)
                norm(lambda n, k: (c + 2) * n + k, c % 2, slice(c * P, c * P + P))

        SD["gn"], SD["yr"] = sem("ssd_gn"), sem("ssd_yr")
        ST_ALL = 4 + 12 + 8

        HEADS = [(t, 4 * j + a, j, u, 8 * j + 4 * u + a) for t in range(NT) for j in range(2) for a in range(4) for u in range(2)]
        s_q = [sem("s_q0"), sem("s_q1")]
        s_ga = s_natd
        AT = {n: sem("att_" + n) for n in ("kh", "kl", "q", "s", "m", "nm", "p", "t", "c0", "c1", "o", "n", "nt", "nr", "mul")}
        N_HEADS = len(HEADS)
        GA_BASE = (48 * 5, 48 * 4)

        def sp_att(sp):
            q3, g3 = d_q.rearrange("m p t -> p m t"), d_g.rearrange("m p t -> p m t")
            for t in range(NT):
                if t == 1:
                    sp.wait_ge(SD["done"], NT)
                    sp.wait_ge(s_out, 64)
                if t >= 2:
                    sp.wait_ge(AT["q"], t - 1)
                for u in range(2):
                    for half in range(2):
                        sp.dma_start(qt[t % 2][64 * half:64 * half + 64, u], q3[64 * u:64 * u + 64, :, t * P:t * P + P]
                                     ).then_inc(s_q[t % 2], 16)
                if t >= 2:
                    sp.wait_ge(AT["mul"], 2 * (t - 1))
                if t:
                    for x in ((0, 1) if t == 1 else (t,)):
                        sp.dma_start(ga[:, x % 2], g3[:, 0:KT, x * P:x * P + P]).then_inc(s_ga[x % 2], 16)

        def pool_att(pool, link):
            pool.wait_ge(SD["done"], NT)
            pool.wait_ge(SD["ste"], 1)
            pool.wait_ge(AT["q"], 1)
            for t in range(1, NT):
                s = t % 2
                pool.wait_ge(s_q[s], 64 * (t // 2 + 1))
                if t >= 2:
                    pool.wait_ge(AT["s"], 16 * (t - 1))
                link(pool.tensor_copy(q_hl[:, s], qt[s][:]))
                for u in range(2):
                    low = slice(64 - 64 * u, P - 64 * u)
                    link(pool.tensor_tensor(q_hl[low, s, u], qt[s][low, u], q_hl[low, s, u].bitcast(F32), ALU.subtract))
                pool.sem_inc(AT["q"], 1)

        def act_keys(act):
            act.wait_ge(s_mm, B_OUT)
            for j in range(2):
                for u in range(2):
                    for half in range(2):
                        act.activation(k_hh[j][64 * half:64 * half + 64, u], kT[64 * u:64 * u + 64, j, 0:T], ACT.Copy
                                       ).then_inc(AT["kh"], 1)

        def pool_keys(pool, link):
            for j in range(2):
                pool.wait_ge(AT["kh"], 4 * j + 4)
                for u in range(2):
                    p = slice(64 * u, 64 * u + 64)
                    pool.tensor_tensor(k_lo[p, j], kT[p, j, 0:T], k_hh[j][p, u].bitcast(F32), ALU.subtract).then_inc(AT["kl"], 1)
                    pool.wait_ge(AT["kl"], 2 * j + u + 1)

        def groups(t):
            return 1 if t < 4 else 2

        def count(n, g):
            return sum(1 for t, *_ in HEADS[:n] if groups(t) > g)

        def pe_att(pe):
            pe.wait_ge(SD["ste"], 1)
            pe.wait_ge(AT["kl"], 4)

            def score(n):
                t, m, j, u, h = HEADS[n]
                w, s, p = P * (t + 1), t % 2, slice(64 * u, 64 * u + 64)
                if n % 16 == 0:
                    pe.wait_ge(AT["q"], t + 1)
                if n >= 2:
                    pe.wait_ge(AT["m"], n - 1)
                for c in range(0, w, 512):
                    e = min(w, c + 512)
                    pe.matmul(pjf[n % 2][:, c:e], q_hl[:, s, u, m], k_hh[j][:, u, c:e], start=True, stop=False)
                    ins = pe.matmul(pjf[n % 2][:, c:e], q_hl[p, s, u, m], k_lo[p, j, c:e], start=False, stop=True)
                ins.then_inc(AT["s"], 1)

            def turn(n):
                t = HEADS[n][0]
                pe.wait_ge(AT["p"], n + 1)
                for g in range(groups(t)):
                    k = count(n, g)
                    if k:
                        pe.wait_ge(AT["c%d" % g], k)
                    if g == 1:
                        pe.wait_ge(AT["nr"], max(n - 3, 0) // 8)
                    for x in range(4 * g, min(4 * g + 4, t + 1)):
                        ins = pe.transpose(pj[:, g, 2, (x % 4) * P:(x % 4) * P + P], Pr[:, n % 2, x * P:x * P + P], ident)
                    ins.then_inc(AT["t"], 1)

            def values(n):
                t, m, j, u, h = HEADS[n]
                if n % 8 == 0 and t:
                    pe.wait_ge(AT["n"], n // 8 - 1)
                for g in range(groups(t)):
                    pe.wait_ge(AT["c%d" % g], count(n, g) + 1)
                    for x in range(4 * g, min(4 * g + 4, t + 1)):
                        ins = pe.matmul(pxf[:, h * 64:h * 64 + 64], PT[:, n % 2, x * P:x * P + P],
                                        vn[:, x, (h // 4) * 64:(h // 4) * 64 + 64], start=(x == 0), stop=(x == t))
                ins.then_inc(AT["o"], 1)

            def outputs(f):
                j = f % 2
                pe.wait_ge(AT["n"], f + 1)
                if count(8 * f + 11, 1):
                    pe.wait_ge(AT["c1"], count(min(8 * f + 11, N_HEADS), 1))
                if f:
                    pe.wait_ge(AT["nr"], f)
                for m in range(4):
                    ins = pe.transpose(pj[:, 1, 2, m * P:m * P + P], an[:, (4 * j + m) * P:(4 * j + m) * P + P], ident)
                ins.then_inc(AT["nt"], 1)

            score(0)
            score(1)
            for n in range(N_HEADS + 3):
                if n + 2 < N_HEADS:
                    score(n + 2)
                if n < N_HEADS:
                    turn(n)
                if 1 <= n <= N_HEADS:
                    values(n - 1)
                if n >= 10 and n % 8 == 2:
                    outputs(n // 8 - 1)

        def act_att(act, link):
            act.wait_ge(SD["ste"], 1)
            act.wait_ge(SD["done"], NT)
            act.wait_ge(s_q[0], 64)
            act.activation(q_hl[:, 0], qt[0][:], ACT.Copy).then_inc(AT["kh"], 1)
            for n in range(N_HEADS + 2):
                if n < N_HEADS:
                    w = P * (HEADS[n][0] + 1)
                    act.wait_ge(AT["nm"], n + 1)
                    if n >= 2:
                        act.wait_ge(AT["t"], count(n - 1, 0) + count(n - 1, 1))
                    act.activation(Pr[:, n % 2, 0:w], Sm[:, n % 2, 0:w], ACT.Exp, bias=nm[:, n:n + 1], scale=ATT_SCALE,
                                   accum_out=sm[:, n:n + 1]).then_inc(AT["p"], 1)
                if n >= 2:
                    second(act, n - 2)

        def second(act, n):
            t = HEADS[n][0]
            if groups(t) == 2:
                act.wait_ge(AT["t"], count(n + 1, 0) + count(n + 1, 1))
                if n >= 2:
                    act.wait_ge(AT["o"], n - 1)
                act.activation(PT[:, n % 2, 512:P * (t + 1)], pj[:, 1, 2, 0:P * (t + 1) - 512], ACT.Copy).then_inc(AT["c1"], 1)

        def dve_att(dve, link):
            dve.wait_ge(SD["done"], NT)
            dve.wait_ge(AT["kh"], 9)
            for u in range(2):
                low = slice(64 - 64 * u, P - 64 * u)
                link(dve.tensor_tensor(q_hl[low, 0, u], qt[0][low, u], q_hl[low, 0, u].bitcast(F32), ALU.subtract))
            dve.sem_inc(AT["q"], 1)

            def first(n):
                t = HEADS[n][0]
                w = min(512, P * (t + 1))
                dve.wait_ge(AT["t"], count(n, 0) + count(n, 1) + 1)
                if n >= 2:
                    dve.wait_ge(AT["o"], n - 1)
                dve.tensor_copy(PT[:, n % 2, 0:w], pj[:, 0, 2, 0:w]).then_inc(AT["c0"], 1)

            def normalize(f):
                t, j = f // 2, f % 2
                c = slice(8 * f, 8 * f + 8)
                dve.wait_ge(AT["p"], 8 * f + 8)
                link(dve.reciprocal(ri[:, c], sm[:, c]))
                dve.wait_ge(AT["o"], 8 * f + 8)
                if f >= 2:
                    dve.wait_ge(AT["nt"], f - 1)
                r = ri[:, c].rearrange("p (a u) -> p u a", u=2)
                dve.tensor_tensor(in_blocks(an, j), by_head(pxf, j), r.unsqueeze(3).broadcast_to([P, 2, 4, 64]), ALU.mult
                                  ).then_inc(AT["n"], 1)

            def gate(f):
                t, j = f // 2, f % 2
                g = ga[:, t % 2, 4 * j:4 * j + 4]
                dve.wait_ge(AT["nt"], f + 1)
                dve.wait_ge(s_ga[t % 2], GA_BASE[t % 2] + 16 * (t // 2 + 1))
                dve.tensor_tensor(g, pj[:, 1, 2].rearrange("p (m t) -> p m t", m=4), g, ALU.mult).then_inc(AT["nr"], 1)

            def add(f):
                t, j = f // 2, f % 2
                g, c = ga[:, t % 2, 4 * j:4 * j + 4], slice(t * P, t * P + P)
                dve.wait_ge(AT["nr"], f + 1)
                dve.tensor_tensor(M[:, 4 * j:4 * j + 4, c], M[:, 4 * j:4 * j + 4, c], g, ALU.add).then_inc(AT["mul"], 1)

            for n in range(N_HEADS + 6):
                if n >= 13 and n % 8 == 5:
                    gate(n // 8 - 1)
                if n < N_HEADS:
                    t = HEADS[n][0]
                    w = P * (t + 1)
                    dve.wait_ge(AT["s"], n + 1)
                    if n >= 2:
                        dve.wait_ge(AT["p"], n - 1)
                    dve.tensor_tensor_reduce(out=Sm[:, n % 2, 0:w], in0=pjf[n % 2][:, 0:w], in1=isc[:, off(t):off(t + 1)],
                                             scale=1.0, scalar=-3.0e38, op0=ALU.add, op1=ALU.max,
                                             accum_out=mx[:, n:n + 1]).then_inc(AT["m"], 1)
                    dve.wait_ge(AT["m"], n + 1)
                    dve.tensor_scalar(nm[:, n:n + 1], mx[:, n:n + 1], -ATT_SCALE, None, ALU.mult).then_inc(AT["nm"], 1)
                if 2 <= n < N_HEADS + 2:
                    first(n - 2)
                if n >= 13 and n % 8 == 5:
                    add(n // 8 - 1)
                if n >= 11 and n % 8 == 3:
                    normalize(n // 8 - 1)

        s_pg = [sem("s_pg0"), sem("s_pg1")] + s_xin
        PG_BASE = (512, 512, 16 * 5, 16 * 4)
        page_slot = [v.rearrange("p (k c) -> p k c", k=8) for v in (raw[:, 0], raw[:, 1])] + [pg[:, 0], pg[:, 1]]
        idx_pages = raw[:].rearrange("p s (k c) -> p (s k) c", c=64)

        def slot_of(n):
            return (n + 2) % 4

        def pages_at(n):
            return PG_BASE[slot_of(n)] + 128 * (n // 4 + 1)

        SA = {n: sem("smp_" + n) for n in ("iqz", "it", "ik", "is", "relu", "w", "wc", "sc", "scc", "pick",
                                           "kt", "k0", "k1", "s", "nm", "p", "pn", "pt", "ptc", "o", "att")}
        qzf, iqzf = qz[:], iqz[:]
        heads_out = kTb[0:16].rearrange("p s j t -> p (s j t)")[:, 0:NB * 256].rearrange("p (b n) -> p b n", b=NB)

        def page_loads(eng, ks, ns):
            for n in ns:
                cache, b = (cache_k if n < NB else cache_v), n % NB
                if n == 0:
                    eng.wait_ge(AT["mul"], 2 * NT)
                elif n in (2, 3):
                    eng.wait_ge(SA["it"], 4 * (n - 1))
                elif 4 <= n < 12:
                    eng.wait_ge(SA["kt"], n - 3)
                elif n >= 12:
                    eng.wait_ge(SA["o"], n - 11)
                for k in ks:
                    v = eng.value_load(pgt[0:1, b * 8 + k:b * 8 + k + 1], min_val=0, max_val=n_phys - 1)
                    eng.dma_start(page_slot[slot_of(n)][:, k], cache[0, bass.ds(v, 1)].rearrange("a s h d -> s (a h d)")
                                  ).then_inc(s_pg[slot_of(n)], 16)

        def sp_smp(sp):
            sp.wait_ge(s_pt, 16)
            for half in range(2):
                with sp.Fori(0, NB // 2) as i:
                    for k in range(8):
                        v = sp.value_load(pgt[0:1, bass.ds(i * 8 + (half * 32 + k), 1)], min_val=0, max_val=n_phys - 1)
                        sp.dma_start(idx_pages[:, bass.ds(i * 8 + (half * 32 + k), 1)],
                                     cache_idx_k[0, bass.ds(v, 1)].rearrange("a s d -> s a d")).then_inc(s_pg[half], 16)
            sp.wait_ge(AT["mul"], 2 * NT)
            sp.wait_ge(s_natd[0], 48 * 5)
            sp.dma_start(vrow, v_sample[0, :, 0].rearrange("b h d -> b (h d)").unsqueeze(0)).then_inc(s_pt, 16)
            sp.dma_start(sg[:, 0], d_z.rearrange("m p t -> p m t")[:, :, T:TT]).then_inc(s_vec, 16)
            sp.dma_start(sg[:, 1], d_g.rearrange("m p t -> p m t")[:, 0:KT, T:TT]).then_inc(s_vec, 16)
            sp.dma_start(sg[:, 2], d_g.rearrange("m p t -> p m t")[:, KT:2 * KT, T:TT]).then_inc(s_vec, 16)
            page_loads(sp, range(0, 4), range(2 * NB))

        def pe_smp(pe):
            pe.wait_ge(AT["mul"], 2 * NT)
            for b in range(NB):
                s = b % 2
                o = (pxf, pjf[1])[s]
                pe.wait_ge(s_pg[b // 4], 512)
                if b >= 2:
                    pe.wait_ge(SA["ik"], 2 * (b - 1))
                for k in range(8):
                    ins = pe.transpose(o[0:64, k * P:k * P + P], idx_pages[:, b * 8 + k], ident)
                ins.then_inc(SA["it"], 1)
                if b:
                    idx_scores(pe, b - 1)
            idx_scores(pe, NB - 1)
            pe.transpose(px[0:64, 0, 0:8], bwt, ident[0:8, 0:8]).then_inc(SA["w"], 1)
            pe.wait_ge(SA["relu"], 1)
            pe.wait_ge(SA["wc"], 1)
            for c0, c1 in ((0, 512), (512, 1024), (1024, L)):
                ins = pe.matmul(pjf[1][0:8, c0:c1], bwz[:], sS[0:64, c0:c1], start=True, stop=True)
            ins.then_inc(SA["sc"], 1)
            pe.wait_ge(SA["scc"], 1)
            for b in range(NB):
                pe.wait_ge(s_pg[slot_of(b)], pages_at(b))
                for j in range(2):
                    if b:
                        pe.wait_ge(SA["k%d" % j], (1 + j) * b)
                    o = (pxf, pjf[1])[j]
                    for k in range(8):
                        ins = pe.transpose(o[:, k * P:k * P + P], page_slot[slot_of(b)][:, k, j * P:j * P + P], ident)
                ins.then_inc(SA["kt"], 1)
                if b:
                    key_scores(pe, b - 1)
            key_scores(pe, NB - 1)
            pe.wait_ge(SA["pick"], 1)
            for c0, c1 in ((0, 512), (512, 1024), (1024, L)):
                ins = pe.matmul(pjf[0][:, c0:c1], sel, sP[0:8, c0:c1], start=False, stop=True)
            ins.then_inc(SA["s"], 1)
            pe.wait_ge(SA["pn"], 1)
            for k in range(8):
                pe.transpose(pxf[:, k * P:k * P + P], sS[:, k * P:k * P + P], ident)
            pe.transpose(pj[0:1, 1, 0, 0:P], sS[:, T:L], ident).then_inc(SA["pt"], 1)
            pe.wait_ge(SA["ptc"], 2)
            pe.wait_ge(s_pt, 32)
            for b in range(NB):
                n = NB + b
                pe.wait_ge(s_pg[slot_of(n)], pages_at(n))
                c, o = slice(b * 16, b * 16 + 16), head_rows(b)
                for k in range(8):
                    pe.matmul(o, sT[:, k, c], page_slot[slot_of(n)][:, k], start=(k == 0), stop=False)
                pe.matmul(o, sT[0:1, 8, c], vrow[0:1, b], start=False, stop=True).then_inc(SA["o"], 1)
            for b in range(NB):
                pe.wait_ge(SA["ptc"], 2 + b // 2 + 1)
                for j in range(2):
                    ins = pe.transpose(px[:, 0, j * P + b * 16:j * P + b * 16 + 16], heads_out[:, b, j * P:j * P + P], ident[0:16, 0:16])
            ins.then_inc(SA["pt"], 1)

        def head_rows(b):
            g = b // 2
            return pj[0:16, g // 3, g % 3, (b % 2) * 256:(b % 2) * 256 + 256]

        def idx_scores(pe, b):
            pe.wait_ge(SA["ik"], 2 * b + 2)
            if b == 0:
                pe.wait_ge(SA["iqz"], 1)
            for c0, c1 in ((0, 512), (512, 1024), (1024, L)):
                ins = pe.matmul(pjf[0][0:64, c0:c1], iqzf[:, b * 64:b * 64 + 64], kTb[0:64, b % 2, 0, c0:c1],
                                start=(b == 0), stop=(b == NB - 1))
            ins.then_inc(SA["is"], 1)

        def key_scores(pe, b):
            for j in range(2):
                pe.wait_ge(SA["k%d" % j], (1 + j) * (b + 1))
            for j in range(2):
                for c0, c1 in ((0, 512), (512, 1024), (1024, L)):
                    ins = pe.matmul(pjf[0][:, c0:c1], qzf[:, (2 * b + j) * P:(2 * b + j) * P + P], kTb[:, b % 2, j, c0:c1],
                                    start=(b == 0 and j == 0), stop=False)
            ins.then_inc(SA["is"], 1)

        def act_smp(act, link):
            ks = range(4, 8)
            act.wait_ge(s_pt, 16)
            page_loads(act, ks, range(0, 2))
            for b in range(NB):
                s = b % 2
                act.wait_ge(SA["it"], b + 1)
                if b % 4 == 3:
                    page_loads(act, ks, (2 + b // 4,))
                if b >= 2:
                    act.wait_ge(SA["is"], b - 1)
                act.activation(kTb[0:64, s, 0, 0:T], (pxf, pjf[1])[s][0:64, 0:T], ACT.Copy).then_inc(SA["ik"], 1)
                act.activation(kTb[0:64, s, 0, T:L], ikT[0:64, T + b:T + b + 1], ACT.Copy).then_inc(SA["ik"], 1)
            act.wait_ge(SA["is"], NB)
            act.activation(sS[0:64], pjf[0][0:64, 0:L], ACT.Relu, scale=IDX_SCALE).then_inc(SA["relu"], 1)
            act.wait_ge(SA["sc"], 1)
            act.activation(sP[0:8], pjf[1][0:8, 0:L], ACT.Copy).then_inc(SA["scc"], 1)
            for b in range(NB):
                act.wait_ge(SA["kt"], b + 1)
                page_loads(act, ks, (b + 4,))
                act.wait_ge(SA["is"], NB + max(b - 1, 0))
                act.activation(kTb[:, b % 2, 0, 0:T], pxf, ACT.Copy).then_inc(SA["k0"], 1)
                act.activation(kTb[:, b % 2, 1, 0:T], pjf[1][:, 0:T], ACT.Copy).then_inc(SA["k1"], 1)
                act.activation(kTb[:, b % 2, :, T:L], kT[:, :, T + b:T + b + 1], ACT.Copy).then_inc(SA["k1"], 1)
            act.wait_ge(SA["nm"], 1)
            act.activation(sS, pjf[0][:, 0:L], ACT.Exp, bias=scol[:, 1:2], scale=ATT_SCALE, accum_out=scol[:, 2:3]
                           ).then_inc(SA["p"], 1)
            act.wait_ge(SA["pt"], 1)
            act.activation(sT[:, 0:8], pxf.rearrange("p (k c) -> p k c", k=8), ACT.Copy).then_inc(SA["ptc"], 1)
            act.activation(sT[0:1, 8], pj[0:1, 1, 0, 0:P], ACT.Copy).then_inc(SA["ptc"], 1)
            page_loads(act, ks, range(12, 16))
            for g in range(NB // 2):
                act.wait_ge(SA["o"], 2 * g + 2)
                act.activation(heads_out[:, 2 * g:2 * g + 2], pj[0:16, g // 3, g % 3].rearrange("p (b n) -> p b n", b=2), ACT.Copy
                               ).then_inc(SA["ptc"], 1)

        def dve_smp(dve, link):
            dve.wait_ge(AT["mul"], 2 * NT)
            link(dve.memset(qzf, 0.0))
            link(dve.memset(iqzf, 0.0))
            for j in range(2):
                for u in range(2):
                    at = j * P + 8 * j + 4 * u
                    link(dve.tensor_copy(qzf[64 * u:64 * u + 64, at:at + NB * 272].rearrange("p (b x) -> p b x", x=272)[:, :, 0:4],
                                         qs[64 * u:64 * u + 64, 4 * j:4 * j + 4].rearrange("p a b -> p b a")))
            link(dve.tensor_copy(iqzf[:, 0:NB * 72].rearrange("p (b x) -> p b x", x=72)[:, :, 0:8],
                                 iqs[:].rearrange("p h b -> p b h")))
            link(dve.tensor_tensor(bwt.rearrange("p (b h) -> p b h", h=8), misc[0:8, NT, 0:8].unsqueeze(1).broadcast_to([8, 8, 8]),
                                   ident[0:8, 0:8].unsqueeze(2).broadcast_to([8, 8, 8]), ALU.mult))
            dve.sem_inc(SA["iqz"], 1)
            dve.wait_ge(SA["w"], 1)
            dve.tensor_copy(bwz[:], px[0:64, 0, 0:8]).then_inc(SA["wc"], 1)
            dve.wait_ge(SA["scc"], 1)
            pick(dve, link, sP[0:8], m8b[0:8], 0, ROUNDS)
            dve.sem_inc(SA["pick"], 1)
            dve.wait_ge(SA["s"], 1)
            link(dve.tensor_reduce(scol[:, 0:1], pjf[0][:, 0:L], AX, ALU.max))
            dve.tensor_scalar(scol[:, 1:2], scol[:, 0:1], -ATT_SCALE, None, ALU.mult).then_inc(SA["nm"], 1)
            dve.wait_ge(SA["p"], 1)
            link(dve.reciprocal(scol[:, 3:4], scol[:, 2:3]))
            dve.tensor_scalar(sS, sS, scol[:, 3:4], None, ALU.mult).then_inc(SA["pn"], 1)
            dve.wait_ge(SA["pt"], 2)
            for j in range(2):
                for u in range(2):
                    p = slice(64 * u, 64 * u + 64)
                    h = 8 * j + 4 * u
                    link(dve.tensor_copy(sg[p, 3, 4 * j:4 * j + 4], px[p, 0, j * P:j * P + P].rearrange("p (b h) -> p h b", h=16)[:, h:h + 4]))
            dve.wait_ge(s_vec, 96 + 48)
            link(dve.tensor_tensor(M[:, :, T:TT], sg[:, 3], sg[:, 1], ALU.mult))
            dve.tensor_copy(gates[:, 0:2], sg[:, 0:4:2]).then_inc(SA["att"], 1)
            dve.wait_ge(SA["att"], 1)

        assert NB == KT
        s_mh, s_ml = sem("s_mh"), sem("s_ml")
        s_s0 = [sem("s_s00"), sem("s_s01")]
        s_s1 = [sem("s_s10"), sem("s_s11")]
        SS = {n: sem("sss_" + n) for n in ("dt", "dtc", "e", "ec", "dec", "bx", "bc", "s1", "new", "y", "g", "sq", "ss", "rt", "m")}
        y8, dt8, dc8, xd8, g8, w8 = (sq4[:, n] for n in range(6))
        sq8, rt8 = sq4[:, 6], sq4[:, 7, 0:2]

        def sp_sss(sp):
            sp.wait_ge(SA["att"], 1)
            for b in range(NB):
                s = b % 2
                if b >= 2:
                    sp.wait_ge(SS["s1"], b - 1)
                for j in range(2):
                    for u in range(2):
                        h = 8 * j + 4 * u
                        sp.dma_start(S0[64 * u:64 * u + 64, s, 4 * j:4 * j + 4],
                                     state_ssm[0, b, h:h + 4].rearrange("a d n -> d a n")).then_inc(s_s0[s], 16)

        def pe_sss(pe):
            pe.wait_ge(SA["att"], 1)
            pe.transpose(px[0:16, 1, 0:8], dtn[0:8, NT], ident[0:8, 0:8])
            pe.transpose(px[0:16, 1, 8:16], dta[0:8, NT], ident[0:8, 0:8]).then_inc(SS["dt"], 1)
            pe.wait_ge(SS["dtc"], 1)
            for m in range(KT):
                ins = pe.matmul(px[:, 0, m * 16:m * 16 + 16], expand[:, m], dT[:].rearrange("h w b -> h (w b)"), start=True, stop=True)
            ins.then_inc(SS["e"], 1)
            for b in range(NB):
                if b >= 2:
                    pe.wait_ge(SS["y"], b - 1)
                pe.wait_ge(SS["bx"], b + 1)
                for w in range(4):
                    ins = pe.matmul(pj[:, b % 2, 0, w * P:w * P + P], BX[:, 2 * w:2 * w + 2].rearrange("p u d -> p (u d)"), ident,
                                    start=True, stop=True)
                ins.then_inc(SS["bc"], 1)
            pe.wait_ge(SS["sq"], 1)
            for j in range(2):
                for a in range(4):
                    ins = pe.matmul(px[:, 1, j * 8:j * 8 + 8], halves, sq8[:, 4 * j + a], start=(a == 0), stop=(a == 3))
            ins.then_inc(SS["ss"], 1)

        def act_sss(act, link):
            act.wait_ge(SS["ec"], 1)
            act.activation(dc8, dc8, ACT.Exp).then_inc(SS["dec"], 1)
            for k in range(KT):
                act.activation(ahi[:, k, 0:T], M[:, k, 0:T], ACT.Copy).then_inc(s_mh, 1)
            for b in range(NB):
                act.wait_ge(SS["new"], b + 1)
                for j in range(2):
                    for u in range(2):
                        h = 8 * j + 4 * u
                        act.dma_start(ssm_sample[0, b, h:h + 4].rearrange("a d n -> d a n"),
                                      S1[64 * u:64 * u + 64, b % 2, 4 * j:4 * j + 4]).then_inc(s_s1[b % 2], 16)
            act.wait_ge(SS["g"], 1)
            act.activation(sq8, g8, ACT.Square).then_inc(SS["sq"], 1)
            act.wait_ge(SS["ss"], 1)
            act.activation(rt8, px[:, 1, 0:16].rearrange("p (j b) -> p j b", j=2), ACT.Sqrt, bias=eps[:], scale=1.0 / 256
                           ).then_inc(SS["rt"], 1)
            for s in range(2):
                act.wait_ge(s_s1[s], 64 * 4)

        def pool_sss(pool, link):
            pool.wait_ge(SS["dec"], 1)
            for b in range(NB):
                s = b % 2
                pool.wait_ge(s_s0[s], 64 * (b // 2 + 1))
                if b >= 2:
                    pool.wait_ge(s_s1[s], 64 * (b // 2))
                    pool.wait_ge(SS["y"], b - 1)
                pool.tensor_tensor(S1[:, s], S0[:, s], dc8[:, :, b:b + 1].broadcast_to([P, KT, P]), ALU.mult).then_inc(SS["s1"], 1)
                pool.wait_ge(s_mh, b + 1)
                pool.tensor_tensor(alo[:, b, 0:T], M[:, b, 0:T], ahi[:, b, 0:T].bitcast(F32), ALU.subtract).then_inc(s_ml, 1)

        def dve_sss(dve, link):
            dve.wait_ge(SS["dt"], 1)
            dve.tensor_copy(dT[:], px[0:16, 1, 0:16].rearrange("p (w b) -> p w b", w=2)).then_inc(SS["dtc"], 1)
            dve.wait_ge(SS["e"], 1)
            e = px[:, 0, 0:P].rearrange("p (m w b) -> p m w b", m=KT, w=2)
            link(dve.tensor_copy(dt8, e[:, :, 0]))
            dve.tensor_copy(dc8, e[:, :, 1]).then_inc(SS["ec"], 1)
            link(dve.tensor_tensor(xd8, dt8, convS[:, 0:KT], ALU.mult))

            def spread(b):
                if b:
                    dve.wait_ge(SS["bc"], b)
                dve.tensor_copy(BX[:], convS[:, KT:16, b:b + 1].broadcast_to([P, 8, 64])).then_inc(SS["bx"], 1)

            spread(0)
            for b in range(NB):
                s = b % 2
                if b + 1 < NB:
                    spread(b + 1)
                dve.wait_ge(SS["bc"], b + 1)
                bc = pj[:, s, 0].rearrange("p (w j n) -> p w j n", w=2, j=2)
                for j in range(2):
                    link(dve.tensor_tensor(S2[:, s, 4 * j:4 * j + 4], bc[:, 0, j:j + 1].broadcast_to([P, 4, P]),
                                           xd8[:, 4 * j:4 * j + 4, b:b + 1].broadcast_to([P, 4, P]), ALU.mult))
                dve.wait_ge(SS["s1"], b + 1)
                link(dve.tensor_tensor(S1[:, s], S1[:, s], S2[:, s], ALU.add))
                dve.sem_inc(SS["new"], 1)
                for j in range(2):
                    link(dve.tensor_tensor(S3[:, 4 * j:4 * j + 4], bc[:, 1, j:j + 1].broadcast_to([P, 4, P]),
                                           S1[:, s, 4 * j:4 * j + 4], ALU.mult))
                dve.tensor_reduce(y8[:, :, b:b + 1], S3[:], AX, ALU.add).then_inc(SS["y"], 1)
            dve.wait_ge(SS["y"], NB)
            link(dve.tensor_tensor(w8, convS[:, 0:KT], dskip[:].unsqueeze(2).broadcast_to([P, KT, NB]), ALU.mult))
            link(dve.tensor_tensor(g8, y8, w8, ALU.add))
            dve.tensor_tensor(g8, g8, gates[:, 0], ALU.mult).then_inc(SS["g"], 1)
            dve.wait_ge(SS["g"], 1)
            dve.wait_ge(SS["rt"], 1)
            link(dve.reciprocal(rt8, rt8))
            for j in range(2):
                link(dve.tensor_tensor(g8[:, 4 * j:4 * j + 4], g8[:, 4 * j:4 * j + 4], rt8[:, j:j + 1].broadcast_to([P, 4, NB]), ALU.mult))
            link(dve.tensor_tensor(g8, g8, par[:, 72:80].unsqueeze(2).broadcast_to([P, KT, NB]), ALU.mult))
            link(dve.tensor_tensor(g8, g8, gates[:, 1], ALU.mult))
            dve.tensor_tensor(M[:, :, T:TT], M[:, :, T:TT], g8, ALU.add).then_inc(SS["m"], 1)

        FS = 16
        s_uh, s_ul = sem("s_uh"), sem("s_ul")
        s_yt, s_ye = sem("s_yt"), sem("s_ye")
        s_yo = [sem("s_yo0"), sem("s_yo1")]
        wo_view = [raw[:, s].rearrange("p (k n) -> p k n", k=KT) for s in range(2)]
        N0 = len(PAIRS)

        def out_at(n):
            return raw_at[(N0 + n) % 2] + 64 * (n // 2 + 1)

        SU, SV = (N0 + 4) % 2, (N0 + 5) % 2
        MLP_AT = [raw_at[s] + 128 for s in range(2)]

        def sp_out(sp, out_pairs):
            sp.wait_ge(SA["o"], NB)
            for n in out_pairs:
                s = (N0 + n) % 2
                sp.wait_ge(s_split, 2 * (N0 + n) - 2)
                for j in range(2):
                    for u in range(2):
                        sp.dma_start(wo_view[s][64 * u:64 * u + 64, 4 * j:4 * j + 4], w_out2[j, u][:, :, n * 256:n * 256 + 256]
                                     ).then_inc(s_raw[s], 16)

        def sp_x(sp):
            sp.wait_ge(SS["m"], 1)
            sp.dma_start(wrow[:], final_norm_w.unsqueeze(0).broadcast_to([P, D])).then_inc(s_par, 16)
            x3 = d_x.rearrange("k p t -> p k t")
            sp.wait_ge(s_ml, KT + 1)
            sp.dma_start(x2T[:, 0:2], x3[:, 0:2]).then_inc(s_crow, 16)
            sp.dma_start(x2T[:, 2:KT], x3[:, 2:KT]).then_inc(s_cst, 16)

        def sp_mlp(sp):
            def up(e):
                sp.dma_start(wo_view[SU], w_up2[:, :, bass.ds(e * 256, 256)]).then_inc(s_raw[SU], 16)

            def down(e):
                sp.dma_start(raw[:, SV].rearrange("p (k n) -> p k n", k=2), w_dn3[bass.ds(e, 1)].rearrange("e p k n -> p (e k) n")
                             ).then_inc(s_raw[SV], 16)

            sp.wait_ge(s_split, B_MLP - 2)
            up(0)
            sp.wait_ge(s_split, B_MLP)
            down(0)
            sp.wait_ge(s_split, B_MLP + 2)
            up(1)
            with sp.Fori(0, FS - 2) as e:
                sp.wait_ge(s_split, e * 10 + (B_MLP + 4))
                up(e + 2)
                sp.wait_ge(s_split, e * 10 + (B_MLP + 12))
                down(e + 1)
            sp.wait_ge(s_split, (FS - 2) * 10 + (B_MLP + 12))
            down(FS - 1)
            for t in range(NT + 1):
                sp.wait_ge(s_ye, t + 1)
                sp.dma_start(y_prompt[0, t * P:t * P + P] if t < NT else y_sample[:, 0],
                             OC[0:P if t < NT else NB, t % 2, 0:D]).then_inc(s_yo[t % 2], 16)
            sp.wait_ge(s_yo[0], 16 * 5)
            sp.wait_ge(s_yo[1], 16 * 4)

        w_dn3 = w_down[0].rearrange("(e k p) n -> e p k n", p=P, k=2)

        def pool_mlp(pool, link):
            for n in range(4):
                s = (N0 + n) % 2
                pool.wait_ge(s_raw[s], out_at(n))
                for b in range(2):
                    pool.wait_ge(s_mm, 2 * (N0 + n) + b - 1)
                    split_block(pool, [(wo_view[s][:, :, b * P:b * P + P], 0, P)], KT, b, link)
            pool.wait_ge(SS["m"], 1)
            link(pool.memset(zero, 0.0))
            dn = raw[:, SV].rearrange("p (k n) -> p k n", k=2)

            def up(at, before, raw_n):
                pool.wait_ge(s_raw[SU], at(16, MLP_AT[SU] + 16 * raw_n))
                for b in range(2):
                    pool.wait_ge(s_mm, at(10, before + b + 1))
                    half_split(pool, wo_view[SU][:, :, b * P:b * P + P], whi[:, b], wlo[:, b], link)

            def down(at, block):
                pool.wait_ge(s_raw[SV], at(16, MLP_AT[SV] + 16))
                for b in range(8):
                    pool.wait_ge(s_mm, at(10, block + b - 1))
                    half_split(pool, dn[:, :, b * P:b * P + P], d_hi[:, b % 2], d_lo[:, b % 2], link)

            up(lambda per, c: c, B_MLP - 2, 1)
            norm_lo(pool, OC, ahi, alo, 1)
            up(lambda per, c: c, B_MLP, 2)
            down(lambda per, c: c, B_MLP + 4)
            with pool.Fori(1, FS - 1) as e:
                link.enter(e - 1, 10)
                up(lambda per, c: e * per + c, B_MLP - 8, 2)
                down(lambda per, c: e * per + c, B_MLP + 4)
            link.leave(FS - 2)
            down(lambda per, c: (FS - 1) * per + c, B_MLP + 2)

        def half_split(pool, src, hi, lo, link):
            link(pool.tensor_tensor(hi, src, zero.unsqueeze(1).broadcast_to([P, src.shape[1], P]), ALU.add))
            pool.tensor_tensor(lo, src, hi.bitcast(F32), ALU.subtract).then_inc(s_split, 1)

        def slices(eng, step, link, per=0):
            with eng.Fori(0, FS // 2 - 1) as i:
                if link:
                    link.enter(i, 2 * per)
                for s in range(2):
                    step(lambda n, c: i * (2 * n) + (s * n + c), s)
            if link:
                link.leave(FS // 2 - 1)
            step(lambda n, c: (FS - 2) * n + c, 0)

        def pe_mlp(pe):
            pe.wait_ge(SS["m"], 1)
            pe.wait_ge(s_ml, KT + 1)
            for s in range(2):
                pe.wait_ge(s_split, B_OUT + s + 1)
                products(pe, s, KT, ahi, alo)
            with pe.Fori(1, KT // 2) as i:
                for s in range(2):
                    pe.wait_ge(s_split, i * 2 + (B_OUT + s + 1))
                    pe.wait_ge(s_evd, i * 2 + (s - 1))
                    products(pe, s, KT, ahi, alo)
            pe.wait_ge(s_evd, KT)
            norm_sums(pe, OC, 1)

            def down(at, s, block, last=False):
                pe.wait_ge(s_ul, at(2, 2))
                for m in range(KT):
                    pe.wait_ge(s_split, at(10, block + m + 1))
                    if m < 2 and not last:
                        pe.wait_ge(s_ev, at(2, B_OUT + 2 + m + 1))
                    elif m >= 2:
                        pe.wait_ge(s_evd, at(KT, KT + m - 1))
                    else:
                        pe.wait_ge(s_evd, at(KT, m - 1 + KT))
                    products(pe, m % 2, 2, u_hi[:, s], u_lo[:, s], d_hi, d_lo)

            def step(at, s):
                for b in range(2):
                    pe.wait_ge(s_split, at(10, B_MLP + 2 + b + 1))
                    pe.wait_ge(s_evd, at(KT, KT + b - 1))
                    products(pe, b, KT, ahi, alo)
                down(at, s, B_MLP + 4)

            pe.wait_ge(s_split, B_MLP + 2)
            pe.wait_ge(s_rt, 2)
            first_products(pe, ahi, alo, lambda k: pe.wait_ge(s_hl, 8 + k + 1))
            pe.wait_ge(s_ev, B_OUT + 2)
            slices(pe, step, None)
            down(lambda per, c: (FS - 1) * per + c, 1, B_MLP + 2, last=True)
            pe.wait_ge(s_evd, KT + KT * FS)
            for t in range(NT + 1):
                w = P if t < NT else NB
                if t >= 2:
                    pe.wait_ge(s_ye, t - 1)
                for k in range(KT):
                    ins = pe.transpose(pjf[t % 2][0:w, k * P:k * P + P], x2T[:, k, t * P:t * P + w], ident)
                ins.then_inc(s_yt, 1)

        def act_mlp(act, link):
            act.wait_ge(SS["m"], 1)
            act.activation(ahi[:, :, T:TT], M[:, :, T:TT], ACT.Copy).then_inc(s_mh, 1)
            act.wait_ge(s_x2, KT)
            norm_squares(act, x2T, OC, 1)
            norm_root(act, RC[:], 1)
            norm_hi(act, OC, ahi, 1)

            def up(at, s, e):
                for b in range(2):
                    act.wait_ge(s_mm, at(10, B_MLP + 2 * e + b + 1))
                    if e:
                        act.wait_ge(s_ul, at(2, b + 1))
                    act.activation(three(OC[:, b]), prod[b], ACT.Relu).then_inc(s_ev, 1)
                for b in range(2):
                    act.wait_ge(s_sq2, at(2, 2 * e + b + 1))
                    act.activation(u_hi[:, s, b], OC[:, b], ACT.Copy).then_inc(s_uh, 1)

            up(lambda per, c: c, 0, 0)
            slices(act, lambda at, s: up(at, 1 - s, 1), None)
            for t in range(NT + 1):
                w = P if t < NT else NB
                act.wait_ge(s_yt, t + 1)
                act.activation(RC[0:w, 0:D], pjf[t % 2][0:w, 0:D], ACT.Square, accum_out=rt9[0:w, 0, t:t + 1]).then_inc(s_fn, 1)
                act.wait_ge(s_fn, t + 1)
                act.activation(rt9[0:w, 1, t:t + 1], rt9[0:w, 0, t:t + 1], ACT.Sqrt, bias=eps[0:w], scale=1.0 / D).then_inc(s_rt, 1)

        def add_gated(dve, slot, m, gate):
            x, g = x2T[:, m], modT[:, gate + m, 8:9]
            a = x[:, 0:2 * W3].rearrange("p (a b) -> p a b", a=2)
            end = W3 - NB
            dve.scalar_tensor_tensor(a, prod[slot][:, 0:2], g, a, ALU.mult, ALU.add).then_inc(s_add, 1)
            dve.scalar_tensor_tensor(x[:, 2 * W3:T], prod[slot][:, 2, 0:end], g, x[:, 2 * W3:T], ALU.mult, ALU.add).then_inc(s_add, 1)
            dve.tensor_tensor(tmp8[:, slot], prod[slot][:, 2, end:W3], modT[:, gate + m, 0:8], ALU.mult).then_inc(s_add, 1)

        def dve_mlp(dve, link):
            dve.wait_ge(SS["m"], 1)
            dve.wait_ge(s_mh, KT + 1)
            dve.tensor_tensor(alo[:, :, T:TT], M[:, :, T:TT], ahi[:, :, T:TT].bitcast(F32), ALU.subtract).then_inc(s_ml, 1)
            dve.wait_ge(s_crow, 48)
            for m in range(KT):
                if m == 2:
                    dve.wait_ge(s_cst, 32)
                dve.wait_ge(s_mm, B_OUT + m + 1)
                add_gated(dve, m % 2, m, 16)
                dve.wait_ge(s_add, 3 * m + 3)
                dve.tensor_tensor(x2T[:, m, T:TT], x2T[:, m, T:TT], tmp8[:, m % 2], ALU.add).then_inc(s_x2, 1)
                dve.sem_inc(s_evd, 1)
            dve.wait_ge(s_x2, KT)
            dve.wait_ge(s_rt, 2)
            link(dve.reciprocal(RC[:], RC[:]))
            norm_apply(dve, link, x2T, RC[:], OC, par[:, 56:64], 24 // 8, 32 // 8, 1)

            def up(at, s, e):
                for b in range(2):
                    dve.wait_ge(s_ev, at(2, B_OUT + 2 * e + b + 1))
                    dve.tensor_tensor(OC[:, b], OC[:, b], OC[:, b], ALU.mult).then_inc(s_sq2, 1)
                for b in range(2):
                    dve.wait_ge(s_uh, at(2, 2 * e + b + 1))
                    dve.tensor_tensor(u_lo[:, s, b], OC[:, b], u_hi[:, s, b].bitcast(F32), ALU.subtract).then_inc(s_ul, 1)

            def down(at, block):
                for m in range(KT):
                    dve.wait_ge(s_mm, at(10, block + m + 1))
                    add_gated(dve, m % 2, m, 40)
                    dve.wait_ge(s_add, at(3 * KT, 3 * KT + 3 * m + 3))
                    dve.tensor_tensor(x2T[:, m, T:TT], x2T[:, m, T:TT], tmp8[:, m % 2], ALU.add).then_inc(s_x2, 1)
                    dve.wait_ge(s_x2, at(KT, KT + m + 1))
                    dve.sem_inc(s_evd, 1)

            up(lambda per, c: c, 0, 0)
            slices(dve, lambda at, s: (up(at, 1 - s, 1), down(at, B_MLP + 4)), None)
            down(lambda per, c: (FS - 1) * per + c, B_MLP + 2)
            dve.wait_ge(s_par, 16 * N_PAR + 16)
            for t in range(NT + 1):
                w = P if t < NT else NB
                dve.wait_ge(s_rt, 2 + t + 1)
                link(dve.reciprocal(rt9[0:w, 2, t:t + 1], rt9[0:w, 1, t:t + 1]))
                if t >= 2:
                    dve.wait_ge(s_yo[t % 2], 16 * (t // 2))
                dve.scalar_tensor_tensor(OC[0:w, t % 2, 0:D], pjf[t % 2][0:w, 0:D], rt9[0:w, 2, t:t + 1], wrow[0:w],
                                         ALU.mult, ALU.mult).then_inc(s_ye, 1)

        s_x2, s_add, s_sq2, s_fn, s_evd = (sem(n) for n in ("s_x2", "s_add", "s_sq2", "s_fn", "s_evd"))

        block = ctx.enter_context(nc.Block())

        @block.sync
        def _(sp):
            sp_phase_a(sp)
            sp_ssd(sp)
            sp_att(sp)
            sp_smp(sp)
            sp_sss(sp)
            sp_out(sp, (0, 1))
            sp_x(sp)
            sp_out(sp, (2, 3))
            sp_mlp(sp)

        @block.gpsimd
        def _(pool):
            link = Link(pool, s_c["pool"])
            pool_phase_a(pool, link)
            pool_ssd(pool, link)
            pool_att(pool, link)
            pool_sss(pool, link)
            pool_mlp(pool, link)

        @block.tensor
        def _(pe):
            pe_phase_a(pe)
            pe_ssd(pe)
            pe_att(pe)
            pe_smp(pe)
            pe_sss(pe)
            pe_mlp(pe)

        @block.scalar
        def _(act):
            link = Link(act, s_c["act"])
            act_phase_a(act, link)
            act_ssd(act, link)
            act_att(act, link)
            act_smp(act, link)
            act_sss(act, link)
            act_mlp(act, link)
            act.wait_ge(s_out, n_out[0])

        @block.vector
        def _(dve):
            link = Link(dve, s_c["dve"])
            dve_phase_a(dve, link)
            dve_ssd(dve, link)
            dve_att(dve, link)
            dve_smp(dve, link)
            dve_sss(dve, link)
            dve_mlp(dve, link)


def constants():
    import numpy as np
    f = np.float32
    c = np.zeros((P, K_END), f)
    p, q = np.arange(P)[:, None], np.arange(P)[None, :]
    c[:, K_ID:K_ID + P] = p == q
    c[:, K_ONE:K_ONE + P] = 1
    c[:, K_HALF:K_HALF + P] = p // 64 == q // 64
    c[:, K_LE:K_LE + P] = p <= q
    c[:, K_GT:K_GT + P] = p > q
    c[:, K_DIAG:K_DIAG + P] = -(q > p).astype(f)
    d = np.arange(P) % 64
    pos = np.concatenate([np.arange(T), np.full(NB, T)]).astype(f)
    inv = f(500000.0) ** (-np.arange(8, dtype=f) * f(2.0) / f(16))
    ang = (pos[None, :] * inv.astype(f)[d % 8][:, None]).astype(f)
    turned = (d < 16)[:, None]
    c[:, K_COS:K_COS + TT] = np.where(turned, np.cos(ang), 1)
    c[:, K_SIN:K_SIN + TT] = np.where(turned, np.where((d < 8)[:, None], -np.sin(ang), np.sin(ang)), 0)
    c[0:8, K_SEL:K_SEL + P] = np.arange(8)[:, None] == q // 16
    for m in range(8):
        head = 8 * (m // 4) + 4 * (np.arange(P) // 64) + m % 4
        c[0:16, K_EXP + m * P:K_EXP + (m + 1) * P] = np.arange(16)[:, None] == head[None, :]
    return c


_INS = ["x_prompt", "x_sample", "cache_k", "cache_v", "cache_idx_k", "state_conv", "state_ssm", "page_table",
        "c_prompt", "c_sample", "w_ada", "b_ada", "norm1_w", "w_in", "conv_w", "conv_b", "dt_bias", "a_log", "d_skip",
        "ssm_norm_w", "w_out", "norm2_w", "w_up", "w_down", "final_norm_w"]
_OUTS = [(1, T, D), (NB, 1, D), (1, 1, T, 4, 64), (1, 1, T, 4, 64), (1, 1, T, 64), (1, 1, 3, 2 * D),
         (1, 1, 16, 64, P), (1, NB, 1, 4, 64), (1, NB, 1, 4, 64), (1, NB, 1, 64), (1, NB, 3, 2 * D), (1, NB, 16, 64, P)]


def kernel(**inputs):
    import numpy as np
    import concourse.bacc as bacc
    from concourse.bass_utils import run_bass_kernel_spmd

    nc = bacc.Bacc("TRN2", target_bir_lowering=False, num_devices=1)
    arrays, args = {}, []
    for name in _INS:
        a = np.ascontiguousarray(inputs[name])
        arrays["in_" + name] = a
        args.append(nc.dram_tensor("in_" + name, a.shape, mybir.dt.from_np(a.dtype), kind="ExternalInput").ap())
    arrays["in_consts"] = constants()
    args.append(nc.dram_tensor("in_consts", (P, K_END), F32, kind="ExternalInput").ap())
    for i, shape in enumerate(_OUTS):
        args.append(nc.dram_tensor(f"out_{i}", shape, F32, kind="ExternalOutput").ap())
    program(nc, *args)
    r = run_bass_kernel_spmd(nc, [arrays], core_ids=[0])
    return tuple(r.results[0][f"out_{i}"] for i in range(len(_OUTS)))
```
